# Optimizing a Trainium2 kernel written in Bass

```python
import math
import jax, jax.numpy as jnp
from jax import lax
import numpy as np

D_MODEL = 1024
BATCH = 1
SEQ = 128
DEPTH = 2
DEC_BATCH = 1
DEC_SEQ = 256
PAST_LEN = 128

F32 = jnp.float32
GRID_W = 64
N_HEADS = 8
N_KV_HEADS = 2
GQA_GROUP = N_HEADS // N_KV_HEADS
HEAD_DIM = 128
ATTN_W = N_HEADS * HEAD_DIM
KV_W = N_KV_HEADS * HEAD_DIM
WINDOW = 128
Q_BLOCK = 128
BAND = Q_BLOCK + 2 * WINDOW
ROPE_BASE = 10000.0
ROPE_PAIRS_PER_AXIS = HEAD_DIM // 4
D_RNN = 1024
LRU_BLOCKS = 16
LRU_BW = D_RNN // LRU_BLOCKS
LRU_C = 8.0
CONV_W = 4
CONV_LEFT = 2
N_EXPERTS = 16
N_GROUPS = 4
EXPERTS_PER_GROUP = N_EXPERTS // N_GROUPS
TOP_K = 2
D_EXPERT = 512
N_ADA = 6
EPS = 1e-6
IN_SPLITS = [ATTN_W, ATTN_W + KV_W, ATTN_W + 2 * KV_W, ATTN_W + 2 * KV_W + D_RNN,
             ATTN_W + 2 * KV_W + 2 * D_RNN, ATTN_W + 2 * KV_W + 2 * D_RNN + D_MODEL]
IN_COLS = ATTN_W + 2 * KV_W + 2 * D_RNN + 2 * D_MODEL

kernel_name = "hybrid_dit_prefix_swa_rglru_moe_step"

def _rmsnorm(x, g):
    xf = x.astype(F32)
    y = xf * lax.rsqrt(jnp.mean(xf * xf, axis=-1, keepdims=True) + EPS)
    return (y * g.astype(F32)).astype(x.dtype)

def _modulation(cond, w, b):
    m = jax.nn.silu(cond) @ w + b
    return tuple(mi[:, None, :] for mi in jnp.split(m, N_ADA, axis=-1))

def _rope_2d_tables(n_tokens):
    rows = n_tokens // GRID_W
    row = jnp.repeat(jnp.arange(rows, dtype=F32), GRID_W)
    col = jnp.tile(jnp.arange(GRID_W, dtype=F32), rows)
    inv = ROPE_BASE ** (-jnp.arange(ROPE_PAIRS_PER_AXIS, dtype=F32) / ROPE_PAIRS_PER_AXIS)
    ang = jnp.concatenate([row[:, None] * inv, col[:, None] * inv], axis=-1)
    return jnp.cos(ang), jnp.sin(ang)

def _apply_rope(x, cos, sin):
    xf = x.astype(F32)
    half = HEAD_DIM // 2
    x1, x2 = xf[..., :half], xf[..., half:]
    c = cos[None, :, None, :]
    s = sin[None, :, None, :]
    return jnp.concatenate([x1 * c - x2 * s, x2 * c + x1 * s], axis=-1).astype(x.dtype)

def _attend(q, k, v, mask, sink):
    s = jnp.einsum('bqgrd,bkgd->bgrqk', q, k).astype(F32) * (HEAD_DIM ** -0.5)
    if mask is not None:
        s = jnp.where(mask, s, -jnp.inf)
    sink_col = jnp.broadcast_to(sink.astype(F32)[None, :, :, None, None], s.shape[:-1] + (1,))
    p = jax.nn.softmax(jnp.concatenate([s, sink_col], axis=-1), axis=-1)[..., :-1]
    return jnp.einsum('bgrqk,bkgd->bqgrd', p.astype(v.dtype), v)

def _context_attention(q, k, v, sink):
    B, S = q.shape[:2]
    nb = S // Q_BLOCK
    qb = jnp.moveaxis(q.reshape(B, nb, Q_BLOCK, N_KV_HEADS, GQA_GROUP, HEAD_DIM), 1, 0)
    o = lax.map(lambda q_i: _attend(q_i, k, v, None, sink), qb)
    return jnp.moveaxis(o, 0, 1).reshape(B, S, ATTN_W)

def _latent_attention(q, k, v, k_ctx, v_ctx, sink):
    B, S = q.shape[:2]
    nb = S // Q_BLOCK
    pad = ((0, 0), (WINDOW, WINDOW), (0, 0), (0, 0))
    kp, vp = jnp.pad(k, pad), jnp.pad(v, pad)
    starts = jnp.arange(nb) * Q_BLOCK
    idx = starts[:, None] + jnp.arange(BAND)[None, :]
    k_loc = jnp.moveaxis(kp[:, idx], 1, 0)
    v_loc = jnp.moveaxis(vp[:, idx], 1, 0)
    qpos = starts[:, None] + jnp.arange(Q_BLOCK)[None, :]
    kpos = idx - WINDOW
    mask = ((kpos[:, None, :] >= 0) & (kpos[:, None, :] < S)
            & (jnp.abs(qpos[:, :, None] - kpos[:, None, :]) <= WINDOW))
    ctx_mask = jnp.ones((Q_BLOCK, k_ctx.shape[1]), dtype=bool)
    qb = jnp.moveaxis(q.reshape(B, nb, Q_BLOCK, N_KV_HEADS, GQA_GROUP, HEAD_DIM), 1, 0)

    def block(args):
        q_i, k_i, v_i, m_i = args
        kk = jnp.concatenate([k_i, k_ctx.astype(k_i.dtype)], axis=1)
        vv = jnp.concatenate([v_i, v_ctx.astype(v_i.dtype)], axis=1)
        mm = jnp.concatenate([m_i, ctx_mask], axis=1)
        return _attend(q_i, kk, vv, mm, sink)

    o = lax.map(block, (qb, k_loc, v_loc, mask))
    return jnp.moveaxis(o, 0, 1).reshape(B, S, ATTN_W)

def _conv_centred(x, w, b):
    y = lax.conv_general_dilated(x, w.astype(x.dtype)[:, None, :], window_strides=(1,),
                                 padding=[(CONV_LEFT, CONV_W - 1 - CONV_LEFT)],
                                 dimension_numbers=('NWC', 'WIO', 'NWC'),
                                 feature_group_count=x.shape[-1])
    return y + b

def _block_diag(x, w, b):
    xb = x.reshape(x.shape[:-1] + (LRU_BLOCKS, LRU_BW))
    return jnp.einsum('bsnk,nkj->bsnj', xb, w).reshape(x.shape) + b

def _lru_scan(a, u, h0, reverse):
    def step(h, au):
        h = au[0] * h + au[1]
        return h, h
    h_last, hs = lax.scan(step, h0, (jnp.swapaxes(a, 0, 1), jnp.swapaxes(u, 0, 1)), reverse=reverse)
    return h_last, jnp.swapaxes(hs, 0, 1)

def _rglru_bidir(xr, lp, h0):
    xc = _conv_centred(xr, lp['conv_w'], lp['conv_b']).astype(F32)
    ys, hs = [], []
    for d in range(2):
        r = jax.nn.sigmoid(_block_diag(xc, lp['lru_wa'][d].astype(F32), lp['lru_ba'][d].astype(F32)))
        i = jax.nn.sigmoid(_block_diag(xc, lp['lru_wx'][d].astype(F32), lp['lru_bx'][d].astype(F32)))
        log_a = -LRU_C * r * jax.nn.softplus(-lp['lru_lambda'][d].astype(F32))
        u = jnp.sqrt(-jnp.expm1(2.0 * log_a)) * (i * xc)
        h_last, y = _lru_scan(jnp.exp(log_a), u, h0[:, d], reverse=(d == 1))
        ys.append(y)
        hs.append(h_last)
    return (ys[0] + ys[1]).astype(xr.dtype), jnp.stack(hs, axis=1)

def _moe(h, router_w, router_b, w_gate_up, w_down):
    B, S, D = h.shape
    t = h.reshape(B * S, D)
    scores = jax.nn.sigmoid(t.astype(F32) @ router_w.astype(F32))
    sel = scores + router_b.astype(F32)
    grp_score = lax.top_k(sel.reshape(-1, N_GROUPS, EXPERTS_PER_GROUP), TOP_K)[0].sum(-1)
    best_grp = jnp.argmax(grp_score, axis=-1)
    in_grp = jnp.repeat(best_grp[:, None] == jnp.arange(N_GROUPS)[None, :], EXPERTS_PER_GROUP, axis=-1)
    _, e_idx = lax.top_k(jnp.where(in_grp, sel, -jnp.inf), TOP_K)
    w_sel = jnp.take_along_axis(scores, e_idx, axis=-1)
    w_sel = w_sel / jnp.sum(w_sel, axis=-1, keepdims=True)
    gates = jnp.sum(jax.nn.one_hot(e_idx, N_EXPERTS, dtype=F32) * w_sel[..., None], axis=1)
    gu = jnp.einsum('td,edf->tef', t, w_gate_up)
    g_, u_ = jnp.split(gu, 2, axis=-1)
    act = jax.nn.silu(g_) * u_ * gates[..., None].astype(t.dtype)
    return jnp.einsum('tef,efd->td', act, w_down).reshape(B, S, D)

def _layer(x, mod, lp, router_w, router_b, rope, ctx_kv, h0):
    sh1, sc1, g1, sh2, sc2, g2 = mod
    B, S, _ = x.shape
    h = _rmsnorm(x, lp['norm1']) * (1 + sc1) + sh1
    q, k, v, xr, gr, ga, gb = jnp.split(h @ lp['w_in'], IN_SPLITS, axis=-1)
    q = q.reshape(B, S, N_HEADS, HEAD_DIM)
    k = k.reshape(B, S, N_KV_HEADS, HEAD_DIM)
    v = v.reshape(B, S, N_KV_HEADS, HEAD_DIM)
    sink = lp['sink'].reshape(N_KV_HEADS, GQA_GROUP)
    if ctx_kv is None:
        att = _context_attention(q, k, v, sink)
    else:
        cos, sin = rope
        att = _latent_attention(_apply_rope(q, cos, sin), _apply_rope(k, cos, sin), v,
                                ctx_kv[0], ctx_kv[1], sink)
    rnn, h_last = _rglru_bidir(xr, lp, h0)
    merged = (jax.nn.sigmoid(ga) * (att @ lp['w_attn_proj'])
              + jax.nn.sigmoid(gb) * ((jax.nn.gelu(gr) * rnn) @ lp['w_rnn_proj']))
    x = x + g1 * (merged @ lp['w_out'])
    h2 = _rmsnorm(x, lp['norm2']) * (1 + sc2) + sh2
    x = x + g2 * _moe(h2, router_w, router_b, lp['w_gate_up'], lp['w_down'])
    return x, k, v, h_last

def setup_inputs(seed: int = 0) -> dict:
    key = jax.random.key(seed)
    ks = jax.random.split(key, 32)

    def nrm(k, shape, scale):
        return scale * jax.random.normal(k, shape, F32)

    a0 = jax.random.uniform(ks[18], (DEPTH, 2, D_RNN), F32, 0.9, 0.999)
    s0 = a0 ** (1.0 / LRU_C)
    return {
        'x_prompt': nrm(ks[0], (BATCH, SEQ, D_MODEL), 1.0),
        'x_sample': nrm(ks[1], (DEC_BATCH, DEC_SEQ, D_MODEL), 1.0),
        'cache_k': nrm(ks[2], (DEC_BATCH, DEPTH, PAST_LEN, N_KV_HEADS, HEAD_DIM), 1.0),
        'cache_v': nrm(ks[3], (DEC_BATCH, DEPTH, PAST_LEN, N_KV_HEADS, HEAD_DIM), 1.0),
        'state_h': nrm(ks[4], (DEC_BATCH, DEPTH, 2, D_RNN), 0.5),
        'c': nrm(ks[5], (DEC_BATCH, D_MODEL), 1.0),
        'c_ctx': nrm(ks[6], (D_MODEL,), 1.0),
        'norm1_g': 1.0 + nrm(ks[7], (DEPTH, D_MODEL), 0.02),
        'norm2_g': 1.0 + nrm(ks[8], (DEPTH, D_MODEL), 0.02),
        'w_ada': nrm(ks[9], (DEPTH, D_MODEL, N_ADA * D_MODEL), 0.5 * D_MODEL ** -0.5),
        'b_ada': nrm(ks[10], (DEPTH, N_ADA * D_MODEL), 0.02),
        'w_in': nrm(ks[11], (DEPTH, D_MODEL, IN_COLS), D_MODEL ** -0.5),
        'conv_w': nrm(ks[12], (DEPTH, CONV_W, D_RNN), CONV_W ** -0.5),
        'conv_b': nrm(ks[13], (DEPTH, D_RNN), 0.02),
        'lru_wa': nrm(ks[14], (DEPTH, 2, LRU_BLOCKS, LRU_BW, LRU_BW), LRU_BW ** -0.5),
        'lru_ba': nrm(ks[15], (DEPTH, 2, D_RNN), 0.02),
        'lru_wx': nrm(ks[16], (DEPTH, 2, LRU_BLOCKS, LRU_BW, LRU_BW), LRU_BW ** -0.5),
        'lru_bx': nrm(ks[17], (DEPTH, 2, D_RNN), 0.02),
        'lru_lambda': jnp.log(s0) - jnp.log1p(-s0),
        'attn_sink': nrm(ks[19], (DEPTH, N_HEADS), 0.5),
        'w_attn_proj': nrm(ks[20], (DEPTH, ATTN_W, D_MODEL), ATTN_W ** -0.5),
        'w_rnn_proj': nrm(ks[21], (DEPTH, D_RNN, D_MODEL), D_RNN ** -0.5),
        'w_out': nrm(ks[22], (DEPTH, D_MODEL, D_MODEL), D_MODEL ** -0.5),
        'router_w': nrm(ks[23], (D_MODEL, N_EXPERTS), D_MODEL ** -0.5),
        'router_b': nrm(ks[24], (N_EXPERTS,), 0.01),
        'w_gate_up': nrm(ks[25], (DEPTH, N_EXPERTS, D_MODEL, 2 * D_EXPERT), D_MODEL ** -0.5),
        'w_down': nrm(ks[26], (DEPTH, N_EXPERTS, D_EXPERT, D_MODEL), D_EXPERT ** -0.5),
        'final_norm_g': 1.0 + nrm(ks[27], (D_MODEL,), 0.02),
    }

def reference(x_prompt, x_sample, cache_k, cache_v, state_h, c, c_ctx, norm1_g, norm2_g,
              w_ada, b_ada, w_in, conv_w, conv_b, lru_wa, lru_ba, lru_wx, lru_bx, lru_lambda,
              attn_sink, w_attn_proj, w_rnn_proj, w_out, router_w, router_b, w_gate_up, w_down,
              final_norm_g):
    b_prompt = x_prompt.shape[0]
    rope = _rope_2d_tables(x_sample.shape[1])
    h0_ctx = jnp.zeros((b_prompt, 2, D_RNN), F32)
    xp, xs = x_prompt, x_sample
    ks, vs, hs = [], [], []
    for l in range(DEPTH):
        lp = {
            'norm1': norm1_g[l], 'norm2': norm2_g[l], 'w_in': w_in[l],
            'conv_w': conv_w[l], 'conv_b': conv_b[l],
            'lru_wa': lru_wa[l], 'lru_ba': lru_ba[l], 'lru_wx': lru_wx[l], 'lru_bx': lru_bx[l],
            'lru_lambda': lru_lambda[l], 'sink': attn_sink[l],
            'w_attn_proj': w_attn_proj[l], 'w_rnn_proj': w_rnn_proj[l], 'w_out': w_out[l],
            'w_gate_up': w_gate_up[l], 'w_down': w_down[l],
        }
        mod_ctx = _modulation(c_ctx[None, :], w_ada[l], b_ada[l])
        xp, k_l, v_l, h_l = _layer(xp, mod_ctx, lp, router_w, router_b, None, None, h0_ctx)
        ks.append(k_l)
        vs.append(v_l)
        hs.append(h_l)
        mod_lat = _modulation(c, w_ada[l], b_ada[l])
        xs, _, _, _ = _layer(xs, mod_lat, lp, router_w, router_b, rope,
                             (cache_k[:, l], cache_v[:, l]), state_h[:, l].astype(F32))
    y_prompt = _rmsnorm(xp, final_norm_g)
    y_sample = _rmsnorm(xs, final_norm_g)
    new_cache_k = jnp.stack(ks, axis=1)
    new_cache_v = jnp.stack(vs, axis=1)
    new_state_h = jnp.stack(hs, axis=1).astype(x_prompt.dtype)
    return (y_prompt, y_sample, new_cache_k, new_cache_v, new_state_h)


_drawn_inputs = setup_inputs


def setup_inputs(seed=0):
    import zlib

    import numpy as np

    out = dict(_drawn_inputs(seed))
    spreads = {}
    factors = {'lru_ba': 8.0, 'lru_bx': 5.415, 'attn_sink': 8.0, 'final_norm_g': 9.718, 'cache_k': 2.845}
    for name, (base, spread) in spreads.items():
        noise = np.random.default_rng([zlib.crc32(name.encode()), seed]).standard_normal(out[name].shape)
        drawn = base * np.exp(spread * noise) if base else spread * noise
        out[name] = __import__('jax').numpy.asarray(drawn.astype(out[name].dtype))
    for name, factor in factors.items():
        out[name] = (out[name] * factor).astype(out[name].dtype)
    return out
```

```python
import math
from contextlib import ExitStack

import numpy as np
import concourse.bass as bass
from concourse import mybir

F32 = mybir.dt.float32
U32 = mybir.dt.uint32
I32 = mybir.dt.int32
ALU = mybir.AluOpType
ACT = mybir.ActivationFunctionType
AX = mybir.AxisListType

P = 128
D = 1024
KT = D // P
DEPTH = 2
CTX, LAT = 128, 256
T = CTX + LAT
TT = T // P
HEADS, KVH, HD = 8, 2, 128
GRP = HEADS // KVH
SCALE = HD ** -0.5
LATK = LAT + P
NADA = 6
NE, NG, EG = 16, 4, 4
DE = 512
EPS = 1e-6
CHUNK = 512
SLOTS = 5
CAP = 128
MORE = (2 * T - 1) // CAP
BLOCKS = NE + MORE
SEG = 3
CW = CTX + SEG + LAT
XW = CW + 3
LAT0 = CTX + SEG
GELU_C = math.sqrt(2.0 / math.pi)
BIG = 1e30

W_IN_ORDER = ["kv", "q0", "q1", "xr0", "xr1", "gr0", "gr1", "ga0", "ga1", "gb0", "gb1"]
W_IN_COL = {"q0": 0, "q1": 512, "kv": 1024, "xr0": 1536, "xr1": 2048, "gr0": 2560, "gr1": 3072,
            "ga0": 3584, "ga1": 4096, "gb0": 4608, "gb1": 5120}
DENSE = [f"ada{c}" for c in range(12)] + W_IN_ORDER + ["ap0", "ap1", "rp0", "rp1", "wo0", "wo1"]
PER_LAYER = len(DENSE) + 3 * NE

UNITS = [(h, b) for h in range(HEADS) for b in range(3)]
PAIRS = [(d, j) for j in range(KT) for d in range(2)]


def gemm_order():
    o = [("ada", c) for c in range(12)] + [("ss1", 0), ("k", 0), ("k", 1), ("kvc", 0), ("vl", 0), ("vl", 1)]
    o += [("q", 0), ("krot", 0), ("q", 1), ("krot", 1)]
    for h in range(2, KT):
        o += [("q", h), ("qrot", h - 2)]
    o += [("xr", 0), ("qrot", 6), ("xr", 1), ("qrot", 7)] + [("xr", j) for j in range(2, KT)]
    for i in range(3 * KT):
        o.append((("gr", "ga", "gb")[i // KT], i % KT))
        if i >= KT:
            o += [("gate_a", i - KT), ("gate_x", i - KT)]
    o += [("ap", n) for n in range(KT)] + [("rp", n) for n in range(KT)] + [("wo", n) for n in range(KT)]
    o += [("ss2", 0), ("logits", 0)]
    return o


GEMM = gemm_order()
G_AT = {g: n for n, g in enumerate(GEMM)}
TRAN = ([("vec", 0), ("kc", 0)] + [("mod", c) for c in range(12)] + [("pt", u) for u in range(len(UNITS))]
        + [("h2", t * 2 + i) for t in range(TT) for i in range(2)] + [("state", 0), ("rank", 0)]
        + [("comb", t * 2 + i) for t in range(TT) for i in range(2)])
T_AT = {g: n for n, g in enumerate(TRAN)}


def build(nc, x_prompt, x_sample, cache_k, cache_v, state_h, c, c_ctx, norm1_g, norm2_g, w_ada, b_ada,
          w_in, conv_w, conv_b, lru_wa, lru_ba, lru_wx, lru_bx, lru_lambda, attn_sink, w_attn_proj,
          w_rnn_proj, w_out, router_w, router_b, w_gate_up, w_down, final_norm_g,
          consts, y_prompt, y_sample, new_k, new_v, new_h):
    ctx = ExitStack()
    with ctx:
        def sb(name, shape, dt=F32):
            return ctx.enter_context(nc.sbuf_tensor(name, shape, dt))

        sems = {}

        def S(name):
            if name not in sems:
                sems[name] = ctx.enter_context(nc.semaphore(name))
            return sems[name]

        ring = sb("ring", [P, SLOTS, KT * CHUNK])
        xT = sb("xT", [P, KT, T])
        hT = sb("hT", [P, KT, T])
        qT = sb("qT", [P, HEADS, T])
        kT = sb("kT", [P, KVH, T])
        kcT = sb("kcT", [P, KVH, P])
        kvc = sb("kvc", [P, 512])
        vl = sb("vl", [P, 2, 256])
        vcache = sb("vcache", [P, 256])
        xp = sb("xp", [P, XW])
        xc = sb("xc", [P, KT, CW])
        gr = sb("gr", [P, KT, T])
        ga = sb("ga", [P, KT, T])
        gb = sb("gb", [P, KT, T])
        con = sb("con", [P, consts.shape[1]])
        ident, rotm, cosT, sinT = con[:, 0:128], con[:, 128:256], con[:, 256:512], con[:, 512:768]
        mask = [con[:, 768:896], con[:, 896:1024]]
        before = con[:, 1024:1152]
        sumsel = con[:, 1152:1154]
        iota_e = con[:, 1154:1170]
        iota_g = con[:, 1170:1174]
        tokid = con[:, 1174:1177]
        num_e = con[:, 1177:1193]
        ones = sb("ones", [P, P])
        vrow = sb("vrow", [P, 2, P])
        vec = sb("vec", [P, 2, P])
        crow = sb("crow", [24, P])
        cvec = sb("cvec", [P, 24])
        cpad = sb("cpad", [P, KT, 32])
        modT = sb("modT", [P, 48, 2])
        modA = sb("modA", [P, 4, KT, 2])
        sinkb = sb("sinkb", [P, DEPTH, HEADS])
        nsink = sb("nsink", [P, HEADS])
        sp = sb("sp", [P, 8, 16])
        hb = sb("hb", [P, 2, 16])
        gatew = sb("gatew", [P, 2, 2, P])
        hyb = sb("hyb", [P, CW])
        rs = hyb[:, 0:T]
        pr = sb("pr", [P, 2, LATK])
        pt = sb("pt", [P, 2, LATK])
        kcache = pr[:, 0, 0:256]
        smx = sb("smx", [P, 2, 8])
        tmp = sb("tmp", [P, 7, CW])
        sq = tmp[:, 4:6, 0:T]
        adap = tmp[:, :, :].rearrange("p i n -> p (i n)")[:, 0:1024].rearrange("p (i n) -> p i n", i=2)
        hlast = sb("hlast", [P, 16])
        hrow = crow[0:16, :]
        rb = sb("rb", [P, NE])
        rw = sb("rw", [P, KT, NE])
        rt = pt[:, :, :].rearrange("p i n -> p (i n)")[:, 0:14 * TT * NE].rearrange("p (i t e) -> p i t e", i=14, t=TT)
        rt4 = sb("rt4", [P, 10, TT * NG])
        rt1 = sb("rt1", [P, 10, TT])
        gates = sb("gates", [P, 2, TT])
        posu = sb("posu", [P, 2, TT], U32)
        slotu = sb("slotu", [P, 2, TT], U32)
        toku = sb("toku", [P, TT], U32)
        nrt = sb("nrt", [P, 4])
        nri = sb("nri", [1, 1 + MORE], I32)
        ids = sb("ids", [P, BLOCKS], U32)
        zero_u = sb("zero_u", [P, BLOCKS], U32)
        grf = gr[:, :, :].rearrange("p k t -> p (k t)")
        gaf = ga[:, :, :].rearrange("p k t -> p (k t)")
        gbf = gb[:, :, :].rearrange("p k t -> p (k t)")
        xg = [grf[:, 0:1024], grf[:, 1024:2048]]
        silu_t = grf[:, 2048:2560]
        act = grf[:, 2560:3072]
        xgT = [gaf[:, 0:1024].rearrange("p (k c) -> p k c", k=KT),
               gaf[:, 1024:2048].rearrange("p (k c) -> p k c", k=KT)]
        actT = [gaf[:, 2048 + 512 * i:2560 + 512 * i].rearrange("p (k c) -> p k c", k=4) for i in range(2)]
        yo = [gbf[:, 0:1024], gbf[:, 1024:2048]]
        yg = [grf[:, 0:1024], grf[:, 1024:2048]]
        ysum = gbf[:, 2048:3072]
        zrow = ysum

        banks = [ctx.enter_context(nc.psum_tensor(f"bank{i}", [P, 512], F32)) for i in range(8)]
        G, TB, SB, OB = banks[0:3], banks[3:5], banks[5:7], banks[7]

        h2d = nc.dram_tensor("h2_rows", (T, D), F32, kind="Internal").ap()
        idtab = nc.dram_tensor("slot_tokens", (CAP * BLOCKS, 1), U32, kind="Internal").ap()
        yd = nc.dram_tensor("expert_rows", (BLOCKS * CAP, D), F32, kind="Internal").ap()

        def gidx(l, g):
            return l * len(GEMM) + G_AT[g]

        def tidx(l, g):
            return l * len(TRAN) + T_AT[g]

        def gemm_ready(eng, l, g):
            n = gidx(l, g)
            eng.wait_ge(S("gemm_done"), n + 1)
            return G[n % 3]

        def tran_ready(eng, l, g):
            n = tidx(l, g)
            eng.wait_ge(S("tran_done"), n + 1)
            return TB[n % 2]

        def g_free(l, g):
            return S(f"gbank_free{gidx(l, g) % 3}")

        def t_free(l, g):
            return S(f"tbank_free{tidx(l, g) % 2}")

        def dense_at(l, name):
            n = l * PER_LAYER + DENSE.index(name)
            return n % SLOTS, n // SLOTS

        def moe_at(l, pos):
            n = l * PER_LAYER + len(DENSE) + pos
            return n % SLOTS, n // SLOTS

        def gu_pos(e, half):
            return half if e == 0 else 3 * e - 1 + half

        def dn_pos(e):
            return 3 * e + 4 if e < NE - 1 else 3 * NE - 1

        LAST_USE = {"kv": ("vl", 1)}
        for name in DENSE:
            if name.startswith("ada"):
                LAST_USE[name] = ("ada", int(name[3:]))
            elif name != "kv":
                LAST_USE[name] = (name[:2] if name[0] != "q" else "q", 4 * int(name[-1]) + 3)
        MOE = [None] * (3 * NE)
        for e in range(NE):
            MOE[gu_pos(e, 0)], MOE[gu_pos(e, 1)], MOE[dn_pos(e)] = ("gu_half", e), ("gu_done", e), ("down_done", e)

        def released(n):
            l, at = divmod(n, PER_LAYER)
            if at < len(DENSE):
                return S("gemm_done"), gidx(l, LAST_USE[DENSE[at]]) + 1
            name, e = MOE[at - len(DENSE)]
            return S(name), l * NE + e + 1

        gu_w = w_gate_up.rearrange("l e (h k p) n -> l e h p k n", p=P, h=2)
        dn_w = w_down.rearrange("l e (k p) n -> l e p k n", p=P)

        def dense_src(l, name):
            if name.startswith("ada"):
                c0, w = int(name[3:]) * CHUNK, w_ada
            elif name in W_IN_COL:
                c0, w = W_IN_COL[name], w_in
            else:
                c0, w = int(name[2]) * CHUNK, {"ap": w_attn_proj, "rp": w_rnn_proj, "wo": w_out}[name[0:2]]
            return w[l].rearrange("(k p) n -> p k n", p=P)[:, :, c0:c0 + CHUNK]

        def slot_kn(s):
            return ring[:, s, :].rearrange("p (k n) -> p k n", k=KT)

        def slot_wide(s):
            return ring[:, s, :].rearrange("p (k n) -> p k n", k=4)

        def v_ada(j0, j1):
            return vec[:, 0, j0:j1]

        def v_conv(i, j):
            return vec[:, 0, 48 + i * 8 + j:49 + i * 8 + j]

        def v_convb(j):
            return vec[:, 0, 80 + j:81 + j]

        n1g, n2g = vec[:, 0, 88:96], vec[:, 0, 96:104]
        v_ba, v_bx, v_lam = vec[:, 1, 0:16], vec[:, 1, 16:32], vec[:, 1, 32:48]

        def v_state(d, j):
            return vec[:, 1, 48 + d * 8 + j:49 + d * 8 + j]

        def seg(j, s):
            return slice(0, CTX) if s == 0 else slice(LAT0, CW)

        STREAM = [slice(0, CTX), slice(CTX, T)]

        block = ctx.enter_context(nc.Block())

        @block.sync
        def _(sy):
            def load(l, slot_use, dst, src):
                s, u = slot_use
                if u > 0:
                    sy.wait_ge(*released(u * SLOTS + s - SLOTS))
                sy.dma_start(dst, src).then_inc(S(f"w_loaded{s}"), 16)

            sy.dma_start(con[:, :], consts).then_inc(S("const_loaded"), 16)
            sy.dma_start(crow[0:8, :], c_ctx.rearrange("(k p) -> k p", p=P)).then_inc(S("const_loaded"), 16)
            sy.dma_start(crow[8:16, :], c.rearrange("b (k p) -> (b k) p", p=P)).then_inc(S("const_loaded"), 16)
            sy.dma_start(crow[16:24, :], final_norm_g.rearrange("(k p) -> k p", p=P)).then_inc(S("const_loaded"), 16)
            xs = grf[:, 0:3072].rearrange("p (t n) -> p t n", t=TT)
            sy.dma_start(xs[:, 0, :], x_prompt[0]).then_inc(S("x_loaded"), 16)
            sy.dma_start(xs[:, 1:3, :], x_sample[0].rearrange("(t p) n -> p t n", p=P)).then_inc(S("x_loaded"), 16)
            for l in range(DEPTH):
                for name in DENSE:
                    s, u = dense_at(l, name)
                    load(l, (s, u), slot_kn(s), dense_src(l, name))
                for e in range(NE):
                    for half in range(2):
                        s, u = moe_at(l, gu_pos(e, half))
                        load(l, (s, u), slot_wide(s), gu_w[l, e, half])
                    if e >= 1:
                        s, u = moe_at(l, dn_pos(e - 1))
                        load(l, (s, u), slot_wide(s), dn_w[l, e - 1])
                s, u = moe_at(l, dn_pos(NE - 1))
                load(l, (s, u), slot_wide(s), dn_w[l, NE - 1])
                sy.wait_ge(S("rounds_known"), l + 1)
                more = sy.value_load(nri[0:1, 0:1], min_val=0, max_val=MORE)
                for b in range(MORE):
                    with sy.If(more > b):
                        e = sy.value_load(nri[0:1, 1 + b:2 + b], min_val=0, max_val=NE - 1)
                        if b == 0:
                            sy.wait_ge(S("experts_done"), l + 1)
                        else:
                            sy.wait_ge(S(f"x_stored{l}"), 16 * b)
                        for half in range(2):
                            sy.dma_start(slot_wide(half), gu_w[l, bass.ds(e, 1), half][0]).then_inc(S(f"x_loaded{l}"), 16)
                        sy.dma_start(slot_wide(2), dn_w[l, bass.ds(e, 1)][0]).then_inc(S(f"x_loaded{l}"), 16)
                        sy.wait_ge(S(f"x_y_ready{l}"), b + 1)
                        row = (NE + b) * CAP
                        sy.dma_start(yd[row:row + CAP, :], yo[0][0:CAP, :]).then_inc(S(f"x_stored{l}"), 16)
                        sy.wait_ge(S(f"x_stored{l}"), 16 * (b + 1))
                    with sy.Else():
                        sy.nop()
                sy.nop().then_inc(S("rounds_over"), 1)

        @block.tensor
        def _(pe):
            def g_take(l, g):
                n = gidx(l, g)
                if n >= 3:
                    pe.wait_ge(S(f"gbank_free{n % 3}"), n // 3)
                return G[n % 3]

            def t_take(l, g):
                n = tidx(l, g)
                if n >= 2:
                    pe.wait_ge(S(f"tbank_free{n % 2}"), n // 2)
                return TB[n % 2]

            def weights(s_u):
                s, u = s_u
                pe.wait_ge(S(f"w_loaded{s}"), 16 * (u + 1))
                return s

            def product(l, g, slot, n, rhs, width=T):
                bank = g_take(l, g)
                for k in range(KT):
                    mm = pe.matmul(bank[:, 0:width], slot_kn(slot)[:, k, n * P:(n + 1) * P], rhs(k),
                                   start=(k == 0), stop=(k == KT - 1))
                return mm

            pe.wait_ge(S("const_loaded"), 64)
            pe.wait_ge(S("x_loaded"), 32)
            pe.transpose(OB[:, 0:24], crow[:, :], ident[0:24, 0:24]).then_inc(S("cond_tran"), 1)
            xs = grf[:, 0:3072].rearrange("p (t n) -> p t n", t=TT)
            for k in range(KT):
                if k >= 2:
                    pe.wait_ge(S("x_taken"), k - 1)
                for t in range(TT):
                    mm = pe.transpose(SB[k % 2][:, t * P:(t + 1) * P], xs[:, t, k * P:(k + 1) * P], ident)
                mm.then_inc(S("x_tran"), 1)

            for l in range(DEPTH):
                pe.wait_ge(S("vec_loaded"), (l + 1) * 9 * 16)
                bank = t_take(l, ("vec", 0))
                pe.transpose(bank[:, 0:104], vrow[0:104, 0, :], ident[0:104, 0:104])
                pe.transpose(bank[:, 128:192], vrow[0:64, 1, :], ident[0:64, 0:64]).then_inc(S("tran_done"), 1)
                bank = t_take(l, ("kc", 0))
                pe.wait_ge(S("cache_loaded"), (l + 1) * 32)
                for g in range(KVH):
                    mm = pe.transpose(bank[:, g * P:(g + 1) * P], kcache[:, g * P:(g + 1) * P], ident)
                mm.then_inc(S("tran_done"), 1)
                if l == 0:
                    pe.wait_ge(S("cond_ready"), 1)

                def mod_sum(cc):
                    pe.wait_ge(S("ada_copied"), l * 12 + cc + 1)
                    bank = t_take(l, ("mod", cc))
                    for j in range(4):
                        mm = pe.matmul(bank[:, 2 * j:2 * j + 2], adap[:, cc % 2, j * P:(j + 1) * P], sumsel,
                                       start=(j == 0), stop=(j == 3), skip_group_check=True)
                    mm.then_inc(S("tran_done"), 1)

                for cc in range(12):
                    s = weights(dense_at(l, f"ada{cc}"))
                    bank = g_take(l, ("ada", cc))
                    for k in range(KT):
                        g = 32 * (k % 4)
                        mm = pe.matmul(bank[g:g + 32, :], cpad[:, k, :], slot_kn(s)[:, k, :],
                                       start=(k < 4), stop=(k >= 4), tile_position=(0, g))
                    mm.then_inc(S("gemm_done"), 1)
                    if cc >= 1:
                        mod_sum(cc - 1)
                mod_sum(11)
                def sum_squares(l, which):
                    bank = g_take(l, (which, 0))
                    base = (l * 2 + (which == "ss2")) * KT
                    for k in range(KT):
                        pe.wait_ge(S("sq_ready"), base + k + 1)
                        mm = pe.matmul(bank[:, 0:T], ones[:, :], sq[:, k % 2, :], start=(k == 0), stop=(k == KT - 1))
                        if k < KT - 1:
                            mm.then_inc(S("sq_used"), 1)
                    mm.then_inc(S("gemm_done"), 1)

                sum_squares(l, "ss1")

                def h_all(k):
                    return hT[:, k, :]

                s = weights(dense_at(l, "kv"))
                pe.wait_ge(S("h_ready_v"), 2 * l * KT + KT)
                pe.wait_ge(S("h_ready_a"), 2 * l * KT + KT)
                for g in range(KVH):
                    product(l, ("k", g), s, g, h_all).then_inc(S("gemm_done"), 1)
                bank = g_take(l, ("kvc", 0))
                for k in range(KT):
                    mm = pe.matmul(bank[:, :], hT[:, k, 0:P], slot_kn(s)[:, k, :], start=(k == 0), stop=(k == KT - 1))
                mm.then_inc(S("gemm_done"), 1)
                for t in range(2):
                    bank = g_take(l, ("vl", t))
                    for k in range(KT):
                        mm = pe.matmul(bank[:, 0:256], hT[:, k, (t + 1) * P:(t + 2) * P],
                                       slot_kn(s)[:, k, 256:512], start=(k == 0), stop=(k == KT - 1))
                    mm.then_inc(S("gemm_done"), 1)

                def rotated(l, kind, i):
                    bank = g_take(l, (kind, i))
                    src = kT if kind == "krot" else qT
                    n = i if kind == "krot" else 2 + i
                    pe.wait_ge(S("qk_copied"), l * 10 + n + 1)
                    pe.matmul(bank[:, 0:LAT], rotm, src[:, i, CTX:T], start=True, stop=True).then_inc(S("gemm_done"), 1)

                for h in range(HEADS):
                    if h % 4 == 0:
                        s = weights(dense_at(l, f"q{h // 4}"))
                    product(l, ("q", h), s, h % 4, h_all).then_inc(S("gemm_done"), 1)
                    if h < 2:
                        rotated(l, "krot", h)
                    else:
                        rotated(l, "qrot", h - 2)
                for j in range(KT):
                    if j % 4 == 0:
                        s = weights(dense_at(l, f"xr{j // 4}"))
                    product(l, ("xr", j), s, j % 4, h_all).then_inc(S("gemm_done"), 1)
                    if j < 2:
                        rotated(l, "qrot", 6 + j)

                def scores(u):
                    h, b = UNITS[u]
                    n = l * len(UNITS) + u
                    g = h // GRP
                    if n >= 2:
                        pe.wait_ge(S("exp_done"), n - 1)
                    if b == 0:
                        pe.matmul(SB[u % 2][:, 0:P], qT[:, h, 0:P], kT[:, g, 0:P], start=True, stop=True)\
                            .then_inc(S("scores_done"), 1)
                        return
                    q = qT[:, h, b * P:(b + 1) * P]
                    pe.matmul(SB[u % 2][:, 0:LAT], q, kT[:, g, CTX:T], start=True, stop=True, skip_group_check=True)
                    pe.matmul(SB[u % 2][:, LAT:LATK], q, kcT[:, g, :], start=True, stop=True,
                              skip_group_check=True).then_inc(S("scores_done"), 1)

                def probs_turned(u):
                    h, b = UNITS[u]
                    bank = t_take(l, ("pt", u))
                    pe.wait_ge(S("probs_ready"), l * len(UNITS) + u + 1)
                    for i in range(1 if b == 0 else 3):
                        mm = pe.transpose(bank[:, i * P:(i + 1) * P], pr[:, u % 2, i * P:(i + 1) * P], ident)
                    mm.then_inc(S("tran_done"), 1)

                def attend(u):
                    h, b = UNITS[u]
                    g = h // GRP
                    n = l * len(UNITS) + u
                    pe.wait_ge(S("pt_copied"), n + 1)
                    if n >= 1:
                        pe.wait_ge(S("att_copied"), n)
                    vals = [kvc[:, 256 + g * P:256 + (g + 1) * P]] if b == 0 else \
                        [vl[:, 0, g * P:(g + 1) * P], vl[:, 1, g * P:(g + 1) * P], vcache[:, g * P:(g + 1) * P]]
                    for i, v in enumerate(vals):
                        mm = pe.matmul(OB[:, 0:P], v, pt[:, u % 2, i * P:(i + 1) * P],
                                       start=(i == 0), stop=(i == len(vals) - 1))
                    mm.then_inc(S("att_done"), 1)

                pe.wait_ge(S("rope_done"), (l + 1) * 10)
                for i in range(3 * KT):
                    if i % 4 == 0:
                        s = weights(dense_at(l, ("gr", "ga", "gb")[i // KT] + str(i % KT // 4)))
                    product(l, (("gr", "ga", "gb")[i // KT], i % KT), s, i % 4, h_all).then_inc(S("gemm_done"), 1)
                    scores(i)
                    if i >= 1:
                        probs_turned(i - 1)
                    if i >= 2:
                        attend(i - 2)
                    if i >= KT:
                        n = i - KT
                        d, j = PAIRS[n]
                        pe.wait_ge(S("xc_ready"), l * KT + j + 1)
                        pe.wait_ge(S(f"gatew_loaded{n % 2}"), (l * 8 + n // 2 + 1) * 64)
                        for which, name in ((0, "gate_a"), (1, "gate_x")):
                            bank = g_take(l, (name, n))
                            pe.matmul(bank[:, 0:CW], gatew[:, which, n % 2, :], xc[:, j, :],
                                      start=True, stop=True).then_inc(S("gemm_done"), 1)
                probs_turned(23)
                attend(22)
                attend(23)
                pe.wait_ge(S("att_copied"), (l + 1) * len(UNITS))
                for name, src in (("ap", qT), ("rp", gr), ("wo", ga)):
                    for n in range(KT):
                        if n % 4 == 0:
                            s = weights(dense_at(l, f"{name}{n // 4}"))
                        if n == 0 and name == "rp":
                            pe.wait_ge(S("rnn_ready"), (l + 1) * KT)
                        if n == 0 and name == "wo":
                            pe.wait_ge(S("merged_ready"), (l + 1) * KT)
                        product(l, (name, n), s, n % 4, lambda k, a=src: a[:, k, :]).then_inc(S("gemm_done"), 1)
                sum_squares(l, "ss2")
                pe.wait_ge(S("h_ready_v"), (2 * l + 2) * KT)
                pe.wait_ge(S("h_ready_a"), (2 * l + 2) * KT)
                bank = g_take(l, ("logits", 0))
                for t in range(TT):
                    for k in range(KT):
                        mm = pe.matmul(bank[:, t * NE:(t + 1) * NE], hT[:, k, t * P:(t + 1) * P], rw[:, k, :],
                                       start=(k == 0), stop=(k == KT - 1), skip_group_check=True)
                mm.then_inc(S("gemm_done"), 1)
                for t in range(TT):
                    for i in range(2):
                        bank = t_take(l, ("h2", t * 2 + i))
                        for k in range(4):
                            mm = pe.transpose(bank[:, k * P:(k + 1) * P], hT[:, i * 4 + k, t * P:(t + 1) * P], ident)
                        mm.then_inc(S("tran_done"), 1)
                bank = t_take(l, ("state", 0))
                pe.wait_ge(S("hlast_ready"), (l + 1) * 16)
                pe.transpose(bank[0:16, 0:P], hlast[:, :], ident).then_inc(S("tran_done"), 1)
                bank = t_take(l, ("rank", 0))
                pe.wait_ge(S("picked"), l + 1)
                for t in range(TT + 1):
                    for i in range(min(t + 1, TT)):
                        lhs = before if i == t else ones[:, :]
                        mm = pe.matmul(bank[:, t * NE:(t + 1) * NE], lhs, rt[:, 8, i, :],
                                       start=(i == 0), stop=(i == min(t, TT - 1)), skip_group_check=True)
                mm.then_inc(S("tran_done"), 1)

                def turn_rows(e, xrows, x_done, dst_banks):
                    for i in range(2):
                        for k in range(4):
                            kk = i * 4 + k
                            mm = pe.transpose(dst_banks[i][:, k * CAP:(k + 1) * CAP],
                                              xrows[0:CAP, kk * P:(kk + 1) * P], ident[0:CAP, 0:CAP])
                    mm.then_inc(x_done, 1)

                def gate_up(slots, xt, done, half_done):
                    for half in range(2):
                        for n in range(2):
                            for k in range(4):
                                mm = pe.matmul(G[n][0:CAP, :], xt[:, half * 4 + k, 0:CAP],
                                               slot_wide(slots[half])[:, k, n * 512:(n + 1) * 512],
                                               start=(half == 0 and k == 0), stop=(half == 1 and k == 3))
                        if half == 1:
                            mm.then_inc(done, 1)
                        elif half_done is not None:
                            mm.then_inc(half_done, 1)

                def down(slot, at, done):
                    for n in range(2):
                        for k in range(4):
                            mm = pe.matmul(SB[n][0:CAP, :], at[:, k, 0:CAP], slot_wide(slot)[:, k, n * 512:(n + 1) * 512],
                                           start=(k == 0), stop=(k == 3))
                    mm.then_inc(done, 1)

                def xturn(e):
                    n = l * NE + e
                    pe.wait_ge(S(f"row_gathered{e % 2}"), 16 * (l * NE // 2 + e // 2 + 1))
                    if e == 0:
                        for b in range(2):
                            pe.wait_ge(S(f"tbank_free{b}"), len(range(b, tidx(l, ("comb", 0)), 2)))
                    else:
                        pe.wait_ge(S("xgT_copied"), n)
                    turn_rows(e, xg[e % 2], S("x_turned"), TB)

                def gu(e):
                    n = l * NE + e
                    pe.wait_ge(S("xgT_copied"), n + 1)
                    if e == 0:
                        for b in range(2):
                            pe.wait_ge(S(f"gbank_free{b}"), len(range(b, (l + 1) * len(GEMM), 3)))
                    slots = [weights(moe_at(l, gu_pos(e, half))) for half in range(2)]
                    gate_up(slots, xgT[e % 2], S("gu_done"), S("gu_half"))

                def dn(e):
                    n = l * NE + e
                    if n >= 1:
                        pe.wait_ge(S("y_copied"), n)
                    pe.wait_ge(S("actT_copied"), n + 1)
                    s = weights(moe_at(l, dn_pos(e)))
                    down(s, actT[e % 2], S("down_done"))

                def aturn(e):
                    n = l * NE + e
                    pe.wait_ge(S("act_ready"), n + 1)
                    for k in range(4):
                        mm = pe.transpose(OB[:, k * CAP:(k + 1) * CAP], act[0:CAP, k * P:(k + 1) * P], ident[0:CAP, 0:CAP])
                    mm.then_inc(S("act_turned"), 1)

                xturn(0)
                for e in range(NE):
                    gu(e)
                    if e + 1 < NE:
                        xturn(e + 1)
                    if e >= 1:
                        dn(e - 1)
                    aturn(e)
                dn(NE - 1)
                pe.wait_ge(S("rounds_known"), l + 1)
                more = pe.value_load(nri[0:1, 0:1], min_val=0, max_val=MORE)
                for b in range(MORE):
                    with pe.If(more > b):
                        pe.wait_ge(S("experts_done"), l + 1)
                        pe.wait_ge(S(f"x_gathered{l}"), 16 * (b + 1))
                        turn_rows(0, xg[0], S(f"x_pe{l}"), TB)
                        pe.wait_ge(S(f"x_act{l}"), b * 4 + 1)
                        pe.wait_ge(S(f"x_loaded{l}"), 48 * (b + 1))
                        gate_up([0, 1], xgT[0], S(f"x_pe{l}"), None)
                        pe.wait_ge(S(f"x_dve{l}"), b + 1)
                        for k in range(4):
                            mm = pe.transpose(OB[:, k * CAP:(k + 1) * CAP], act[0:CAP, k * P:(k + 1) * P],
                                              ident[0:CAP, 0:CAP])
                        mm.then_inc(S(f"x_pe{l}"), 1)
                        pe.wait_ge(S(f"x_act{l}"), b * 4 + 3)
                        down(2, actT[0], S(f"x_pe{l}"))
                    with pe.Else():
                        pe.nop()
                for t in range(TT):
                    pe.wait_ge(S("ysum_ready"), l * TT + t + 1)
                    for i in range(2):
                        g = ("comb", t * 2 + i)
                        if t == 0:
                            pe.wait_ge(S("xgT_copied"), (l + 1) * NE)
                            bank = TB[tidx(l, g) % 2]
                        else:
                            bank = t_take(l, g)
                        for k in range(4):
                            kk = i * 4 + k
                            mm = pe.transpose(bank[:, k * P:(k + 1) * P], ysum[:, kk * P:(kk + 1) * P], ident)
                        mm.then_inc(S("tran_done"), 1)
            for k in range(KT):
                pe.wait_ge(S("sq_ready"), DEPTH * 2 * KT + k + 1)
                mm = pe.matmul(OB[:, 0:T], ones[:, :], sq[:, k % 2, :], start=(k == 0), stop=(k == KT - 1))
                if k < KT - 1:
                    mm.then_inc(S("sq_used"), 1)
            mm.then_inc(S("final_ss"), 1)
            pe.wait_ge(S("final_h"), KT)
            for t in range(TT):
                for i in range(2):
                    n = t * 2 + i
                    if n >= 2:
                        pe.wait_ge(S("y_out_copied"), n - 1)
                    for k in range(4):
                        mm = pe.transpose(SB[i][:, k * P:(k + 1) * P], hT[:, i * 4 + k, t * P:(t + 1) * P], ident)
                    mm.then_inc(S("y_out_turned"), 1)

        @block.scalar
        def _(ac):
            chain = [0]

            def link(ins):
                chain[0] += 1
                ins.then_inc(S("act_chain"), 1)
                ac.wait_ge(S("act_chain"), chain[0])

            def small_loads(l):
                rows = [(0, 0, 48, b_ada[l].rearrange("(k p) -> k p", p=P)),
                        (0, 48, 32, conv_w[l].rearrange("i (k p) -> (i k) p", p=P)),
                        (0, 80, 8, conv_b[l].rearrange("(k p) -> k p", p=P)),
                        (0, 88, 8, norm1_g[l].rearrange("(k p) -> k p", p=P)),
                        (0, 96, 8, norm2_g[l].rearrange("(k p) -> k p", p=P)),
                        (1, 0, 16, lru_ba[l].rearrange("d (k p) -> (d k) p", p=P)),
                        (1, 16, 16, lru_bx[l].rearrange("d (k p) -> (d k) p", p=P)),
                        (1, 32, 16, lru_lambda[l].rearrange("d (k p) -> (d k) p", p=P)),
                        (1, 48, 16, state_h[0, l].rearrange("d (k p) -> (d k) p", p=P))]
                for which, r0, n, src in rows:
                    ac.dma_start(vrow[r0:r0 + n, which, :], src).then_inc(S("vec_loaded"), 16)
                ac.dma_start(kcache[:, :], cache_k[0, l].rearrange("t g d -> t (g d)")).then_inc(S("cache_loaded"), 16)
                ac.dma_start(vcache[:, :], cache_v[0, l].rearrange("t g d -> t (g d)")).then_inc(S("cache_loaded"), 16)

            small_loads(0)
            ac.dma_start(rb[:, :], router_b.rearrange("(a n) -> a n", a=1).broadcast_to([P, NE])).then_inc(S("router_loaded"), 16)
            ac.dma_start(rw[:, :, :], router_w.rearrange("(k p) n -> p k n", p=P)).then_inc(S("router_loaded"), 16)
            ac.dma_start(sinkb[:, :, :].rearrange("p l h -> p (l h)"),
                         attn_sink.rearrange("(a l) h -> a (l h)", a=1).broadcast_to([P, DEPTH * HEADS])).then_inc(S("router_loaded"), 16)
            ac.wait_ge(S("cond_tran"), 1)
            ac.activation(cvec[:, :], OB[:, 0:24], ACT.Copy).then_inc(S("cvec_ready"), 1)
            ac.activation(smx[:, 0, :].rearrange("p n -> p n")[:, 0:1], OB[:, 0:1], ACT.Tanh, scale=0.5)
            ac.activation(tmp[:, 0, 0:16], OB[:, 0:16], ACT.Tanh, scale=0.5).then_inc(S("cond_tanh"), 1)
            for l in range(DEPTH):
                if l:
                    ac.wait_ge(S("vec_taken"), l)
                    ac.wait_ge(S("att_done"), l * len(UNITS))
                    small_loads(l)
                ac.wait_ge(S("lam_abs"), l + 1)
                ac.activation(sp[:, 1, :], sp[:, 0, :], ACT.Exp, scale=-1.0).then_inc(S("lam_exp"), 1)

                for cc in range(12):
                    g = ("ada", cc)
                    bank = gemm_ready(ac, l, g)
                    n = l * 12 + cc
                    if n >= 2:
                        ac.wait_ge(S("tran_done"), tidx((n - 2) // 12, ("mod", (n - 2) % 12)) + 1)
                    link(ac.activation(adap[:, cc % 2, :], bank[:, :], ACT.Copy))
                    ac.nop().then_inc(g_free(l, g), 1)
                    ac.nop().then_inc(S("ada_copied"), 1)

                def modulated(which):
                    g = (("ss1", "ss2")[which], 0)
                    bank = gemm_ready(ac, l, g)
                    link(ac.activation(rs, bank[:, 0:T], ACT.Sqrt, bias=EPS, scale=1.0 / D))
                    ac.nop().then_inc(g_free(l, g), 1)
                    ac.nop().then_inc(S("rms_ready"), 1)
                    base = (2 * l + which) * KT
                    for k in range(KT):
                        ac.wait_ge(S("xn_ready"), base + k + 1)
                        ac.activation(hT[:, k, CTX:T], hT[:, k, CTX:T], ACT.Identity,
                                      bias=modT[:, which * 24 + k, 1:2], scale=modA[:, which, k, 1:2])\
                            .then_inc(S("h_ready_a"), 1)

                modulated(0)

                def copy_out(g, dst, src_cols, sem):
                    bank = gemm_ready(ac, l, g)
                    link(ac.activation(dst, bank[:, src_cols], ACT.Copy))
                    ac.nop().then_inc(g_free(l, g), 1)
                    ac.nop().then_inc(sem, 1)

                for g in range(KVH):
                    copy_out(("k", g), kT[:, g, :], slice(0, T), S("qk_copied"))
                if l:
                    ac.wait_ge(S("cache_stored"), l * 32)
                copy_out(("kvc", 0), kvc[:, :], slice(0, 512), S("kv_copied"))
                ac.dma_start(new_k[0, l].rearrange("t g d -> t (g d)"), kvc[:, 0:256]).then_inc(S("cache_stored"), 16)
                ac.dma_start(new_v[0, l].rearrange("t g d -> t (g d)"), kvc[:, 256:512]).then_inc(S("cache_stored"), 16)
                for t in range(2):
                    copy_out(("vl", t), vl[:, t, :], slice(0, 256), S("kv_copied"))
                for h in range(HEADS):
                    copy_out(("q", h), qT[:, h, :], slice(0, T), S("qk_copied"))
                for j in range(KT):
                    bank = gemm_ready(ac, l, ("xr", j))
                    n = l * KT + j
                    if n >= 1:
                        ac.wait_ge(S("xc_ready"), n)
                    else:
                        ac.wait_ge(S("zeroed"), 1)
                    link(ac.activation(xp[:, 2:2 + CTX], bank[:, 0:CTX], ACT.Copy))
                    link(ac.activation(xp[:, 2 + LAT0:2 + CW], bank[:, CTX:T], ACT.Copy))
                    ac.nop().then_inc(g_free(l, ("xr", j)), 1)
                    ac.nop().then_inc(S("xr_copied"), 1)

                def exps(u):
                    h, b = UNITS[u]
                    n = l * len(UNITS) + u
                    w = P if b == 0 else LATK
                    ac.wait_ge(S("max_ready"), n + 1)
                    if n >= 2:
                        ac.wait_ge(S("tran_done"), tidx((n - 2) // 24, ("pt", (n - 2) % 24)) + 1)
                    ac.activation(pr[:, u % 2, 0:w], SB[u % 2][:, 0:w], ACT.Exp, bias=smx[:, u % 2, 1:2],
                                  scale=SCALE, accum_out=smx[:, u % 2, 2:3])
                    ac.activation(smx[:, u % 2, 3:4], sinkb[:, l, h:h + 1], ACT.Exp, bias=smx[:, u % 2, 1:2])\
                        .then_inc(S("exp_done"), 1)

                def pt_copy(u):
                    h, b = UNITS[u]
                    n = l * len(UNITS) + u
                    w = P if b == 0 else LATK
                    bank = tran_ready(ac, l, ("pt", u))
                    if n >= 2:
                        ac.wait_ge(S("att_done"), n - 1)
                    link(ac.activation(pt[:, u % 2, 0:w], bank[:, 0:w], ACT.Copy))
                    ac.nop().then_inc(t_free(l, ("pt", u)), 1)
                    ac.nop().then_inc(S("pt_copied"), 1)

                def att_copy(u):
                    h, b = UNITS[u]
                    ac.wait_ge(S("att_done"), l * len(UNITS) + u + 1)
                    ac.activation(qT[:, h, b * P:(b + 1) * P], OB[:, 0:P], ACT.Copy).then_inc(S("att_copied"), 1)

                def lru_tables(n):
                    d, j = PAIRS[n]
                    m = l * 16 + n
                    if m >= 2:
                        ac.wait_ge(S("lru_used"), m - 1)
                    if n < 2:
                        ac.wait_ge(S("gelu_done"), (l + 1) * KT)
                    a, th, ti = tmp[:, n % 2, :], tmp[:, 2 + n % 2, :], tmp[:, 4 + n % 2, :]
                    bank = gemm_ready(ac, l, ("gate_a", n))
                    cb = d * 8 + j
                    link(ac.activation(a, bank[:, 0:CW], ACT.Tanh, bias=hb[:, 0, cb:cb + 1], scale=0.5))
                    ac.nop().then_inc(g_free(l, ("gate_a", n)), 1)
                    ac.activation(th, a, ACT.Tanh, bias=sp[:, 7, cb:cb + 1], scale=sp[:, 7, cb:cb + 1])
                    link(ac.activation(a, a, ACT.Exp, bias=sp[:, 6, cb:cb + 1], scale=sp[:, 6, cb:cb + 1]))
                    bank = gemm_ready(ac, l, ("gate_x", n))
                    link(ac.activation(ti, bank[:, 0:CW], ACT.Tanh, bias=hb[:, 1, cb:cb + 1], scale=0.5))
                    ac.nop().then_inc(g_free(l, ("gate_x", n)), 1)
                    ac.nop().then_inc(S("lru_act"), 1)

                def lru_root(n):
                    ac.wait_ge(S("ratio_ready"), l * 16 + n + 1)
                    th = tmp[:, 2 + n % 2, :]
                    ac.activation(th, th, ACT.Sqrt, scale=0.5).then_inc(S("root_ready"), 1)

                for i in range(3 * KT):
                    kind = ("gr", "ga", "gb")[i // KT]
                    j = i % KT
                    bank = gemm_ready(ac, l, (kind, j))
                    if kind == "gr":
                        if l and j == 0:
                            ac.wait_ge(S("x_updated2"), l * 2 * KT)
                        link(ac.activation(gr[:, j, :], bank[:, 0:T], ACT.Copy))
                        ac.nop().then_inc(g_free(l, (kind, j)), 1)
                        if l * KT + j:
                            ac.wait_ge(S("gelu_done"), l * KT + j)
                        link(ac.activation(sq[:, 0, :], gr[:, j, :], ACT.Square))
                        ac.nop().then_inc(S("gelu_sq"), 1)
                        ac.wait_ge(S("gelu_arg"), l * KT + j + 1)
                        link(ac.activation(sq[:, 0, :], sq[:, 0, :], ACT.Tanh, scale=GELU_C))
                        ac.nop().then_inc(S("gelu_tanh"), 1)
                    else:
                        dst = ga if kind == "ga" else gb
                        if kind == "gb" and l == 0 and j == 0:
                            ac.wait_ge(S("rows_zero"), 16 * MORE)
                        link(ac.activation(dst[:, j, :], bank[:, 0:T], ACT.Tanh, scale=0.5))
                        ac.nop().then_inc(g_free(l, (kind, j)), 1)
                        ac.nop().then_inc(S("merge_gate"), 1)
                    exps(i)
                    if i >= 1:
                        pt_copy(i - 1)
                    if i >= 2:
                        att_copy(i - 2)
                    if i >= KT:
                        lru_tables(i - KT)
                    if i > KT:
                        lru_root(i - KT - 1)
                lru_root(15)
                pt_copy(23)
                att_copy(22)
                att_copy(23)
                modulated(1)
                for t in range(TT):
                    for i in range(2):
                        g = ("h2", t * 2 + i)
                        bank = tran_ready(ac, l, g)
                        if l and t == 0 and i == 0:
                            pass
                        link(ac.activation(grf[:, t * 1024 + i * 512:t * 1024 + (i + 1) * 512], bank[:, :], ACT.Copy))
                        ac.nop().then_inc(t_free(l, g), 1)
                    ac.dma_start(h2d[t * P:(t + 1) * P, :], grf[:, t * 1024:(t + 1) * 1024]).then_inc(S("h2_stored"), 16)
                bank = gemm_ready(ac, l, ("logits", 0))
                link(ac.activation(rt[:, 0, :, :].rearrange("p t e -> p (t e)"), bank[:, 0:TT * NE], ACT.Exp, scale=-1.0))
                ac.nop().then_inc(g_free(l, ("logits", 0)), 1)
                ac.nop().then_inc(S("router_exp"), 1)
                bank = tran_ready(ac, l, ("state", 0))
                if l:
                    ac.wait_ge(S("state_stored"), 16 * l)
                link(ac.activation(hrow[:, :], bank[0:16, 0:P], ACT.Copy))
                ac.nop().then_inc(t_free(l, ("state", 0)), 1)
                ac.dma_start(new_h[0, l].rearrange("d (k p) -> (d k) p", p=P), hrow[:, :]).then_inc(S("state_stored"), 16)

                def copy_x(e):
                    n = l * NE + e
                    ac.wait_ge(S("x_turned"), n + 1)
                    if n >= 2:
                        ac.wait_ge(S("gu_done"), n - 1)
                    for i in range(2):
                        ins = ac.activation(xgT[e % 2][:, i * 4:(i + 1) * 4, 0:CAP],
                                            TB[i][:, 0:4 * CAP].rearrange("p (k c) -> p k c", k=4), ACT.Copy)
                    ins.then_inc(S("xgT_copied"), 1)

                def tanh_g(e):
                    n = l * NE + e
                    ac.wait_ge(S("gu_done"), n + 1)
                    if n:
                        ac.wait_ge(S("act_ready"), n)
                    ac.activation(silu_t[0:CAP, :], G[0][0:CAP, :], ACT.Tanh, scale=0.5).then_inc(S("silu_tanh"), 1)

                def copy_act(e):
                    n = l * NE + e
                    ac.wait_ge(S("act_turned"), n + 1)
                    if n >= 2:
                        ac.wait_ge(S("down_done"), n - 1)
                    ac.activation(actT[e % 2][:, :, 0:CAP], OB[:, 0:4 * CAP].rearrange("p (k c) -> p k c", k=4),
                                  ACT.Copy).then_inc(S("actT_copied"), 1)

                def copy_y(e):
                    n = l * NE + e
                    ac.wait_ge(S("down_done"), n + 1)
                    if n >= 2:
                        ac.wait_ge(S(f"y_stored{e % 2}"), 16 * (n // 2))
                    for i in range(2):
                        link(ac.activation(yo[e % 2][0:CAP, i * 512:(i + 1) * 512], SB[i][0:CAP, :], ACT.Copy))
                    ac.nop().then_inc(S("y_copied"), 1)
                    ac.dma_start(yd[e * CAP:(e + 1) * CAP, :], yo[e % 2][0:CAP, :]).then_inc(S(f"y_stored{e % 2}"), 16)

                copy_x(0)
                for e in range(NE):
                    tanh_g(e)
                    if e + 1 < NE:
                        copy_x(e + 1)
                    if e >= 1:
                        copy_y(e - 1)
                    copy_act(e)
                copy_y(NE - 1)
                for b in range(2):
                    ac.wait_ge(S(f"y_stored{b}"), 16 * (l + 1) * NE // 2)
                ac.nop().then_inc(S("experts_done"), 1)
                ac.wait_ge(S("rounds_known"), l + 1)
                more = ac.value_load(nri[0:1, 0:1], min_val=0, max_val=MORE)
                for b in range(MORE):
                    with ac.If(more > b):
                        ac.wait_ge(S(f"x_pe{l}"), b * 4 + 1)
                        for i in range(2):
                            ins = ac.activation(xgT[0][:, i * 4:(i + 1) * 4, 0:CAP],
                                                TB[i][:, 0:4 * CAP].rearrange("p (k c) -> p k c", k=4), ACT.Copy)
                        ins.then_inc(S(f"x_act{l}"), 1)
                        ac.wait_ge(S(f"x_pe{l}"), b * 4 + 2)
                        ac.activation(silu_t[0:CAP, :], G[0][0:CAP, :], ACT.Tanh, scale=0.5).then_inc(S(f"x_act{l}"), 1)
                        ac.wait_ge(S(f"x_pe{l}"), b * 4 + 3)
                        ac.activation(actT[0][:, :, 0:CAP], OB[:, 0:4 * CAP].rearrange("p (k c) -> p k c", k=4),
                                      ACT.Copy).then_inc(S(f"x_act{l}"), 1)
                        ac.wait_ge(S(f"x_pe{l}"), b * 4 + 4)
                        if b:
                            ac.wait_ge(S(f"x_stored{l}"), 16 * b)
                        ac.activation(yo[0][0:CAP, 0:512], SB[0][0:CAP, :], ACT.Copy).then_inc(S(f"x_act{l}"), 1)
                        ac.activation(yo[0][0:CAP, 512:1024], SB[1][0:CAP, :], ACT.Copy).then_inc(S(f"x_y_ready{l}"), 1)
                    with ac.Else():
                        ac.nop()
            ac.wait_ge(S("final_ss"), 1)
            ac.activation(rs, OB[:, 0:T], ACT.Sqrt, bias=EPS, scale=1.0 / D).then_inc(S("rms_ready"), 1)
            for t in range(TT):
                for i in range(2):
                    n = t * 2 + i
                    ac.wait_ge(S("y_out_turned"), n + 1)
                    ac.activation(grf[:, n * 512:(n + 1) * 512], SB[i][:, :], ACT.Copy).then_inc(S("y_out_copied"), 1)
                ac.wait_ge(S("y_out_copied"), 2 * t + 2)
                dst = y_prompt[0] if t == 0 else y_sample[0, (t - 1) * P:t * P, :]
                ac.dma_start(dst, grf[:, t * 1024:(t + 1) * 1024]).then_inc(S("y_out_stored"), 16)
            ac.wait_ge(S("y_out_stored"), TT * 16)
            ac.wait_ge(S("cache_stored"), DEPTH * 32)
            ac.wait_ge(S("state_stored"), DEPTH * 16)

        @block.vector
        def _(ve):
            chain = [0]

            def link(ins):
                chain[0] += 1
                ins.then_inc(S("dve_chain"), 1)
                ve.wait_ge(S("dve_chain"), chain[0])
                return ins

            ve.memset(ones[:, :], 1.0)
            ve.memset(cpad[:, :, :], 0.0)
            ve.memset(zero_u[:, :], 0).then_inc(S("zero_ready"), 1)
            ve.memset(zrow, 0.0)
            link(ve.memset(xp[:, :], 0.0))
            ve.nop().then_inc(S("zeroed"), 1)
            ve.wait_ge(S("const_loaded"), 64)
            link(ve.tensor_copy(toku[:, :], tokid))
            ve.nop().then_inc(S("toku_ready"), 1)
            ve.wait_ge(S("cvec_ready"), 1)
            ve.wait_ge(S("cond_tanh"), 1)
            link(ve.tensor_scalar(tmp[:, 1, 0:16], tmp[:, 0, 0:16], 0.5, 0.5, ALU.mult, ALU.add))
            for st in range(2):
                link(ve.tensor_tensor(cpad[:, :, st], tmp[:, 1, st * 8:st * 8 + 8], cvec[:, st * 8:st * 8 + 8], ALU.mult))
            ve.nop().then_inc(S("cond_ready"), 1)
            for k in range(KT):
                ve.wait_ge(S("x_tran"), k + 1)
                link(ve.tensor_copy(xT[:, k, :], SB[k % 2][:, 0:T]))
                ve.nop().then_inc(S("x_taken"), 1)

            def squares(base):
                for k in range(KT):
                    if base + k >= 2:
                        m = base + k - 2
                        if m % KT != KT - 1:
                            ve.wait_ge(S("sq_used"), m // KT * (KT - 1) + m % KT + 1)
                    ve.tensor_tensor(sq[:, k % 2, :], xT[:, k, :], xT[:, k, :], ALU.mult).then_inc(S("sq_ready"), 1)

            norms = [0]

            def rstd():
                norms[0] += 1
                ve.wait_ge(S("rms_ready"), norms[0])
                link(ve.reciprocal(rs, rs))

            for l in range(DEPTH):
                bank = tran_ready(ve, l, ("vec", 0))
                ve.tensor_copy(vec[:, 0, 0:104], bank[:, 0:104])
                link(ve.tensor_copy(vec[:, 1, 0:64], bank[:, 128:192]))
                ve.nop().then_inc(t_free(l, ("vec", 0)), 1)
                ve.nop().then_inc(S("vec_taken"), 1)
                bank = tran_ready(ve, l, ("kc", 0))
                link(ve.tensor_copy(kcT[:, :, :], bank[:, 0:256].rearrange("p (g t) -> p g t", g=2)))
                ve.nop().then_inc(t_free(l, ("kc", 0)), 1)
                link(ve.tensor_scalar(sp[:, 3, :], v_lam, -1.0, 0.0, ALU.mult, ALU.max))
                link(ve.tensor_scalar(sp[:, 2, :], v_lam, -1.0, None, ALU.mult))
                link(ve.tensor_tensor(sp[:, 0, :], sp[:, 2, :], v_lam, ALU.max))
                ve.nop().then_inc(S("lam_abs"), 1)
                ve.wait_ge(S("lam_exp"), l + 1)
                link(ve.tensor_scalar(sp[:, 2, :], sp[:, 1, :], 2.0, None, ALU.add))
                link(ve.reciprocal(sp[:, 4, :], sp[:, 2, :]))
                link(ve.tensor_tensor(sp[:, 4, :], sp[:, 4, :], sp[:, 1, :], ALU.mult))
                link(ve.tensor_tensor(sp[:, 5, :], sp[:, 4, :], sp[:, 4, :], ALU.mult))
                link(ve.tensor_scalar(sp[:, 2, :], sp[:, 5, :], 1.0 / 19, 1.0 / 17, ALU.mult, ALU.add))
                for m in range(15, 0, -2):
                    link(ve.tensor_tensor(sp[:, 2, :], sp[:, 2, :], sp[:, 5, :], ALU.mult))
                    link(ve.tensor_scalar(sp[:, 2, :], sp[:, 2, :], 1.0 / m, None, ALU.add))
                link(ve.tensor_tensor(sp[:, 2, :], sp[:, 2, :], sp[:, 4, :], ALU.mult))
                link(ve.scalar_tensor_tensor(sp[:, 2, :], sp[:, 2, :], 2.0, sp[:, 3, :], ALU.mult, ALU.add))
                link(ve.tensor_scalar(sp[:, 6, :], sp[:, 2, :], -4.0, None, ALU.mult))
                link(ve.tensor_scalar(sp[:, 7, :], sp[:, 2, :], 4.0, None, ALU.mult))
                link(ve.tensor_scalar(hb[:, 0, :], v_ba, 0.5, None, ALU.mult))
                link(ve.tensor_scalar(hb[:, 1, :], v_bx, 0.5, None, ALU.mult))
                if l == 0:
                    ve.wait_ge(S("router_loaded"), 48)
                link(ve.tensor_scalar(nsink[:, :], sinkb[:, l, :], -1.0, None, ALU.mult))
                ve.nop().then_inc(S("lru_consts"), 1)
                for cc in range(12):
                    bank = tran_ready(ve, l, ("mod", cc))
                    for st in range(2):
                        link(ve.tensor_tensor(modT[:, cc * 4:cc * 4 + 4, st],
                                              bank[:, 0:8].rearrange("p (j s) -> p j s", s=2)[:, :, st],
                                              v_ada(cc * 4, cc * 4 + 4), ALU.add))
                    ve.nop().then_inc(t_free(l, ("mod", cc)), 1)
                for st in range(2):
                    for a, (sc, g) in enumerate(((8, n1g), (32, n2g))):
                        link(ve.scalar_tensor_tensor(modA[:, a, :, st], modT[:, sc:sc + 8, st], 1.0, g, ALU.add, ALU.mult))
                    link(ve.tensor_scalar(modA[:, 2, :, st], modT[:, 16:24, st], 0.5, None, ALU.mult))
                    link(ve.tensor_copy(modA[:, 3, :, st], modT[:, 40:48, st]))

                def modulated(which):
                    g = ("ss1", "ss2")[which]
                    rstd()
                    for k in range(KT):
                        link(ve.tensor_tensor(hT[:, k, :], xT[:, k, :], rs, ALU.mult))
                        ve.nop().then_inc(S("xn_ready"), 1)
                        ve.tensor_scalar(hT[:, k, 0:CTX], hT[:, k, 0:CTX], modA[:, which, k, 0:1],
                                         modT[:, which * 24 + k, 0:1], ALU.mult, ALU.add).then_inc(S("h_ready_v"), 1)

                squares(2 * l * KT)
                modulated(0)

                def rope(kind, i):
                    bank = gemm_ready(ve, l, (kind, i))
                    x = (kT if kind == "krot" else qT)[:, i, CTX:T]
                    link(ve.tensor_tensor(tmp[:, 6, 0:LAT], bank[:, 0:LAT], sinT, ALU.mult))
                    ve.nop().then_inc(g_free(l, (kind, i)), 1)
                    link(ve.tensor_tensor(x, x, cosT, ALU.mult))
                    link(ve.tensor_tensor(x, x, tmp[:, 6, 0:LAT], ALU.add))
                    ve.nop().then_inc(S("rope_done"), 1)

                for i in range(2):
                    rope("krot", i)
                for i in range(6):
                    rope("qrot", i)

                def conv(j):
                    ve.wait_ge(S("xr_copied"), l * KT + j + 1)
                    x = xp[:, :]
                    link(ve.tensor_scalar(xc[:, j, :], x[:, 0:CW], v_conv(0, j), v_convb(j), ALU.mult, ALU.add))
                    for i in range(1, 4):
                        ins = ve.scalar_tensor_tensor(xc[:, j, :], x[:, i:i + CW], v_conv(i, j), xc[:, j, :], ALU.mult, ALU.add)
                        if i < 3:
                            link(ins)
                    ins.then_inc(S("xc_ready"), 1)

                rope("qrot", 6)
                conv(0)
                rope("qrot", 7)
                for j in range(1, KT):
                    conv(j)

                def softmax_max(u):
                    h, b = UNITS[u]
                    n = l * len(UNITS) + u
                    w = P if b == 0 else LATK
                    ve.wait_ge(S("scores_done"), n + 1)
                    if b:
                        cols = slice(P, LAT) if b == 1 else slice(0, P)
                        link(ve.tensor_tensor(SB[u % 2][:, cols], SB[u % 2][:, cols], mask[b - 1], ALU.add))
                    link(ve.tensor_reduce(smx[:, u % 2, 0:1], SB[u % 2][:, 0:w], AX.X, ALU.max))
                    ve.tensor_scalar(smx[:, u % 2, 1:2], smx[:, u % 2, 0:1], -SCALE, nsink[:, h:h + 1], ALU.mult, ALU.min)\
                        .then_inc(S("max_ready"), 1)

                def softmax_norm(u):
                    h, b = UNITS[u]
                    w = P if b == 0 else LATK
                    ve.wait_ge(S("exp_done"), l * len(UNITS) + u + 1)
                    link(ve.tensor_tensor(smx[:, u % 2, 4:5], smx[:, u % 2, 2:3], smx[:, u % 2, 3:4], ALU.add))
                    link(ve.reciprocal(smx[:, u % 2, 5:6], smx[:, u % 2, 4:5]))
                    ve.tensor_scalar(pr[:, u % 2, 0:w], pr[:, u % 2, 0:w], smx[:, u % 2, 5:6], None, ALU.mult)\
                        .then_inc(S("probs_ready"), 1)

                def ratio(n):
                    ve.wait_ge(S("lru_act"), l * 16 + n + 1)
                    th, w = tmp[:, 2 + n % 2, :], tmp[:, 6, :]
                    link(ve.tensor_scalar(w, th, 1.0, None, ALU.add))
                    link(ve.reciprocal(w, w))
                    link(ve.tensor_tensor(th, w, th, ALU.mult))
                    ve.nop().then_inc(S("ratio_ready"), 1)

                def scan(n):
                    d, j = PAIRS[n]
                    m = l * 16 + n
                    a, th, ti, w = tmp[:, n % 2, :], tmp[:, 2 + n % 2, :], tmp[:, 4 + n % 2, :], tmp[:, 6, :]
                    link(ve.scalar_tensor_tensor(ti, ti, 1.0, xc[:, j, :], ALU.add, ALU.mult))
                    ve.wait_ge(S("root_ready"), m + 1)
                    link(ve.tensor_tensor(w, th, ti, ALU.mult))
                    dst = hyb[:, :] if d == 0 else ti
                    for st in range(2):
                        cs = slice(0, CTX) if st == 0 else slice(LAT0, CW)
                        init = 0.0 if st == 0 else v_state(d, j)
                        aa, ww, oo = a[:, cs], w[:, cs], dst[:, cs]
                        if d == 1:
                            aa, ww, oo = aa[:, ::-1], ww[:, ::-1], oo[:, ::-1]
                        link(ve.tensor_tensor_scan(oo, aa, ww, init, ALU.mult, ALU.add))
                    last = dst[:, CTX - 1:CTX] if d == 0 else dst[:, 0:1]
                    if l and n == 0:
                        ve.wait_ge(S("tran_done"), tidx(l - 1, ("state", 0)) + 1)
                    link(ve.tensor_copy(hlast[:, d * 8 + j:d * 8 + j + 1], last))
                    ve.nop().then_inc(S("hlast_ready"), 1)
                    if d == 1:
                        for st in range(2):
                            cs = slice(0, CTX) if st == 0 else slice(LAT0, CW)
                            link(ve.tensor_tensor(w[:, cs], hyb[:, cs], ti[:, cs], ALU.add))
                            ins = ve.scalar_tensor_tensor(gr[:, j, STREAM[st]], gr[:, j, STREAM[st]], 0.5, w[:, cs],
                                                          ALU.mult, ALU.mult)
                            link(ins)
                        ve.nop().then_inc(S("rnn_ready"), 1)
                    ve.nop().then_inc(S("lru_used"), 1)

                for i in range(3 * KT):
                    kind = ("gr", "ga", "gb")[i // KT]
                    j = i % KT
                    if kind == "gr":
                        ve.wait_ge(S("gelu_sq"), l * KT + j + 1)
                        link(ve.tensor_scalar(sq[:, 0, :], sq[:, 0, :], 0.044715, 1.0, ALU.mult, ALU.add))
                        link(ve.tensor_tensor(sq[:, 0, :], sq[:, 0, :], gr[:, j, :], ALU.mult))
                        ve.nop().then_inc(S("gelu_arg"), 1)
                        ve.wait_ge(S("gelu_tanh"), l * KT + j + 1)
                        link(ve.scalar_tensor_tensor(gr[:, j, :], sq[:, 0, :], 1.0, gr[:, j, :], ALU.add, ALU.mult))
                        ve.nop().then_inc(S("gelu_done"), 1)
                    softmax_max(i)
                    softmax_norm(i)
                    if i >= KT:
                        ratio(i - KT)
                    if i > KT:
                        scan(i - KT - 1)
                scan(15)

                for n in range(KT):
                    bank = gemm_ready(ve, l, ("ap", n))
                    if n == 0:
                        ve.wait_ge(S("merge_gate"), (l + 1) * 2 * KT)
                    link(ve.scalar_tensor_tensor(ga[:, n, :], ga[:, n, :], 1.0, bank[:, 0:T], ALU.add, ALU.mult))
                    ve.nop().then_inc(g_free(l, ("ap", n)), 1)
                for n in range(KT):
                    bank = gemm_ready(ve, l, ("rp", n))
                    link(ve.scalar_tensor_tensor(gb[:, n, :], gb[:, n, :], 1.0, bank[:, 0:T], ALU.add, ALU.mult))
                    ve.nop().then_inc(g_free(l, ("rp", n)), 1)
                    ve.tensor_tensor(ga[:, n, :], ga[:, n, :], gb[:, n, :], ALU.add).then_inc(S("merged_ready"), 1)
                for n in range(KT):
                    bank = gemm_ready(ve, l, ("wo", n))
                    for st in range(2):
                        link(ve.scalar_tensor_tensor(xT[:, n, STREAM[st]], bank[:, STREAM[st]], modA[:, 2, n, st:st + 1],
                                                     xT[:, n, STREAM[st]], ALU.mult, ALU.add))
                    ve.nop().then_inc(g_free(l, ("wo", n)), 1)
                squares((2 * l + 1) * KT)
                modulated(1)

                ve.wait_ge(S("router_exp"), l + 1)
                R = lambda i: rt[:, i, :, :]
                bc_e = lambda v: v.rearrange("p (a e) -> p a e", a=1).broadcast_to([P, TT, NE])
                link(ve.tensor_scalar(R(0), R(0), 1.0, None, ALU.add))
                link(ve.reciprocal(R(1), R(0)))
                link(ve.tensor_tensor(R(2), R(1), bc_e(rb[:, :]), ALU.add))
                quad = rt[:, 2, :, :].rearrange("p t (g i) -> p (t g) i", i=EG)
                q4 = lambda i: rt4[:, i, :]
                mx, mn = ALU.max, ALU.min
                link(ve.tensor_tensor(q4(0), quad[:, :, 0], quad[:, :, 1], mx))
                link(ve.tensor_tensor(q4(1), quad[:, :, 0], quad[:, :, 1], mn))
                link(ve.tensor_tensor(q4(2), quad[:, :, 2], quad[:, :, 3], mx))
                link(ve.tensor_tensor(q4(3), quad[:, :, 2], quad[:, :, 3], mn))
                link(ve.tensor_tensor(q4(4), q4(0), q4(2), mx))
                link(ve.tensor_tensor(q4(5), q4(0), q4(2), mn))
                link(ve.tensor_tensor(q4(6), q4(1), q4(3), mx))
                link(ve.tensor_tensor(q4(6), q4(5), q4(6), mx))
                link(ve.tensor_tensor(q4(4), q4(4), q4(6), ALU.add))
                g3 = lambda i: rt4[:, i, :].rearrange("p (t g) -> p t g", g=NG)
                r1 = lambda i: rt1[:, i, :]
                bc1 = lambda v, w: v.rearrange("p (t a) -> p t a", a=1).broadcast_to([P, TT, w])
                bg = iota_g.rearrange("p (a g) -> p a g", a=1).broadcast_to([P, TT, NG])
                link(ve.tensor_reduce(r1(0), g3(4), AX.X, mx))
                link(ve.tensor_tensor(g3(5), g3(4), bc1(r1(0), NG), ALU.is_equal))
                link(ve.tensor_tensor(g3(5), g3(5), bg, ALU.mult))
                link(ve.tensor_reduce(r1(1), g3(5), AX.X, mx))
                link(ve.tensor_tensor(g3(6), g3(5), bc1(r1(1), NG), ALU.is_equal))
                in_grp = rt4[:, 6, :].rearrange("p (g a) -> p g a", a=1).broadcast_to([P, TT * NG, EG])
                r3 = lambda i: rt[:, i, :, :].rearrange("p t (g i) -> p (t g) i", i=EG)
                link(ve.tensor_tensor(r3(3), r3(2), in_grp, ALU.mult))
                link(ve.tensor_scalar(q4(7), q4(6), BIG, -BIG, ALU.mult, ALU.add))
                off = rt4[:, 7, :].rearrange("p (g a) -> p g a", a=1).broadcast_to([P, TT * NG, EG])
                link(ve.tensor_tensor(r3(3), r3(3), off, ALU.add))
                for pick in range(2):
                    hot = R(6 + pick)
                    link(ve.tensor_reduce(r1(2), R(3), AX.X, mx))
                    link(ve.tensor_tensor(R(4), R(3), bc1(r1(2), NE), ALU.is_equal))
                    link(ve.tensor_tensor(R(4), R(4), bc_e(iota_e), ALU.mult))
                    link(ve.tensor_reduce(r1(3), R(4), AX.X, mx))
                    link(ve.tensor_tensor(hot, R(4), bc1(r1(3), NE), ALU.is_equal))
                    if pick == 0:
                        link(ve.scalar_tensor_tensor(R(3), hot, -BIG, R(3), ALU.mult, ALU.add))
                    link(ve.tensor_tensor(R(5), hot, R(1), ALU.mult))
                    link(ve.tensor_reduce(r1(4 + pick), R(5), AX.X, ALU.add))
                link(ve.tensor_tensor(R(8), R(6), R(7), ALU.add))
                ve.nop().then_inc(S("picked"), 1)
                link(ve.tensor_tensor(r1(6), r1(4), r1(5), ALU.add))
                link(ve.reciprocal(r1(7), r1(6)))
                for pick in range(2):
                    link(ve.tensor_tensor(gates[:, pick, :], r1(4 + pick), r1(7), ALU.mult))
                bank = tran_ready(ve, l, ("rank", 0))
                ranks = bank[:, 0:TT * NE].rearrange("p (t e) -> p t e", e=NE)
                rows = bank[:, TT * NE:(TT + 1) * NE]
                e_more, e_upto, e_shift = (rt[:, 12, i, :] for i in range(3))
                e_tmp = rt[:, 13, 0, :]
                link(ve.tensor_scalar(e_more, rows, float(CAP), None, ALU.is_gt))
                for k in range(2, T // CAP):
                    link(ve.tensor_scalar(e_tmp, rows, float(CAP * k), None, ALU.is_gt))
                    link(ve.tensor_tensor(e_more, e_more, e_tmp, ALU.add))
                link(ve.tensor_tensor_scan(e_upto, ones[:, 0:NE], e_more, 0.0, ALU.mult, ALU.add))
                link(ve.tensor_tensor(e_shift, e_upto, e_more, ALU.subtract))
                link(ve.scalar_tensor_tensor(e_shift, e_shift, float(NE), num_e, ALU.add, ALU.subtract))
                link(ve.tensor_copy(nri[0:1, 0:1], e_upto[0:1, NE - 1:NE]))
                for b in range(MORE):
                    link(ve.tensor_scalar(e_tmp[0:1, :], e_upto[0:1, :], float(b), None, ALU.is_le))
                    link(ve.tensor_reduce(nrt[0:1, 0:1], e_tmp[0:1, :], AX.X, ALU.add))
                    link(ve.tensor_scalar(nri[0:1, 1 + b:2 + b], nrt[0:1, 0:1], float(NE - 1), None, ALU.min))
                ve.nop().then_inc(S("rounds_known"), 1)
                link(ve.tensor_scalar(R(11), ranks, float(CAP), None, ALU.is_ge))
                link(ve.tensor_tensor(R(9), R(11), bc_e(e_shift), ALU.mult))
                link(ve.tensor_tensor(R(9), R(9), bc_e(num_e), ALU.add))
                link(ve.scalar_tensor_tensor(R(10), R(11), -float(CAP), ranks, ALU.mult, ALU.add))
                for k in range(2, T // CAP):
                    link(ve.tensor_scalar(R(11), ranks, float(CAP * k), None, ALU.is_ge))
                    link(ve.tensor_tensor(R(9), R(9), R(11), ALU.add))
                    link(ve.scalar_tensor_tensor(R(10), R(11), -float(CAP), R(10), ALU.mult, ALU.add))
                ve.nop().then_inc(t_free(l, ("rank", 0)), 1)
                if l:
                    for pick in range(2):
                        ve.wait_ge(S(f"back{pick}"), 16 * l * TT)
                for pick in range(2):
                    link(ve.tensor_tensor(R(5), R(9), R(6 + pick), ALU.mult))
                    link(ve.tensor_reduce(r1(8), R(5), AX.X, ALU.add))
                    link(ve.tensor_tensor(R(5), R(10), R(6 + pick), ALU.mult))
                    link(ve.tensor_reduce(r1(9), R(5), AX.X, ALU.add))
                    link(ve.scalar_tensor_tensor(posu[:, pick, :], r1(8), float(CAP), r1(9), ALU.mult, ALU.add))
                    link(ve.scalar_tensor_tensor(slotu[:, pick, :], r1(9), float(BLOCKS), r1(8), ALU.mult, ALU.add))
                ve.nop().then_inc(S("pos_ready"), 1)

                for e in range(NE):
                    n = l * NE + e
                    ve.wait_ge(S("silu_tanh"), n + 1)
                    if n:
                        ve.wait_ge(S("act_turned"), n)
                    link(ve.scalar_tensor_tensor(silu_t[0:CAP, :], silu_t[0:CAP, :], 1.0, G[0][0:CAP, :], ALU.add, ALU.mult))
                    ve.scalar_tensor_tensor(act[0:CAP, :], silu_t[0:CAP, :], 0.5, G[1][0:CAP, :], ALU.mult, ALU.mult)\
                        .then_inc(S("act_ready"), 1)
                more = ve.value_load(nri[0:1, 0:1], min_val=0, max_val=MORE)
                for b in range(MORE):
                    with ve.If(more > b):
                        ve.wait_ge(S(f"x_act{l}"), b * 4 + 2)
                        ve.scalar_tensor_tensor(silu_t[0:CAP, :], silu_t[0:CAP, :], 1.0, G[0][0:CAP, :], ALU.add, ALU.mult)\
                            .then_inc(S(f"x_silu{l}"), 1)
                        ve.wait_ge(S(f"x_silu{l}"), b + 1)
                        ve.scalar_tensor_tensor(act[0:CAP, :], silu_t[0:CAP, :], 0.5, G[1][0:CAP, :], ALU.mult, ALU.mult)\
                            .then_inc(S(f"x_dve{l}"), 1)
                    with ve.Else():
                        ve.nop()
                for t in range(TT):
                    ve.wait_ge(S("back0"), 16 * (l * TT + t + 1))
                    ve.wait_ge(S("back1"), 16 * (l * TT + t + 1))
                    if t:
                        ve.wait_ge(S("tran_done"), tidx(l, ("comb", 2 * t - 1)) + 1)
                    link(ve.tensor_scalar(ysum, yg[0], gates[:, 0, t:t + 1], None, ALU.mult))
                    link(ve.scalar_tensor_tensor(ysum, yg[1], gates[:, 1, t:t + 1], ysum, ALU.mult, ALU.add))
                    ve.nop().then_inc(S("ysum_ready"), 1)
                    st = 0 if t == 0 else 1
                    for i in range(2):
                        g = ("comb", t * 2 + i)
                        bank = tran_ready(ve, l, g)
                        for k in range(4):
                            kk = i * 4 + k
                            x = xT[:, kk, t * P:(t + 1) * P]
                            link(ve.scalar_tensor_tensor(x, bank[:, k * P:(k + 1) * P], modA[:, 3, kk, st:st + 1], x,
                                                         ALU.mult, ALU.add))
                        ve.nop().then_inc(t_free(l, g), 1)
                ve.nop().then_inc(S("x_updated2"), 2 * KT)
            squares(DEPTH * 2 * KT)
            rstd()
            for k in range(KT):
                link(ve.tensor_tensor(hT[:, k, :], xT[:, k, :], rs, ALU.mult))
                ve.tensor_scalar(hT[:, k, :], hT[:, k, :], cvec[:, 16 + k:17 + k], None, ALU.mult).then_inc(S("final_h"), 1)

        @block.gpsimd
        def _(po):
            po.memset(gatew[:, :, :, :], 0.0).then_inc(S("gatew_zero"), 1)
            po.wait_ge(S("gatew_zero"), 1)
            po.wait_ge(S("zero_ready"), 1)
            po.dma_start(idtab.rearrange("(p n) a -> p (n a)", p=CAP), zero_u[0:CAP, :]).then_inc(S("idtab_zero"), 16)
            po.wait_ge(S("toku_ready"), 1)
            po.wait_ge(S("zeroed"), 1)
            for b in range(MORE):
                row = (NE + b) * CAP
                po.dma_start(yd[row:row + CAP, :], zrow[0:CAP, :]).then_inc(S("rows_zero"), 16)
            for l in range(DEPTH):
                for n, (d, j) in enumerate(PAIRS):
                    m = l * 16 + n
                    if m >= 2:
                        q = m - 2
                        po.wait_ge(S("gemm_done"), gidx(q // 16, ("gate_x", q % 16)) + 1)
                    for which, w in enumerate((lru_wa, lru_wx)):
                        for half in range(2):
                            po.dma_start(gatew[half * 64:half * 64 + 64, which, n % 2, half * 64:half * 64 + 64],
                                         w[l, d, 2 * j + half]).then_inc(S(f"gatew_loaded{n % 2}"), 16)
                po.wait_ge(S("pos_ready"), l + 1)
                po.wait_ge(S("idtab_zero"), 16)
                if l:
                    po.wait_ge(S("rounds_over"), l)
                for pick in range(2):
                    for t in range(TT):
                        po.indirect_dma_start(out=idtab[:, :], out_offset=bass.IndirectOffsetOnAxis(ap=slotu[:, pick, t:t + 1], axis=0),
                                              in_=toku[:, t:t + 1], in_offset=None).then_inc(S("ids_placed"), 16)
                po.wait_ge(S("ids_placed"), (l + 1) * 2 * TT * 16)
                po.dma_start(ids[0:CAP, :], idtab.rearrange("(r e) a -> r (e a)", e=BLOCKS)).then_inc(S("ids_loaded"), 16)
                po.wait_ge(S("ids_loaded"), (l + 1) * 16)
                po.wait_ge(S("h2_stored"), (l + 1) * TT * 16)

                def gather(dst, idx, sem):
                    po.indirect_dma_start(out=dst, out_offset=None, in_=h2d[:, :],
                                          in_offset=bass.IndirectOffsetOnAxis(ap=idx, axis=0)).then_inc(sem, 16)

                for e in range(NE):
                    n = l * NE + e
                    if e >= 2:
                        po.wait_ge(S("x_turned"), n - 1)
                    gather(xg[e % 2][0:CAP, :], ids[0:CAP, e:e + 1], S(f"row_gathered{e % 2}"))
                po.wait_ge(S("rounds_known"), l + 1)
                more = po.value_load(nri[0:1, 0:1], min_val=0, max_val=MORE)
                for b in range(MORE):
                    with po.If(more > b):
                        po.wait_ge(S("experts_done"), l + 1)
                        if b:
                            po.wait_ge(S(f"x_pe{l}"), 4 * b)
                        gather(xg[0][0:CAP, :], ids[0:CAP, NE + b:NE + b + 1], S(f"x_gathered{l}"))
                    with po.Else():
                        po.nop()
                po.wait_ge(S("experts_done"), l + 1)
                po.wait_ge(S("rounds_over"), l + 1)
                po.wait_ge(S("rows_zero"), 16 * MORE)
                for t in range(TT):
                    if t:
                        po.wait_ge(S("ysum_ready"), l * TT + t)
                    for pick in range(2):
                        po.indirect_dma_start(out=yg[pick], out_offset=None, in_=yd[:, :],
                                              in_offset=bass.IndirectOffsetOnAxis(ap=posu[:, pick, t:t + 1], axis=0))\
                            .then_inc(S(f"back{pick}"), 16)


_INS = ["x_prompt", "x_sample", "cache_k", "cache_v", "state_h", "c", "c_ctx", "norm1_g", "norm2_g", "w_ada",
        "b_ada", "w_in", "conv_w", "conv_b", "lru_wa", "lru_ba", "lru_wx", "lru_bx", "lru_lambda", "attn_sink",
        "w_attn_proj", "w_rnn_proj", "w_out", "router_w", "router_b", "w_gate_up", "w_down", "final_norm_g"]
_OUTS = [(1, CTX, D), (1, LAT, D), (1, DEPTH, CTX, KVH, HD), (1, DEPTH, CTX, KVH, HD), (1, DEPTH, 2, D)]


def shape_constants():
    ident = np.eye(P, dtype=np.float32)
    rot = np.zeros((P, P), np.float32)
    half = HD // 2
    for i in range(half):
        rot[half + i, i] = -1.0
        rot[i, half + i] = 1.0
    t = np.arange(LAT)
    inv = (np.float32(10000.0) ** (-np.arange(HD // 4, dtype=np.float32) / np.float32(HD // 4))).astype(np.float32)
    ang = np.concatenate([(t // 64).astype(np.float32)[:, None] * inv, (t % 64).astype(np.float32)[:, None] * inv], 1)
    ang = np.concatenate([ang, ang], 1).T.astype(np.float32)
    i, j = np.meshgrid(np.arange(P), np.arange(P), indexing="ij")
    m0 = np.where(j <= i, 0.0, -BIG)
    m1 = np.where(j >= i, 0.0, -BIG)
    before = (i < j).astype(np.float32)
    sumsel = np.zeros((P, 2))
    sumsel[0::32, 0] = 1
    sumsel[1::32, 1] = 1
    row = lambda v: np.tile(np.asarray(v, np.float32)[None, :], (P, 1))
    tok = np.arange(T).reshape(TT, P).T
    parts = [ident, rot, np.cos(ang), np.sin(ang), m0, m1, before, sumsel, row(NE - np.arange(NE)),
             row(NG - np.arange(NG)), tok, row(np.arange(NE))]
    return np.concatenate([np.asarray(p, np.float32) for p in parts], 1)


def kernel(**inputs):
    import concourse.bacc as _bacc
    from concourse.bass_utils import run_bass_kernel_spmd as _run

    nc = _bacc.Bacc("TRN2", target_bir_lowering=False, num_devices=1)
    arrays, args = {}, []
    for name in _INS:
        a = np.ascontiguousarray(inputs[name])
        arrays[f"in_{name}"] = a
        args.append(nc.dram_tensor(f"in_{name}", a.shape, mybir.dt.from_np(a.dtype), kind="ExternalInput").ap())
    a = shape_constants()
    arrays["shape_constants"] = a
    args.append(nc.dram_tensor("shape_constants", a.shape, F32, kind="ExternalInput").ap())
    for i, shape in enumerate(_OUTS):
        args.append(nc.dram_tensor(f"out_{i}", shape, F32, kind="ExternalOutput").ap())
    build(nc, *args)
    r = _run(nc, [arrays], core_ids=[0])
    return tuple(r.results[0][f"out_{i}"] for i in range(len(_OUTS)))
```

```python
import math
from contextlib import ExitStack

import numpy as np
import concourse.bass as bass
from concourse import mybir

F32 = mybir.dt.float32
U32 = mybir.dt.uint32
I32 = mybir.dt.int32
ALU = mybir.AluOpType
ACT = mybir.ActivationFunctionType
AX = mybir.AxisListType

P = 128
D = 1024
KT = D // P
DEPTH = 2
CTX, LAT = 128, 256
T = CTX + LAT
TT = T // P
HEADS, KVH, HD = 8, 2, 128
GRP = HEADS // KVH
SCALE = HD ** -0.5
LATK = LAT + P
NADA = 6
NE, NG, EG = 16, 4, 4
DE = 512
EPS = 1e-6
CHUNK = 512
SLOTS = 4
CAP = 128
MORE = (2 * T - 1) // CAP
BLOCKS = NE + MORE
SEG = 3
CW = CTX + SEG + LAT
XW = CW + 3
LAT0 = CTX + SEG
GELU_C = math.sqrt(2.0 / math.pi)
BIG = 1e30

W_IN_COL = {"q0": 0, "q1": 512, "kv": 1024, "xr0": 1536, "xr1": 2048, "gr0": 2560, "gr1": 3072,
            "ga0": 3584, "ga1": 4096, "gb0": 4608, "gb1": 5120}
ADA_FIRST, ADA_LATE = range(4), range(10, 12)


def chunk_order():
    o = [(0, f"ada{c}") for c in ADA_FIRST]
    for l in range(DEPTH):
        o += [(l, n) for n in ("kv", "q0", "ada4", "q1", "ada5", "xr0", "ada6", "xr1", "ada7", "gr0", "ada8",
                               "gr1", "ada9", "ga0", "ga1", "gb0", "gb1", "ap0", "ap1", "rp0", "rp1", "wo0",
                               "wo1")]
        o += [(l, f"ada{c}") for c in ADA_LATE]
        if l + 1 < DEPTH:
            o += [(l + 1, f"ada{c}") for c in ADA_FIRST]
        for e in range(NE):
            o += [(l, f"gu{e}.0"), (l, f"gu{e}.1")]
            if e:
                o.append((l, f"dn{e - 1}"))
        o.append((l, f"dn{NE - 1}"))
    return o


CHUNKS = chunk_order()
CHUNK_AT = {c: n for n, c in enumerate(CHUNKS)}

UNITS = [(h, b) for h in range(HEADS) for b in range(3)]
PAIRS = [(d, j) for j in range(KT) for d in range(2)]


def gemm_order():
    o = [(0, "ada", c) for c in ADA_FIRST]
    for l in range(DEPTH):
        o += [(l, "k", 0), (l, "k", 1), (l, "kvc", 0), (l, "vl", 0), (l, "vl", 1)]
        for h in range(HEADS):
            o += [(l, "q", h), (l, "krot", h) if h < 2 else (l, "qrot", h - 2)]
            if h % 4 == 3:
                o.append((l, "ada", 4 + h // 4))
        for j in range(KT):
            o.append((l, "xr", j))
            if j < 2:
                o.append((l, "qrot", 6 + j))
            if j % 4 == 3:
                o.append((l, "ada", 6 + j // 4))
        for i in range(3 * KT):
            o.append((l, ("gr", "ga", "gb")[i // KT], i % KT))
            if i in (3, 7):
                o.append((l, "ada", 8 + i // 4))
            if i >= KT:
                o += [(l, "gate_a", i - KT), (l, "gate_x", i - KT)]
        o += [(l, kind, n) for kind in ("ap", "rp", "wo") for n in range(KT)]
        o += [(l, "logits", 0)] + [(l, "ada", c) for c in ADA_LATE]
        if l + 1 < DEPTH:
            o += [(l + 1, "ada", c) for c in ADA_FIRST]
    return o


def tran_order():
    o = [(l, "vec", 0) for l in range(DEPTH)] + [(l, "kc", 0) for l in range(DEPTH)]
    o += [(0, "mod", c) for c in ADA_FIRST]
    for l in range(DEPTH):
        o += [(l, "mod", c) for c in range(4, 8)]
        for i in range(len(UNITS)):
            o.append((l, "pt", i))
            if i in (3, 7):
                o.append((l, "mod", 8 + i // 4))
        o += [(l, "h2", i) for i in range(2 * TT)] + [(l, "state", 0), (l, "rank", 0)]
        o += [(l, "mod", c) for c in ADA_LATE]
        if l + 1 < DEPTH:
            o += [(l + 1, "mod", c) for c in ADA_FIRST]
        o += [(l, "ids", 0)]
        o += [(l, "comb", i) for i in range(2 * TT)]
    return o


G_AT = {g: n for n, g in enumerate(gemm_order())}
T_AT = {g: n for n, g in enumerate(tran_order())}


def build(nc, x_prompt, x_sample, cache_k, cache_v, state_h, c, c_ctx, norm1_g, norm2_g, w_ada, b_ada,
          w_in, conv_w, conv_b, lru_wa, lru_ba, lru_wx, lru_bx, lru_lambda, attn_sink, w_attn_proj,
          w_rnn_proj, w_out, router_w, router_b, w_gate_up, w_down, final_norm_g,
          consts, y_prompt, y_sample, new_k, new_v, new_h):
    ctx = ExitStack()
    with ctx:
        def sb(name, shape, dt=F32):
            return ctx.enter_context(nc.sbuf_tensor(name, shape, dt))

        sems = {}

        def S(name):
            if name not in sems:
                sems[name] = ctx.enter_context(nc.semaphore(name))
            return sems[name]

        ring = sb("ring", [P, SLOTS, KT * CHUNK])
        xT = sb("xT", [P, KT, T])
        hT = sb("hT", [P, KT, T])
        qT = sb("qT", [P, HEADS, T])
        kT = sb("kT", [P, KVH, T])
        kcT = sb("kcT", [P, DEPTH, KVH, P])
        kvc = sb("kvc", [P, 512])
        vl = sb("vl", [P, 2, 256])
        vcache = sb("vcache", [P, DEPTH, 256])
        xp = sb("xp", [P, XW])
        xc = sb("xc", [P, KT, CW])
        gr = sb("gr", [P, KT, T])
        ga = sb("ga", [P, KT, T])
        gb = sb("gb", [P, KT, T])
        con = sb("con", [P, consts.shape[1]])
        ident, rotm, cosT, sinT = con[:, 0:128], con[:, 128:256], con[:, 256:512], con[:, 512:768]
        mask = [con[:, 768:896], con[:, 896:1024]]
        before = con[:, 1024:1152]
        sumsel = con[:, 1152:1154]
        iota_e = con[:, 1154:1170]
        iota_g = con[:, 1170:1174]
        tokid = con[:, 1174:1177]
        num_e = con[:, 1177:1193]
        num_b = con[:, 1193:1193 + BLOCKS]
        num_c = con[:, 1193 + BLOCKS:1193 + BLOCKS + CAP]
        ones = sb("ones", [P, P])
        vec = sb("vec", [P, DEPTH, 2, P])
        crow = sb("crow", [24, P])
        cvec = sb("cvec", [P, 24])
        cpad = sb("cpad", [P, KT, 32])
        modT = sb("modT", [P, 48, 2])
        modA = sb("modA", [P, 4, KT, 2])
        sinkb = sb("sinkb", [P, DEPTH, HEADS])
        nsink = sb("nsink", [P, DEPTH, HEADS])
        sp = sb("sp", [P, 8, DEPTH, 16])
        hb = sb("hb", [P, 2, DEPTH, 16])
        gatew = sb("gatew", [P, 2, 2, P])
        hyb = sb("hyb", [P, CW])
        rs = hyb[:, 0:T]
        pr = sb("pr", [P, 2, LATK])
        pt = sb("pt", [P, 2, LATK])
        smx = sb("smx", [P, 2, 8])
        tmp = sb("tmp", [P, 7, CW])
        gelu_t = tmp[:, 4:6, 0:T]
        a2 = tmp[:, 6, :]
        adap = tmp[:, :, :].rearrange("p i n -> p (i n)")[:, 0:1024].rearrange("p (i n) -> p i n", i=2)
        hlast = sb("hlast", [P, 16])
        hrow = crow[0:16, :]
        rb = sb("rb", [P, NE])
        rw = sb("rw", [P, KT, NE])
        rt = pt[:, :, :].rearrange("p i n -> p (i n)")[:, 0:14 * TT * NE].rearrange("p (i t e) -> p i t e", i=14, t=TT)
        rt4 = sb("rt4", [P, 10, TT * NG])
        rt1 = sb("rt1", [P, 10, TT])
        gates = sb("gates", [P, 2, TT])
        posu = sb("posu", [P, 2, TT], U32)
        nrt = sb("nrt", [P, 4])
        nri = sb("nri", [1, 1 + MORE], I32)
        ids = sb("ids", [P, BLOCKS], U32)
        grf = gr[:, :, :].rearrange("p k t -> p (k t)")
        gaf = ga[:, :, :].rearrange("p k t -> p (k t)")
        gbf = gb[:, :, :].rearrange("p k t -> p (k t)")
        xg = [grf[:, 0:1024], grf[:, 1024:2048]]
        silu_t = grf[:, 2048:2560]
        act = grf[:, 2560:3072]
        xgT = [gaf[:, 0:1024].rearrange("p (k c) -> p k c", k=KT),
               gaf[:, 1024:2048].rearrange("p (k c) -> p k c", k=KT)]
        actT = [gaf[:, 2048 + 512 * i:2560 + 512 * i].rearrange("p (k c) -> p k c", k=4) for i in range(2)]
        yo = [gbf[:, 0:1024], gbf[:, 1024:2048]]
        yg = [grf[:, 0:1024], grf[:, 1024:2048]]
        ysum = gbf[:, 2048:3072]
        zrow = ysum
        vrow = gaf[:, 0:DEPTH * 2 * P].rearrange("p (l i n) -> p l i n", l=DEPTH, i=2)
        kcache = gaf[:, 512:512 + DEPTH * 256].rearrange("p (l n) -> p l n", l=DEPTH)
        hot_c = gbf[:, 0:6 * CAP].rearrange("p (i c) -> p i c", i=6)
        hot_b = gbf[:, 768:768 + 6 * BLOCKS].rearrange("p (i b) -> p i b", i=6)

        banks = [ctx.enter_context(nc.psum_tensor(f"bank{i}", [P, 512], F32)) for i in range(8)]
        G, TB, SB, OB = banks[0:3], banks[3:5], banks[5:7], banks[7]

        h2d = nc.dram_tensor("h2_rows", (T, D), F32, kind="Internal").ap()
        yd = nc.dram_tensor("expert_rows", (BLOCKS * CAP, D), F32, kind="Internal").ap()

        def g_ready(eng, g):
            eng.wait_ge(S("gemm_done"), G_AT[g] + 1)
            return G[G_AT[g] % 3]

        def g_free(g):
            return S(f"gbank_read{G_AT[g] % 3}")

        def g_read(eng, g):
            eng.wait_ge(g_free(g), G_AT[g] // 3 + 1)

        def t_ready(eng, g):
            eng.wait_ge(S("tran_done"), T_AT[g] + 1)
            return TB[T_AT[g] % 2]

        def t_free(g):
            return S(f"tbank_read{T_AT[g] % 2}")

        def t_read(eng, g):
            eng.wait_ge(t_free(g), T_AT[g] // 2 + 1)

        def released(n):
            l, name = CHUNKS[n]
            if name.startswith("gu"):
                e, half = name[2:].split(".")
                return S(("gu_half", "gu_done")[int(half)]), l * NE + int(e) + 1
            if name.startswith("dn"):
                return S("down_done"), l * NE + int(name[2:]) + 1
            if name.startswith("ada"):
                g = (l, "ada", int(name[3:]))
            elif name == "kv":
                g = (l, "vl", 1)
            else:
                g = (l, name[:-1], 4 * int(name[-1]) + 3)
            return S("gemm_done"), G_AT[g] + 1

        gu_w = w_gate_up.rearrange("l e (h k p) n -> l e h p k n", p=P, h=2)
        dn_w = w_down.rearrange("l e (k p) n -> l e p k n", p=P)

        def chunk_src(l, name):
            if name.startswith("gu"):
                e, half = name[2:].split(".")
                return gu_w[l, int(e), int(half)]
            if name.startswith("dn"):
                return dn_w[l, int(name[2:])]
            if name.startswith("ada"):
                c0, w = int(name[3:]) * CHUNK, w_ada
            elif name in W_IN_COL:
                c0, w = W_IN_COL[name], w_in
            else:
                c0, w = int(name[2]) * CHUNK, {"ap": w_attn_proj, "rp": w_rnn_proj, "wo": w_out}[name[0:2]]
            return w[l].rearrange("(k p) n -> p k n", p=P)[:, :, c0:c0 + CHUNK]

        def slot_kn(s):
            return ring[:, s, :].rearrange("p (k n) -> p k n", k=KT)

        def slot_wide(s):
            return ring[:, s, :].rearrange("p (k n) -> p k n", k=4)

        def v_ada(l, j0, j1):
            return vec[:, l, 0, j0:j1]

        def v_conv(l, i, j):
            return vec[:, l, 0, 48 + i * 8 + j:49 + i * 8 + j]

        def v_convb(l, j):
            return vec[:, l, 0, 80 + j:81 + j]

        def v_state(l, d, j):
            return vec[:, l, 1, 48 + d * 8 + j:49 + d * 8 + j]

        STREAM = [slice(0, CTX), slice(CTX, T)]

        block = ctx.enter_context(nc.Block())

        @block.sync
        def _(sy):
            sy.dma_start(con[:, :], consts).then_inc(S("const_loaded"), 16)
            sy.dma_start(crow[0:8, :], c_ctx.rearrange("(k p) -> k p", p=P)).then_inc(S("const_loaded"), 16)
            sy.dma_start(crow[8:16, :], c.rearrange("b (k p) -> (b k) p", p=P)).then_inc(S("const_loaded"), 16)
            sy.dma_start(crow[16:24, :], final_norm_g.rearrange("(k p) -> k p", p=P)).then_inc(S("const_loaded"), 16)
            xs = grf[:, 0:3072].rearrange("p (t n) -> p t n", t=TT)
            for t in range(TT):
                src = x_prompt[0] if t == 0 else x_sample[0, (t - 1) * P:t * P, :]
                sy.dma_start(xs[:, t, :], src).then_inc(S(f"x_loaded{t}"), 16)

            def more_blocks(l):
                sy.wait_ge(S("blocks_known"), l + 1)
                more = sy.value_load(nri[0:1, 0:1], min_val=0, max_val=MORE)
                for b in range(MORE):
                    with sy.If(more > b):
                        e = sy.value_load(nri[0:1, 1 + b:2 + b], min_val=0, max_val=NE - 1)
                        if b == 0:
                            sy.wait_ge(S("experts_done"), l + 1)
                        for half in range(2):
                            sy.dma_start(slot_wide(half), gu_w[l, bass.ds(e, 1), half][0]).then_inc(S(f"x_loaded_w{l}"), 16)
                        sy.dma_start(slot_wide(2), dn_w[l, bass.ds(e, 1)][0]).then_inc(S(f"x_loaded_w{l}"), 16)
                        sy.wait_ge(S(f"x_y_ready{l}"), b + 1)
                        row = (NE + b) * CAP
                        sy.dma_start(yd[row:row + CAP, :], yo[0][0:CAP, :]).then_inc(S(f"x_stored{l}"), 16)
                        sy.wait_ge(S(f"x_stored{l}"), 16 * (b + 1))
                    with sy.Else():
                        sy.nop()
                sy.nop().then_inc(S("blocks_over"), 1)

            for n, (l, name) in enumerate(CHUNKS):
                s = n % SLOTS
                if n >= SLOTS:
                    sy.wait_ge(*released(n - SLOTS))
                dst = slot_wide(s) if name[:2] in ("gu", "dn") else slot_kn(s)
                sy.dma_start(dst, chunk_src(l, name)).then_inc(S(f"w_loaded{s}"), 16)
                if name == f"dn{NE - 1}":
                    more_blocks(l)

        @block.tensor
        def _(pe):
            def g_take(g):
                n = G_AT[g]
                if n >= 3:
                    pe.wait_ge(S(f"gbank_read{n % 3}"), n // 3)
                return G[n % 3]

            def t_take(g):
                n = T_AT[g]
                if n >= 2:
                    pe.wait_ge(S(f"tbank_read{n % 2}"), n // 2)
                return TB[n % 2]

            def weights(l, name):
                n = CHUNK_AT[(l, name)]
                pe.wait_ge(S(f"w_loaded{n % SLOTS}"), 16 * (n // SLOTS + 1))
                return n % SLOTS

            def product(g, slot, n, rhs, width=T):
                bank = g_take(g)
                for k in range(KT):
                    mm = pe.matmul(bank[:, 0:width], slot_kn(slot)[:, k, n * P:(n + 1) * P], rhs(k),
                                   start=(k == 0), stop=(k == KT - 1))
                mm.then_inc(S("gemm_done"), 1)

            def modulation(l, cc):
                s = weights(l, f"ada{cc}")
                bank = g_take((l, "ada", cc))
                for k in range(KT):
                    g = 32 * (k % 4)
                    mm = pe.matmul(bank[g:g + 32, :], cpad[:, k, :], slot_kn(s)[:, k, :],
                                   start=(k < 4), stop=(k >= 4), tile_position=(0, g))
                mm.then_inc(S("gemm_done"), 1)

            def mod_sum(l, cc):
                g_read(pe, (l, "ada", cc))
                bank = t_take((l, "mod", cc))
                for j in range(4):
                    mm = pe.matmul(bank[:, 2 * j:2 * j + 2], adap[:, cc % 2, j * P:(j + 1) * P], sumsel,
                                   start=(j == 0), stop=(j == 3), skip_group_check=True)
                mm.then_inc(S("tran_done"), 1)

            def square_sum(k, cols, count):
                pe.wait_ge(S("sq_ready"), count)
                return pe.matmul(OB[:, cols], ones[:, :], hT[:, k, cols], start=(k == 0), stop=(k == KT - 1),
                                 skip_group_check=True)

            def square_sum_tiles(base, done):
                for t in range(TT):
                    cols = slice(t * P, (t + 1) * P)
                    for k in range(KT):
                        mm = square_sum(k, cols, base + t + 1)
                mm.then_inc(done, 1)

            pe.wait_ge(S("const_loaded"), 64)
            pe.transpose(OB[:, 0:24], crow[:, :], ident[0:24, 0:24]).then_inc(S("cond_tran"), 1)
            xs = grf[:, 0:3072].rearrange("p (t n) -> p t n", t=TT)
            for t in range(TT):
                pe.wait_ge(S(f"x_loaded{t}"), 16)
                for i in range(2):
                    n = t * 2 + i
                    if n >= 2:
                        pe.wait_ge(S("x_taken"), n - 1)
                    for k in range(4):
                        kk = i * 4 + k
                        mm = pe.transpose(SB[i][:, k * P:(k + 1) * P], xs[:, t, kk * P:(kk + 1) * P], ident)
                    mm.then_inc(S("x_tran"), 1)
            pe.wait_ge(S("vec_loaded"), DEPTH * 9 * 16)
            for l in range(DEPTH):
                bank = t_take((l, "vec", 0))
                pe.transpose(bank[:, 0:104], vrow[0:104, l, 0, :], ident[0:104, 0:104])
                pe.transpose(bank[:, 128:192], vrow[0:64, l, 1, :], ident[0:64, 0:64]).then_inc(S("tran_done"), 1)
            pe.wait_ge(S("cache_loaded"), DEPTH * 32)
            for l in range(DEPTH):
                bank = t_take((l, "kc", 0))
                for g in range(KVH):
                    mm = pe.transpose(bank[:, g * P:(g + 1) * P], kcache[:, l, g * P:(g + 1) * P], ident)
                mm.then_inc(S("tran_done"), 1)
            pe.wait_ge(S("cond_ready"), 1)
            for cc in ADA_FIRST:
                modulation(0, cc)
                if cc:
                    mod_sum(0, cc - 1)
            mod_sum(0, ADA_FIRST[-1])
            square_sum_tiles(0, S("ss_done"))

            for l in range(DEPTH):
                sq_base = TT + l * (KT + TT)

                def h_all(k):
                    return hT[:, k, :]

                s = weights(l, "kv")
                pe.wait_ge(S("h_ready_p"), 2 * l * KT + KT)
                pe.wait_ge(S("h_ready_a"), 2 * l * KT + KT)
                for g in range(KVH):
                    product((l, "k", g), s, g, h_all)
                bank = g_take((l, "kvc", 0))
                for k in range(KT):
                    mm = pe.matmul(bank[:, :], hT[:, k, 0:P], slot_kn(s)[:, k, :], start=(k == 0), stop=(k == KT - 1))
                mm.then_inc(S("gemm_done"), 1)
                for t in range(2):
                    bank = g_take((l, "vl", t))
                    for k in range(KT):
                        mm = pe.matmul(bank[:, 0:256], hT[:, k, (t + 1) * P:(t + 2) * P],
                                       slot_kn(s)[:, k, 256:512], start=(k == 0), stop=(k == KT - 1))
                    mm.then_inc(S("gemm_done"), 1)

                def rotated(kind, i):
                    bank = g_take((l, kind, i))
                    src = kT if kind == "krot" else qT
                    g_read(pe, (l, kind[0], i))
                    pe.matmul(bank[:, 0:LAT], rotm, src[:, i, CTX:T], start=True, stop=True).then_inc(S("gemm_done"), 1)

                for h in range(HEADS):
                    if h % 4 == 0:
                        s = weights(l, f"q{h // 4}")
                    product((l, "q", h), s, h % 4, h_all)
                    if h == 4:
                        mod_sum(l, 4)
                    if h < 2:
                        rotated("krot", h)
                    else:
                        rotated("qrot", h - 2)
                    if h % 4 == 3:
                        modulation(l, 4 + h // 4)
                for j in range(KT):
                    if j % 4 == 0:
                        s = weights(l, f"xr{j // 4}")
                    product((l, "xr", j), s, j % 4, h_all)
                    if j < 2:
                        rotated("qrot", 6 + j)
                    if j % 4 == 0:
                        mod_sum(l, 5 + j // 4)
                    if j % 4 == 3:
                        modulation(l, 6 + j // 4)

                def scores(u):
                    h, b = UNITS[u]
                    n = l * len(UNITS) + u
                    g = h // GRP
                    if n >= 2:
                        pe.wait_ge(S("exp_done"), n - 1)
                    if b == 0:
                        pe.matmul(SB[u % 2][:, 0:P], qT[:, h, 0:P], kT[:, g, 0:P], start=True, stop=True)\
                            .then_inc(S("scores_done"), 1)
                        return
                    q = qT[:, h, b * P:(b + 1) * P]
                    pe.matmul(SB[u % 2][:, 0:LAT], q, kT[:, g, CTX:T], start=True, stop=True, skip_group_check=True)
                    pe.matmul(SB[u % 2][:, LAT:LATK], q, kcT[:, l, g, :], start=True, stop=True,
                              skip_group_check=True).then_inc(S("scores_done"), 1)

                def probs_turned(u):
                    h, b = UNITS[u]
                    bank = t_take((l, "pt", u))
                    pe.wait_ge(S("probs_ready"), l * len(UNITS) + u + 1)
                    for i in range(1 if b == 0 else 3):
                        mm = pe.transpose(bank[:, i * P:(i + 1) * P], pr[:, u % 2, i * P:(i + 1) * P], ident)
                    mm.then_inc(S("tran_done"), 1)

                def attend(u):
                    h, b = UNITS[u]
                    g = h // GRP
                    n = l * len(UNITS) + u
                    t_read(pe, (l, "pt", u))
                    if n >= 1:
                        pe.wait_ge(S("att_copied"), n)
                    vals = [kvc[:, 256 + g * P:256 + (g + 1) * P]] if b == 0 else \
                        [vl[:, 0, g * P:(g + 1) * P], vl[:, 1, g * P:(g + 1) * P], vcache[:, l, g * P:(g + 1) * P]]
                    for i, v in enumerate(vals):
                        mm = pe.matmul(OB[:, 0:P], v, pt[:, u % 2, i * P:(i + 1) * P],
                                       start=(i == 0), stop=(i == len(vals) - 1))
                    mm.then_inc(S("att_done"), 1)

                pe.wait_ge(S("rope_done"), (l + 1) * 10)
                for i in range(3 * KT):
                    if i % 4 == 0:
                        s = weights(l, ("gr", "ga", "gb")[i // KT] + str(i % KT // 4))
                    scores(i)
                    product((l, ("gr", "ga", "gb")[i // KT], i % KT), s, i % 4, h_all)
                    if i % 4 == 0 and i <= KT:
                        mod_sum(l, 7 + i // 4)
                    probs_turned(i)
                    if i in (3, 7):
                        modulation(l, 8 + i // 4)
                    if i >= KT:
                        n = i - KT
                        d, j = PAIRS[n]
                        pe.wait_ge(S("xc_ready"), l * KT + j + 1)
                        pe.wait_ge(S(f"gatew_loaded{n % 2}"), (l * 8 + n // 2 + 1) * 64)
                        for which, name in ((0, "gate_a"), (1, "gate_x")):
                            bank = g_take((l, name, n))
                            pe.matmul(bank[:, 0:CW], gatew[:, which, n % 2, :], xc[:, j, :],
                                      start=True, stop=True).then_inc(S("gemm_done"), 1)
                    if i >= 1:
                        attend(i - 1)
                attend(3 * KT - 1)
                pe.wait_ge(S("att_copied"), (l + 1) * len(UNITS))
                for name, src in (("ap", qT), ("rp", gr), ("wo", ga)):
                    for n in range(KT):
                        if n % 4 == 0:
                            s = weights(l, f"{name}{n // 4}")
                        if n == 0 and name == "rp":
                            pe.wait_ge(S("rnn_ready"), (l + 1) * KT)
                        if n == 0 and name == "wo":
                            pe.wait_ge(S("merged_ready"), (l + 1) * KT)
                        product((l, name, n), s, n % 4, lambda k, a=src: a[:, k, :])
                        if n and name == "wo":
                            square_sum(n - 1, slice(0, T), sq_base + n)
                square_sum(KT - 1, slice(0, T), sq_base + KT).then_inc(S("ss_done"), 1)
                pe.wait_ge(S("h_ready_p"), (2 * l + 2) * KT)
                pe.wait_ge(S("h_ready_a"), (2 * l + 2) * KT)
                bank = g_take((l, "logits", 0))
                for t in range(TT):
                    for k in range(KT):
                        mm = pe.matmul(bank[:, t * NE:(t + 1) * NE], hT[:, k, t * P:(t + 1) * P], rw[:, k, :],
                                       start=(k == 0), stop=(k == KT - 1), skip_group_check=True)
                mm.then_inc(S("gemm_done"), 1)
                for t in range(TT):
                    for i in range(2):
                        bank = t_take((l, "h2", t * 2 + i))
                        for k in range(4):
                            mm = pe.transpose(bank[:, k * P:(k + 1) * P], hT[:, i * 4 + k, t * P:(t + 1) * P], ident)
                        mm.then_inc(S("tran_done"), 1)
                bank = t_take((l, "state", 0))
                pe.wait_ge(S("hlast_ready"), (l + 1) * 16)
                pe.transpose(bank[0:16, 0:P], hlast[:, :], ident).then_inc(S("tran_done"), 1)
                late = [(l, c) for c in ADA_LATE] + [(l + 1, c) for c in ADA_FIRST if l + 1 < DEPTH]
                modulation(*late[0])
                modulation(*late[1])
                bank = t_take((l, "rank", 0))
                pe.wait_ge(S("picked"), l + 1)
                for t in range(TT + 1):
                    for i in range(min(t + 1, TT)):
                        lhs = before if i == t else ones[:, :]
                        mm = pe.matmul(bank[:, t * NE:(t + 1) * NE], lhs, rt[:, 8, i, :],
                                       start=(i == 0), stop=(i == min(t, TT - 1)), skip_group_check=True)
                mm.then_inc(S("tran_done"), 1)
                for i in range(len(late)):
                    mod_sum(*late[i])
                    if i + 2 < len(late):
                        modulation(*late[i + 2])
                bank = t_take((l, "ids", 0))
                pe.wait_ge(S("hot_ready"), l + 1)
                for i in range(6):
                    mm = pe.matmul(bank[0:CAP, 0:BLOCKS], hot_c[:, i, :], hot_b[:, i, :], start=(i == 0), stop=(i == 5))
                mm.then_inc(S("tran_done"), 1)

                def turn_rows(e, xrows, x_done, dst_banks):
                    for i in range(2):
                        for k in range(4):
                            kk = i * 4 + k
                            mm = pe.transpose(dst_banks[i][:, k * CAP:(k + 1) * CAP],
                                              xrows[0:CAP, kk * P:(kk + 1) * P], ident[0:CAP, 0:CAP])
                    mm.then_inc(x_done, 1)

                def gate_up(slots, xt, done, half_done):
                    for half in range(2):
                        for n in range(2):
                            for k in range(4):
                                mm = pe.matmul(G[n][0:CAP, :], xt[:, half * 4 + k, 0:CAP],
                                               slot_wide(slots[half])[:, k, n * 512:(n + 1) * 512],
                                               start=(half == 0 and k == 0), stop=(half == 1 and k == 3))
                        if half == 1:
                            mm.then_inc(done, 1)
                        elif half_done is not None:
                            mm.then_inc(half_done, 1)

                def down(slot, at, done):
                    for n in range(2):
                        for k in range(4):
                            mm = pe.matmul(SB[n][0:CAP, :], at[:, k, 0:CAP], slot_wide(slot)[:, k, n * 512:(n + 1) * 512],
                                           start=(k == 0), stop=(k == 3))
                    mm.then_inc(done, 1)

                def xturn(e):
                    n = l * NE + e
                    pe.wait_ge(S(f"row_gathered{e % 2}"), 16 * (l * NE // 2 + e // 2 + 1))
                    if e == 0:
                        for b in range(2):
                            pe.wait_ge(S(f"tbank_read{b}"), len(range(b, T_AT[(l, "comb", 0)], 2)))
                    else:
                        pe.wait_ge(S("xgT_copied"), n)
                    turn_rows(e, xg[e % 2], S("x_turned"), TB)

                def gu(e):
                    n = l * NE + e
                    pe.wait_ge(S("xgT_copied"), n + 1)
                    if e == 0:
                        done = G_AT[(l + 1, "ada", ADA_FIRST[-1])] if l + 1 < DEPTH else len(G_AT) - 1
                        for b in range(2):
                            pe.wait_ge(S(f"gbank_read{b}"), len(range(b, done + 1, 3)))
                    slots = [weights(l, f"gu{e}.{half}") for half in range(2)]
                    gate_up(slots, xgT[e % 2], S("gu_done"), S("gu_half"))

                def dn(e):
                    n = l * NE + e
                    if n >= 1:
                        pe.wait_ge(S("y_copied"), n)
                    pe.wait_ge(S("actT_copied"), n + 1)
                    down(weights(l, f"dn{e}"), actT[e % 2], S("down_done"))

                def aturn(e):
                    n = l * NE + e
                    pe.wait_ge(S("act_ready"), n + 1)
                    for k in range(4):
                        mm = pe.transpose(OB[:, k * CAP:(k + 1) * CAP], act[0:CAP, k * P:(k + 1) * P], ident[0:CAP, 0:CAP])
                    mm.then_inc(S("act_turned"), 1)

                xturn(0)
                for e in range(NE):
                    gu(e)
                    if e + 1 < NE:
                        xturn(e + 1)
                    if e >= 1:
                        dn(e - 1)
                    aturn(e)
                dn(NE - 1)
                pe.wait_ge(S("blocks_known"), l + 1)
                more = pe.value_load(nri[0:1, 0:1], min_val=0, max_val=MORE)
                for b in range(MORE):
                    with pe.If(more > b):
                        pe.wait_ge(S("experts_done"), l + 1)
                        pe.wait_ge(S(f"x_gathered{l}"), 16 * (b + 1))
                        turn_rows(0, xg[0], S(f"x_pe{l}"), TB)
                        pe.wait_ge(S(f"x_act{l}"), b * 4 + 1)
                        pe.wait_ge(S(f"x_loaded_w{l}"), 48 * (b + 1))
                        gate_up([0, 1], xgT[0], S(f"x_pe{l}"), None)
                        pe.wait_ge(S(f"x_dve{l}"), b + 1)
                        for k in range(4):
                            mm = pe.transpose(OB[:, k * CAP:(k + 1) * CAP], act[0:CAP, k * P:(k + 1) * P],
                                              ident[0:CAP, 0:CAP])
                        mm.then_inc(S(f"x_pe{l}"), 1)
                        pe.wait_ge(S(f"x_act{l}"), b * 4 + 3)
                        down(2, actT[0], S(f"x_pe{l}"))
                    with pe.Else():
                        pe.nop()
                for t in range(TT):
                    pe.wait_ge(S("ysum_ready"), l * TT + t + 1)
                    for i in range(2):
                        g = (l, "comb", t * 2 + i)
                        if t == 0:
                            pe.wait_ge(S("xgT_copied"), (l + 1) * NE)
                            bank = TB[T_AT[g] % 2]
                        else:
                            bank = t_take(g)
                        for k in range(4):
                            kk = i * 4 + k
                            mm = pe.transpose(bank[:, k * P:(k + 1) * P], ysum[:, kk * P:(kk + 1) * P], ident)
                        mm.then_inc(S("tran_done"), 1)
                square_sum_tiles(sq_base + KT, S("ss_done"))
            pe.wait_ge(S("final_h"), KT)
            for t in range(TT):
                for i in range(2):
                    n = t * 2 + i
                    if n >= 2:
                        pe.wait_ge(S("y_out_copied"), n - 1)
                    for k in range(4):
                        mm = pe.transpose(SB[i][:, k * P:(k + 1) * P], hT[:, i * 4 + k, t * P:(t + 1) * P], ident)
                    mm.then_inc(S("y_out_turned"), 1)

        @block.scalar
        def _(ac):
            chain = [0]

            def link(ins):
                chain[0] += 1
                ins.then_inc(S("act_chain"), 1)
                ac.wait_ge(S("act_chain"), chain[0])

            def small_loads(l):
                rows = [(0, 0, 48, b_ada[l].rearrange("(k p) -> k p", p=P)),
                        (0, 48, 32, conv_w[l].rearrange("i (k p) -> (i k) p", p=P)),
                        (0, 80, 8, conv_b[l].rearrange("(k p) -> k p", p=P)),
                        (0, 88, 8, norm1_g[l].rearrange("(k p) -> k p", p=P)),
                        (0, 96, 8, norm2_g[l].rearrange("(k p) -> k p", p=P)),
                        (1, 0, 16, lru_ba[l].rearrange("d (k p) -> (d k) p", p=P)),
                        (1, 16, 16, lru_bx[l].rearrange("d (k p) -> (d k) p", p=P)),
                        (1, 32, 16, lru_lambda[l].rearrange("d (k p) -> (d k) p", p=P)),
                        (1, 48, 16, state_h[0, l].rearrange("d (k p) -> (d k) p", p=P))]
                for which, r0, n, src in rows:
                    ac.dma_start(vrow[r0:r0 + n, l, which, :], src).then_inc(S("vec_loaded"), 16)
                ac.dma_start(kcache[:, l, :], cache_k[0, l].rearrange("t g d -> t (g d)")).then_inc(S("cache_loaded"), 16)
                ac.dma_start(vcache[:, l, :], cache_v[0, l].rearrange("t g d -> t (g d)")).then_inc(S("cache_loaded"), 16)

            for l in range(DEPTH):
                small_loads(l)
            ac.dma_start(rb[:, :], router_b.rearrange("(a n) -> a n", a=1).broadcast_to([P, NE])).then_inc(S("router_loaded"), 16)
            ac.dma_start(rw[:, :, :], router_w.rearrange("(k p) n -> p k n", p=P)).then_inc(S("router_loaded"), 16)
            ac.dma_start(sinkb[:, :, :].rearrange("p l h -> p (l h)"),
                         attn_sink.rearrange("(a l) h -> a (l h)", a=1).broadcast_to([P, DEPTH * HEADS])).then_inc(S("router_loaded"), 16)
            ac.wait_ge(S("cond_tran"), 1)
            ac.activation(cvec[:, :], OB[:, 0:24], ACT.Copy).then_inc(S("cvec_ready"), 1)
            ac.activation(tmp[:, 6, 0:16], OB[:, 0:16], ACT.Tanh, scale=0.5).then_inc(S("cond_tanh"), 1)
            ac.wait_ge(S("lam_abs"), 1)
            ac.activation(sp[:, 1, :, :], sp[:, 0, :, :], ACT.Exp, scale=-1.0).then_inc(S("lam_exp"), 1)

            def ada_copy(l, cc):
                bank = g_ready(ac, (l, "ada", cc))
                n = l * 12 + cc
                if n >= 2:
                    m = n - 2
                    ac.wait_ge(S("tran_done"), T_AT[(m // 12, "mod", m % 12)] + 1)
                ac.activation(adap[:, cc % 2, :], bank[:, :], ACT.Copy).then_inc(g_free((l, "ada", cc)), 1)

            for cc in ADA_FIRST:
                ada_copy(0, cc)

            def rms(n):
                ac.wait_ge(S("ss_done"), n + 1)
                ac.activation(rs, OB[:, 0:T], ACT.Sqrt, bias=EPS, scale=1.0 / D).then_inc(S("rms_ready"), 1)

            for l in range(DEPTH):

                def modulated(which):
                    rms(2 * l + which)
                    base = (2 * l + which) * KT
                    for k in range(KT):
                        ac.wait_ge(S("xn_ready"), base + k + 1)
                        ac.activation(hT[:, k, CTX:T], hT[:, k, CTX:T], ACT.Identity,
                                      bias=modT[:, which * 24 + k, 1:2], scale=modA[:, which, k, 1:2])\
                            .then_inc(S("h_ready_a"), 1)

                modulated(0)

                def copy_out(g, dst, width):
                    bank = g_ready(ac, g)
                    ac.activation(dst, bank[:, 0:width], ACT.Copy).then_inc(g_free(g), 1)

                for g in range(KVH):
                    copy_out((l, "k", g), kT[:, g, :], T)
                if l:
                    ac.wait_ge(S("cache_stored"), l * 32)
                copy_out((l, "kvc", 0), kvc[:, :], 512)
                for t in range(2):
                    copy_out((l, "vl", t), vl[:, t, :], 256)
                for h in range(HEADS):
                    copy_out((l, "q", h), qT[:, h, :], T)
                    if h == 0:
                        g_read(ac, (l, "kvc", 0))
                        ac.dma_start(new_k[0, l].rearrange("t g d -> t (g d)"), kvc[:, 0:256]).then_inc(S("cache_stored"), 16)
                        ac.dma_start(new_v[0, l].rearrange("t g d -> t (g d)"), kvc[:, 256:512]).then_inc(S("cache_stored"), 16)
                    if h % 4 == 3:
                        ada_copy(l, 4 + h // 4)
                for j in range(KT):
                    bank = g_ready(ac, (l, "xr", j))
                    n = l * KT + j
                    if n >= 1:
                        ac.wait_ge(S("xc_ready"), n)
                    else:
                        ac.wait_ge(S("zeroed"), 1)
                    ac.activation(xp[:, 2:2 + CTX], bank[:, 0:CTX], ACT.Copy)
                    ac.activation(xp[:, 2 + LAT0:2 + CW], bank[:, CTX:T], ACT.Copy).then_inc(g_free((l, "xr", j)), 1)
                    if j % 4 == 3:
                        ada_copy(l, 6 + j // 4)

                def exps(u):
                    h, b = UNITS[u]
                    n = l * len(UNITS) + u
                    w = P if b == 0 else LATK
                    ac.wait_ge(S("max_ready"), n + 1)
                    if n >= 2:
                        m = n - 2
                        ac.wait_ge(S("tran_done"), T_AT[(m // 24, "pt", m % 24)] + 1)
                    ac.activation(pr[:, u % 2, 0:w], SB[u % 2][:, 0:w], ACT.Exp, bias=smx[:, u % 2, 1:2],
                                  scale=SCALE, accum_out=smx[:, u % 2, 2:3])
                    ac.activation(smx[:, u % 2, 3:4], sinkb[:, l, h:h + 1], ACT.Exp, bias=smx[:, u % 2, 1:2])\
                        .then_inc(S("exp_done"), 1)

                def pt_copy(u):
                    h, b = UNITS[u]
                    n = l * len(UNITS) + u
                    w = P if b == 0 else LATK
                    bank = t_ready(ac, (l, "pt", u))
                    if n >= 2:
                        ac.wait_ge(S("att_done"), n - 1)
                    ac.activation(pt[:, u % 2, 0:w], bank[:, 0:w], ACT.Copy).then_inc(t_free((l, "pt", u)), 1)

                def att_copy(u):
                    h, b = UNITS[u]
                    ac.wait_ge(S("att_done"), l * len(UNITS) + u + 1)
                    ac.activation(qT[:, h, b * P:(b + 1) * P], OB[:, 0:P], ACT.Copy).then_inc(S("att_copied"), 1)

                def lru_tables(n):
                    d, j = PAIRS[n]
                    m = l * 16 + n
                    if m >= 2:
                        ac.wait_ge(S("lru_used"), m - 1)
                    if n < 2:
                        ac.wait_ge(S("gelu_done"), (l + 1) * KT)
                    a, th, ti = tmp[:, n % 2, :], tmp[:, 2 + n % 2, :], tmp[:, 4 + n % 2, :]
                    bank = g_ready(ac, (l, "gate_a", n))
                    cb = d * 8 + j
                    c_log = [sp[:, i, l, cb:cb + 1] for i in (6, 7)]
                    ac.activation(a, bank[:, 0:CW], ACT.Tanh, bias=hb[:, 0, l, cb:cb + 1], scale=0.5)\
                        .then_inc(g_free((l, "gate_a", n)), 1)
                    bank = g_ready(ac, (l, "gate_x", n))
                    ac.activation(ti, bank[:, 0:CW], ACT.Tanh, bias=hb[:, 1, l, cb:cb + 1], scale=0.5)\
                        .then_inc(g_free((l, "gate_x", n)), 1)
                    g_read(ac, (l, "gate_a", n))
                    ac.activation(th, a, ACT.Tanh, bias=c_log[1], scale=c_log[1])
                    link(ac.activation(a, a, ACT.Exp, bias=c_log[0], scale=c_log[0]))
                    if m:
                        ac.wait_ge(S("lru_square"), m)
                    ac.activation(a2, a, ACT.Square).then_inc(S("lru_act"), 1)

                def lru_root(n):
                    ac.wait_ge(S("lru_square"), l * 16 + n + 1)
                    th = tmp[:, 2 + n % 2, :]
                    ac.activation(th, th, ACT.Sqrt, scale=0.25).then_inc(S("root_ready"), 1)

                def gelu_tanh(j):
                    ac.wait_ge(S("gelu_arg"), l * KT + j + 1)
                    ac.activation(gelu_t[:, j % 2, :], gelu_t[:, j % 2, :], ACT.Tanh, scale=GELU_C)\
                        .then_inc(S("gelu_tanh"), 1)

                for i in range(3 * KT):
                    kind = ("gr", "ga", "gb")[i // KT]
                    j = i % KT
                    exps(i)
                    if 1 <= i <= KT:
                        gelu_tanh(i - 1)
                    if i > KT:
                        lru_root(i - KT - 1)
                    if kind == "gr":
                        copy_out((l, kind, j), gr[:, j, :], T)
                        g_read(ac, (l, kind, j))
                        if l * KT + j >= 2:
                            ac.wait_ge(S("gelu_done"), l * KT + j - 1)
                        if l and j == 0:
                            ac.wait_ge(S("lru_used"), l * 16)
                        ac.activation(gelu_t[:, j % 2, :], gr[:, j, :], ACT.Square).then_inc(S("gelu_sq"), 1)
                    else:
                        dst = ga if kind == "ga" else gb
                        if kind == "gb" and l == 0 and j == 0:
                            ac.wait_ge(S("rows_zero"), 16 * MORE)
                        g = (l, kind, j)
                        bank = g_ready(ac, g)
                        ac.activation(dst[:, j, :], bank[:, 0:T], ACT.Tanh, scale=0.5).then_inc(g_free(g), 1)
                    pt_copy(i)
                    if i in (3, 7):
                        ada_copy(l, 8 + i // 4)
                    if i >= KT:
                        lru_tables(i - KT)
                    if i >= 1:
                        att_copy(i - 1)
                lru_root(15)
                att_copy(23)
                modulated(1)
                bank = g_ready(ac, (l, "logits", 0))
                ac.activation(rt[:, 0, :, :].rearrange("p t e -> p (t e)"), bank[:, 0:TT * NE], ACT.Exp, scale=-1.0)\
                    .then_inc(g_free((l, "logits", 0)), 1)
                for t in range(TT):
                    for i in range(2):
                        g = (l, "h2", t * 2 + i)
                        bank = t_ready(ac, g)
                        ac.activation(grf[:, t * 1024 + i * 512:t * 1024 + (i + 1) * 512], bank[:, :], ACT.Copy)\
                            .then_inc(t_free(g), 1)
                    for i in range(2):
                        t_read(ac, (l, "h2", t * 2 + i))
                    ac.dma_start(h2d[t * P:(t + 1) * P, :], grf[:, t * 1024:(t + 1) * 1024]).then_inc(S("h2_stored"), 16)
                bank = t_ready(ac, (l, "state", 0))
                if l:
                    ac.wait_ge(S("state_stored"), 16 * l)
                ac.activation(hrow[:, :], bank[0:16, 0:P], ACT.Copy).then_inc(t_free((l, "state", 0)), 1)
                for c in ADA_LATE:
                    ada_copy(l, c)
                if l + 1 < DEPTH:
                    for c in ADA_FIRST:
                        ada_copy(l + 1, c)
                t_read(ac, (l, "state", 0))
                ac.dma_start(new_h[0, l].rearrange("d (k p) -> (d k) p", p=P), hrow[:, :]).then_inc(S("state_stored"), 16)

                def copy_x(e):
                    n = l * NE + e
                    ac.wait_ge(S("x_turned"), n + 1)
                    if n >= 2:
                        ac.wait_ge(S("gu_done"), n - 1)
                    for i in range(2):
                        ins = ac.activation(xgT[e % 2][:, i * 4:(i + 1) * 4, 0:CAP],
                                            TB[i][:, 0:4 * CAP].rearrange("p (k c) -> p k c", k=4), ACT.Copy)
                    ins.then_inc(S("xgT_copied"), 1)

                def tanh_g(e):
                    n = l * NE + e
                    ac.wait_ge(S("gu_done"), n + 1)
                    if n:
                        ac.wait_ge(S("act_ready"), n)
                    ac.activation(silu_t[0:CAP, :], G[0][0:CAP, :], ACT.Tanh, scale=0.5).then_inc(S("silu_tanh"), 1)

                def copy_act(e):
                    n = l * NE + e
                    ac.wait_ge(S("act_turned"), n + 1)
                    if n >= 2:
                        ac.wait_ge(S("down_done"), n - 1)
                    ac.activation(actT[e % 2][:, :, 0:CAP], OB[:, 0:4 * CAP].rearrange("p (k c) -> p k c", k=4),
                                  ACT.Copy).then_inc(S("actT_copied"), 1)

                def copy_y(e):
                    n = l * NE + e
                    ac.wait_ge(S("down_done"), n + 1)
                    if n >= 2:
                        ac.wait_ge(S(f"y_stored{e % 2}"), 16 * (n // 2))
                    for i in range(2):
                        ins = ac.activation(yo[e % 2][0:CAP, i * 512:(i + 1) * 512], SB[i][0:CAP, :], ACT.Copy)
                    ins.then_inc(S("y_copied"), 1)
                    ac.wait_ge(S("y_copied"), n + 1)
                    ac.dma_start(yd[e * CAP:(e + 1) * CAP, :], yo[e % 2][0:CAP, :]).then_inc(S(f"y_stored{e % 2}"), 16)

                copy_x(0)
                for e in range(NE):
                    tanh_g(e)
                    if e + 1 < NE:
                        copy_x(e + 1)
                    if e >= 1:
                        copy_y(e - 1)
                    copy_act(e)
                copy_y(NE - 1)
                for b in range(2):
                    ac.wait_ge(S(f"y_stored{b}"), 16 * (l + 1) * NE // 2)
                ac.nop().then_inc(S("experts_done"), 1)
                ac.wait_ge(S("blocks_known"), l + 1)
                more = ac.value_load(nri[0:1, 0:1], min_val=0, max_val=MORE)
                for b in range(MORE):
                    with ac.If(more > b):
                        ac.wait_ge(S(f"x_pe{l}"), b * 4 + 1)
                        for i in range(2):
                            ins = ac.activation(xgT[0][:, i * 4:(i + 1) * 4, 0:CAP],
                                                TB[i][:, 0:4 * CAP].rearrange("p (k c) -> p k c", k=4), ACT.Copy)
                        ins.then_inc(S(f"x_act{l}"), 1)
                        ac.wait_ge(S(f"x_pe{l}"), b * 4 + 2)
                        ac.activation(silu_t[0:CAP, :], G[0][0:CAP, :], ACT.Tanh, scale=0.5).then_inc(S(f"x_act{l}"), 1)
                        ac.wait_ge(S(f"x_pe{l}"), b * 4 + 3)
                        ac.activation(actT[0][:, :, 0:CAP], OB[:, 0:4 * CAP].rearrange("p (k c) -> p k c", k=4),
                                      ACT.Copy).then_inc(S(f"x_act{l}"), 1)
                        ac.wait_ge(S(f"x_pe{l}"), b * 4 + 4)
                        if b:
                            ac.wait_ge(S(f"x_stored{l}"), 16 * b)
                        ac.activation(yo[0][0:CAP, 0:512], SB[0][0:CAP, :], ACT.Copy).then_inc(S(f"x_act{l}"), 1)
                        ac.activation(yo[0][0:CAP, 512:1024], SB[1][0:CAP, :], ACT.Copy).then_inc(S(f"x_y_ready{l}"), 1)
                    with ac.Else():
                        ac.nop()
            rms(2 * DEPTH)
            for t in range(TT):
                for i in range(2):
                    n = t * 2 + i
                    ac.wait_ge(S("y_out_turned"), n + 1)
                    ac.activation(grf[:, n * 512:(n + 1) * 512], SB[i][:, :], ACT.Copy).then_inc(S("y_out_copied"), 1)
                ac.wait_ge(S("y_out_copied"), 2 * t + 2)
                dst = y_prompt[0] if t == 0 else y_sample[0, (t - 1) * P:t * P, :]
                ac.dma_start(dst, grf[:, t * 1024:(t + 1) * 1024]).then_inc(S("y_out_stored"), 16)
            ac.wait_ge(S("y_out_stored"), TT * 16)
            ac.wait_ge(S("cache_stored"), DEPTH * 32)
            ac.wait_ge(S("state_stored"), DEPTH * 16)

        @block.vector
        def _(ve):
            chain = [0]

            def link(ins):
                chain[0] += 1
                ins.then_inc(S("dve_chain"), 1)
                ve.wait_ge(S("dve_chain"), chain[0])
                return ins

            ve.memset(ones[:, :], 1.0)
            ve.memset(cpad[:, :, :], 0.0)
            ve.memset(zrow, 0.0)
            link(ve.memset(xp[:, :], 0.0))
            ve.nop().then_inc(S("zeroed"), 1)
            ve.wait_ge(S("cvec_ready"), 1)
            ve.wait_ge(S("cond_tanh"), 1)
            link(ve.tensor_scalar(tmp[:, 6, 16:32], tmp[:, 6, 0:16], 0.5, 0.5, ALU.mult, ALU.add))
            ve.tensor_tensor(cpad[:, :, 0], tmp[:, 6, 16:24], cvec[:, 0:8], ALU.mult)
            ve.tensor_tensor(cpad[:, :, 1], tmp[:, 6, 24:32], cvec[:, 8:16], ALU.mult).then_inc(S("cond_ready"), 1)

            def squares_of_tile(t):
                cols = slice(t * P, (t + 1) * P)
                ve.tensor_tensor(hT[:, :, cols], xT[:, :, cols], xT[:, :, cols], ALU.mult).then_inc(S("sq_ready"), 1)

            for t in range(TT):
                for i in range(2):
                    ve.wait_ge(S("x_tran"), t * 2 + i + 1)
                    ve.tensor_copy(xT[:, i * 4:i * 4 + 4, t * P:(t + 1) * P],
                                   SB[i][:, :].rearrange("p (k c) -> p k c", k=4)).then_inc(S("x_taken"), 1)
                ve.wait_ge(S("x_taken"), 2 * t + 2)
                squares_of_tile(t)
            for l in range(DEPTH):
                bank = t_ready(ve, (l, "vec", 0))
                ve.tensor_copy(vec[:, l, 0, 0:104], bank[:, 0:104])
                ve.tensor_copy(vec[:, l, 1, 0:64], bank[:, 128:192]).then_inc(t_free((l, "vec", 0)), 1)
            for l in range(DEPTH):
                bank = t_ready(ve, (l, "kc", 0))
                ve.tensor_copy(kcT[:, l, :, :], bank[:, 0:256].rearrange("p (g t) -> p g t", g=2))\
                    .then_inc(t_free((l, "kc", 0)), 1)
            for l in range(DEPTH):
                t_read(ve, (l, "vec", 0))
            v_lam = vec[:, :, 1, 32:48]
            sp_ = lambda i: sp[:, i, :, :]
            ve.tensor_scalar(sp_(3), v_lam, -1.0, 0.0, ALU.mult, ALU.max)
            link(ve.tensor_scalar(sp_(2), v_lam, -1.0, None, ALU.mult))
            ve.tensor_tensor(sp_(0), sp_(2), v_lam, ALU.max).then_inc(S("lam_abs"), 1)

            def softplus():
                ve.wait_ge(S("lam_exp"), 1)
                link(ve.tensor_scalar(sp_(2), sp_(1), 2.0, None, ALU.add))
                link(ve.reciprocal(sp_(4), sp_(2)))
                link(ve.tensor_tensor(sp_(4), sp_(4), sp_(1), ALU.mult))
                link(ve.tensor_tensor(sp_(5), sp_(4), sp_(4), ALU.mult))
                link(ve.tensor_scalar(sp_(2), sp_(5), 1.0 / 19, 1.0 / 17, ALU.mult, ALU.add))
                for m in range(15, 0, -2):
                    link(ve.tensor_tensor(sp_(2), sp_(2), sp_(5), ALU.mult))
                    link(ve.tensor_scalar(sp_(2), sp_(2), 1.0 / m, None, ALU.add))
                link(ve.tensor_tensor(sp_(2), sp_(2), sp_(4), ALU.mult))
                link(ve.scalar_tensor_tensor(sp_(2), sp_(2), 2.0, sp_(3), ALU.mult, ALU.add))
                ve.tensor_scalar(sp_(6), sp_(2), -4.0, None, ALU.mult)
                ve.tensor_scalar(sp_(7), sp_(2), 4.0, None, ALU.mult)
                ve.tensor_scalar(hb[:, 0, :, :], vec[:, :, 1, 0:16], 0.5, None, ALU.mult)
                ve.tensor_scalar(hb[:, 1, :, :], vec[:, :, 1, 16:32], 0.5, None, ALU.mult)
                ve.wait_ge(S("router_loaded"), 48)
                link(ve.tensor_scalar(nsink[:, :, :], sinkb[:, :, :], -1.0, None, ALU.mult))

            def mod_add(l, cc):
                bank = t_ready(ve, (l, "mod", cc))
                b = v_ada(l, cc * 4, cc * 4 + 4)
                pair = bank[:, 0:8].rearrange("p (j s) -> p j s", s=2)
                ve.tensor_tensor(modT[:, cc * 4:cc * 4 + 4, 0], pair[:, :, 0], b, ALU.add)
                ve.tensor_tensor(modT[:, cc * 4:cc * 4 + 4, 1], pair[:, :, 1], b, ALU.add)\
                    .then_inc(t_free((l, "mod", cc)), 1)
                kk = 4 * (cc % 2)
                m = modT[:, cc * 4:cc * 4 + 4, :]
                if cc // 2 in (1, 4):
                    t_read(ve, (l, "mod", cc))
                    g0 = 88 if cc // 2 == 1 else 96
                    g = vec[:, l, 0, g0 + kk:g0 + kk + 4]
                    for st in range(2):
                        link(ve.scalar_tensor_tensor(modA[:, cc // 8, kk:kk + 4, st], m[:, :, st], 1.0, g, ALU.add, ALU.mult))
                elif cc // 2 == 2:
                    t_read(ve, (l, "mod", cc))
                    link(ve.tensor_scalar(modA[:, 2, kk:kk + 4, :], m, 0.5, None, ALU.mult))
                elif cc // 2 == 5:
                    t_read(ve, (l, "mod", cc))
                    link(ve.tensor_copy(modA[:, 3, kk:kk + 4, :], m))

            for cc in ADA_FIRST:
                mod_add(0, cc)

            norms = [0]

            def rstd():
                norms[0] += 1
                ve.wait_ge(S("rms_ready"), norms[0])
                link(ve.reciprocal(rs, rs))

            for l in range(DEPTH):

                def normed():
                    rstd()
                    for k in range(KT):
                        ve.tensor_tensor(hT[:, k, :], xT[:, k, :], rs, ALU.mult).then_inc(S("xn_ready"), 1)

                normed()
                if l == 0:
                    softplus()

                def rope(kind, i):
                    bank = g_ready(ve, (l, kind, i))
                    x = (kT if kind == "krot" else qT)[:, i, CTX:T]
                    turned = tmp[:, 6, 0:LAT]
                    ve.tensor_tensor(turned, bank[:, 0:LAT], sinT, ALU.mult).then_inc(g_free((l, kind, i)), 1)
                    link(ve.tensor_tensor(x, x, cosT, ALU.mult))
                    g_read(ve, (l, kind, i))
                    link(ve.tensor_tensor(x, x, turned, ALU.add))
                    ve.nop().then_inc(S("rope_done"), 1)

                def conv(j):
                    g_read(ve, (l, "xr", j))
                    x = xp[:, :]
                    link(ve.tensor_scalar(xc[:, j, :], x[:, 0:CW], v_conv(l, 0, j), v_convb(l, j), ALU.mult, ALU.add))
                    for i in range(1, 4):
                        ins = ve.scalar_tensor_tensor(xc[:, j, :], x[:, i:i + CW], v_conv(l, i, j), xc[:, j, :], ALU.mult, ALU.add)
                        if i < 3:
                            link(ins)
                    ins.then_inc(S("xc_ready"), 1)

                for i in range(2):
                    rope("krot", i)
                for i in range(6):
                    rope("qrot", i)
                    if i == 2:
                        mod_add(l, 4)
                conv(0)
                rope("qrot", 6)
                mod_add(l, 5)
                conv(1)
                rope("qrot", 7)
                for j in range(2, KT):
                    conv(j)
                    if j == 4:
                        mod_add(l, 6)

                def softmax_max(u):
                    h, b = UNITS[u]
                    n = l * len(UNITS) + u
                    w = P if b == 0 else LATK
                    ve.wait_ge(S("scores_done"), n + 1)
                    if b:
                        cols = slice(P, LAT) if b == 1 else slice(0, P)
                        link(ve.tensor_tensor(SB[u % 2][:, cols], SB[u % 2][:, cols], mask[b - 1], ALU.add))
                    link(ve.tensor_reduce(smx[:, u % 2, 0:1], SB[u % 2][:, 0:w], AX.X, ALU.max))
                    ve.tensor_scalar(smx[:, u % 2, 1:2], smx[:, u % 2, 0:1], -SCALE, nsink[:, l, h:h + 1], ALU.mult, ALU.min)\
                        .then_inc(S("max_ready"), 1)

                def softmax_norm(u):
                    h, b = UNITS[u]
                    w = P if b == 0 else LATK
                    ve.wait_ge(S("exp_done"), l * len(UNITS) + u + 1)
                    link(ve.tensor_tensor(smx[:, u % 2, 4:5], smx[:, u % 2, 2:3], smx[:, u % 2, 3:4], ALU.add))
                    link(ve.reciprocal(smx[:, u % 2, 5:6], smx[:, u % 2, 4:5]))
                    ve.tensor_scalar(pr[:, u % 2, 0:w], pr[:, u % 2, 0:w], smx[:, u % 2, 5:6], None, ALU.mult)\
                        .then_inc(S("probs_ready"), 1)

                def one_minus_square(n):
                    ve.wait_ge(S("lru_act"), l * 16 + n + 1)
                    th = tmp[:, 2 + n % 2, :]
                    ve.scalar_tensor_tensor(th, a2, 1.0, th, ALU.add, ALU.mult).then_inc(S("lru_square"), 1)

                def scan(n):
                    d, j = PAIRS[n]
                    m = l * 16 + n
                    a, th, ti = tmp[:, n % 2, :], tmp[:, 2 + n % 2, :], tmp[:, 4 + n % 2, :]
                    link(ve.scalar_tensor_tensor(ti, ti, 1.0, xc[:, j, :], ALU.add, ALU.mult))
                    ve.wait_ge(S("root_ready"), m + 1)
                    link(ve.tensor_tensor(th, th, ti, ALU.mult))
                    dst = hyb[:, :] if d == 0 else ti
                    for st in range(2):
                        cs = slice(0, CTX) if st == 0 else slice(LAT0, CW)
                        init = 0.0 if st == 0 else v_state(l, d, j)
                        aa, ww, oo = a[:, cs], th[:, cs], dst[:, cs]
                        if d == 1:
                            aa, ww, oo = aa[:, ::-1], ww[:, ::-1], oo[:, ::-1]
                        ins = ve.tensor_tensor_scan(oo, aa, ww, init, ALU.mult, ALU.add)
                    link(ins)
                    last = dst[:, CTX - 1:CTX] if d == 0 else dst[:, 0:1]
                    if l and n == 0:
                        ve.wait_ge(S("tran_done"), T_AT[(l - 1, "state", 0)] + 1)
                    ve.tensor_copy(hlast[:, d * 8 + j:d * 8 + j + 1], last).then_inc(S("hlast_ready"), 1)
                    if d == 1:
                        for st in range(2):
                            cs = slice(0, CTX) if st == 0 else slice(LAT0, CW)
                            ins = ve.tensor_tensor(th[:, cs], hyb[:, cs], ti[:, cs], ALU.add)
                        link(ins)
                        for st in range(2):
                            cs = slice(0, CTX) if st == 0 else slice(LAT0, CW)
                            ins = ve.scalar_tensor_tensor(gr[:, j, STREAM[st]], gr[:, j, STREAM[st]], 0.5, th[:, cs],
                                                          ALU.mult, ALU.mult)
                        link(ins)
                        ve.nop().then_inc(S("rnn_ready"), 1)
                    ve.wait_ge(S("hlast_ready"), m + 1)
                    ve.nop().then_inc(S("lru_used"), 1)

                def gelu_arg(j):
                    ve.wait_ge(S("gelu_sq"), l * KT + j + 1)
                    x = gelu_t[:, j % 2, :]
                    link(ve.tensor_scalar(x, x, 0.044715, 1.0, ALU.mult, ALU.add))
                    ve.tensor_tensor(x, x, gr[:, j, :], ALU.mult).then_inc(S("gelu_arg"), 1)

                def gelu_end(j):
                    ve.wait_ge(S("gelu_tanh"), l * KT + j + 1)
                    ve.scalar_tensor_tensor(gr[:, j, :], gelu_t[:, j % 2, :], 1.0, gr[:, j, :], ALU.add, ALU.mult)\
                        .then_inc(S("gelu_done"), 1)

                for i in range(3 * KT):
                    softmax_max(i)
                    softmax_norm(i)
                    if 1 <= i <= KT:
                        gelu_end(i - 1)
                    if i % 4 == 0 and i <= KT:
                        mod_add(l, 7 + i // 4)
                    if i < KT:
                        gelu_arg(i)
                    if i > KT:
                        one_minus_square(i - KT - 1)
                        scan(i - KT - 1)
                one_minus_square(15)
                scan(15)

                for n in range(KT):
                    bank = g_ready(ve, (l, "ap", n))
                    g_read(ve, (l, "ga", n))
                    ve.scalar_tensor_tensor(ga[:, n, :], ga[:, n, :], 1.0, bank[:, 0:T], ALU.add, ALU.mult)\
                        .then_inc(g_free((l, "ap", n)), 1)
                for n in range(KT):
                    bank = g_ready(ve, (l, "rp", n))
                    g_read(ve, (l, "gb", n))
                    ve.scalar_tensor_tensor(gb[:, n, :], gb[:, n, :], 1.0, bank[:, 0:T], ALU.add, ALU.mult)\
                        .then_inc(g_free((l, "rp", n)), 1)
                    g_read(ve, (l, "rp", n))
                    ve.tensor_tensor(ga[:, n, :], ga[:, n, :], gb[:, n, :], ALU.add).then_inc(S("merged_ready"), 1)
                for n in range(KT):
                    bank = g_ready(ve, (l, "wo", n))
                    for st in range(2):
                        ins = ve.scalar_tensor_tensor(xT[:, n, STREAM[st]], bank[:, STREAM[st]], modA[:, 2, n, st:st + 1],
                                                      xT[:, n, STREAM[st]], ALU.mult, ALU.add)
                    ins.then_inc(g_free((l, "wo", n)), 1)
                    g_read(ve, (l, "wo", n))
                    ve.tensor_tensor(hT[:, n, :], xT[:, n, :], xT[:, n, :], ALU.mult).then_inc(S("sq_ready"), 1)
                normed()

                g_read(ve, (l, "logits", 0))
                R = lambda i: rt[:, i, :, :]
                bc_e = lambda v: v.rearrange("p (a e) -> p a e", a=1).broadcast_to([P, TT, NE])
                link(ve.tensor_scalar(R(0), R(0), 1.0, None, ALU.add))
                link(ve.reciprocal(R(1), R(0)))
                link(ve.tensor_tensor(R(2), R(1), bc_e(rb[:, :]), ALU.add))
                quad = rt[:, 2, :, :].rearrange("p t (g i) -> p (t g) i", i=EG)
                q4 = lambda i: rt4[:, i, :]
                mx, mn = ALU.max, ALU.min
                link(ve.tensor_tensor(q4(0), quad[:, :, 0], quad[:, :, 1], mx))
                link(ve.tensor_tensor(q4(1), quad[:, :, 0], quad[:, :, 1], mn))
                link(ve.tensor_tensor(q4(2), quad[:, :, 2], quad[:, :, 3], mx))
                link(ve.tensor_tensor(q4(3), quad[:, :, 2], quad[:, :, 3], mn))
                link(ve.tensor_tensor(q4(4), q4(0), q4(2), mx))
                link(ve.tensor_tensor(q4(5), q4(0), q4(2), mn))
                link(ve.tensor_tensor(q4(6), q4(1), q4(3), mx))
                link(ve.tensor_tensor(q4(6), q4(5), q4(6), mx))
                link(ve.tensor_tensor(q4(4), q4(4), q4(6), ALU.add))
                g3 = lambda i: rt4[:, i, :].rearrange("p (t g) -> p t g", g=NG)
                r1 = lambda i: rt1[:, i, :]
                bc1 = lambda v, w: v.rearrange("p (t a) -> p t a", a=1).broadcast_to([P, TT, w])
                bg = iota_g.rearrange("p (a g) -> p a g", a=1).broadcast_to([P, TT, NG])
                link(ve.tensor_reduce(r1(0), g3(4), AX.X, mx))
                link(ve.tensor_tensor(g3(5), g3(4), bc1(r1(0), NG), ALU.is_equal))
                link(ve.tensor_tensor(g3(5), g3(5), bg, ALU.mult))
                link(ve.tensor_reduce(r1(1), g3(5), AX.X, mx))
                link(ve.tensor_tensor(g3(6), g3(5), bc1(r1(1), NG), ALU.is_equal))
                in_grp = rt4[:, 6, :].rearrange("p (g a) -> p g a", a=1).broadcast_to([P, TT * NG, EG])
                r3 = lambda i: rt[:, i, :, :].rearrange("p t (g i) -> p (t g) i", i=EG)
                link(ve.tensor_tensor(r3(3), r3(2), in_grp, ALU.mult))
                link(ve.tensor_scalar(q4(7), q4(6), BIG, -BIG, ALU.mult, ALU.add))
                off = rt4[:, 7, :].rearrange("p (g a) -> p g a", a=1).broadcast_to([P, TT * NG, EG])
                link(ve.tensor_tensor(r3(3), r3(3), off, ALU.add))
                for pick in range(2):
                    hot = R(6 + pick)
                    link(ve.tensor_reduce(r1(2), R(3), AX.X, mx))
                    link(ve.tensor_tensor(R(4), R(3), bc1(r1(2), NE), ALU.is_equal))
                    link(ve.tensor_tensor(R(4), R(4), bc_e(iota_e), ALU.mult))
                    link(ve.tensor_reduce(r1(3), R(4), AX.X, mx))
                    link(ve.tensor_tensor(hot, R(4), bc1(r1(3), NE), ALU.is_equal))
                    if pick == 0:
                        link(ve.scalar_tensor_tensor(R(3), hot, -BIG, R(3), ALU.mult, ALU.add))
                    link(ve.tensor_tensor(R(5), hot, R(1), ALU.mult))
                    link(ve.tensor_reduce(r1(4 + pick), R(5), AX.X, ALU.add))
                link(ve.tensor_tensor(R(8), R(6), R(7), ALU.add))
                ve.nop().then_inc(S("picked"), 1)
                link(ve.tensor_tensor(r1(6), r1(4), r1(5), ALU.add))
                link(ve.reciprocal(r1(7), r1(6)))
                for pick in range(2):
                    link(ve.tensor_tensor(gates[:, pick, :], r1(4 + pick), r1(7), ALU.mult))
                bank = t_ready(ve, (l, "rank", 0))
                ranks = bank[:, 0:TT * NE].rearrange("p (t e) -> p t e", e=NE)
                rows = bank[:, TT * NE:(TT + 1) * NE]
                e_more, e_upto, e_shift = (rt[:, 12, i, :] for i in range(3))
                e_tmp = rt[:, 13, 0, :]
                link(ve.tensor_scalar(e_more, rows, float(CAP), None, ALU.is_gt))
                for k in range(2, T // CAP):
                    link(ve.tensor_scalar(e_tmp, rows, float(CAP * k), None, ALU.is_gt))
                    link(ve.tensor_tensor(e_more, e_more, e_tmp, ALU.add))
                link(ve.tensor_tensor_scan(e_upto, ones[:, 0:NE], e_more, 0.0, ALU.mult, ALU.add))
                link(ve.tensor_tensor(e_shift, e_upto, e_more, ALU.subtract))
                link(ve.scalar_tensor_tensor(e_shift, e_shift, float(NE), num_e, ALU.add, ALU.subtract))
                link(ve.tensor_copy(nri[0:1, 0:1], e_upto[0:1, NE - 1:NE]))
                for b in range(MORE):
                    link(ve.tensor_scalar(e_tmp[0:1, :], e_upto[0:1, :], float(b), None, ALU.is_le))
                    link(ve.tensor_reduce(nrt[0:1, 0:1], e_tmp[0:1, :], AX.X, ALU.add))
                    link(ve.tensor_scalar(nri[0:1, 1 + b:2 + b], nrt[0:1, 0:1], float(NE - 1), None, ALU.min))
                ve.nop().then_inc(S("blocks_known"), 1)
                link(ve.tensor_scalar(R(11), ranks, float(CAP), None, ALU.is_ge))
                link(ve.tensor_tensor(R(9), R(11), bc_e(e_shift), ALU.mult))
                link(ve.tensor_tensor(R(9), R(9), bc_e(num_e), ALU.add))
                link(ve.scalar_tensor_tensor(R(10), R(11), -float(CAP), ranks, ALU.mult, ALU.add))
                for k in range(2, T // CAP):
                    link(ve.tensor_scalar(R(11), ranks, float(CAP * k), None, ALU.is_ge))
                    link(ve.tensor_tensor(R(9), R(9), R(11), ALU.add))
                    link(ve.scalar_tensor_tensor(R(10), R(11), -float(CAP), R(10), ALU.mult, ALU.add))
                ve.nop().then_inc(t_free((l, "rank", 0)), 1)
                if l:
                    for pick in range(2):
                        ve.wait_ge(S(f"back{pick}"), 16 * l * TT)
                for pick in range(2):
                    link(ve.tensor_tensor(R(5), R(9), R(6 + pick), ALU.mult))
                    link(ve.tensor_reduce(r1(8), R(5), AX.X, ALU.add))
                    link(ve.tensor_tensor(R(5), R(10), R(6 + pick), ALU.mult))
                    link(ve.tensor_reduce(r1(9), R(5), AX.X, ALU.add))
                    for t in range(TT):
                        i = pick * TT + t
                        ve.tensor_scalar(hot_c[:, i, :], num_c, r1(9)[:, t:t + 1], None, ALU.is_equal)
                        ve.tensor_scalar(hot_b[:, i, :], num_b, r1(8)[:, t:t + 1], tokid[:, t:t + 1], ALU.is_equal, ALU.mult)
                    link(ve.scalar_tensor_tensor(posu[:, pick, :], r1(8), float(CAP), r1(9), ALU.mult, ALU.add))
                ve.nop().then_inc(S("hot_ready"), 1)
                for cc in ADA_LATE:
                    mod_add(l, cc)
                if l + 1 < DEPTH:
                    for cc in ADA_FIRST:
                        mod_add(l + 1, cc)
                bank = t_ready(ve, (l, "ids", 0))
                ve.tensor_copy(ids[0:CAP, :], bank[0:CAP, 0:BLOCKS]).then_inc(t_free((l, "ids", 0)), 1)

                for e in range(NE):
                    n = l * NE + e
                    ve.wait_ge(S("silu_tanh"), n + 1)
                    if n:
                        ve.wait_ge(S("act_turned"), n)
                    link(ve.scalar_tensor_tensor(silu_t[0:CAP, :], silu_t[0:CAP, :], 1.0, G[0][0:CAP, :], ALU.add, ALU.mult))
                    ve.scalar_tensor_tensor(act[0:CAP, :], silu_t[0:CAP, :], 0.5, G[1][0:CAP, :], ALU.mult, ALU.mult)\
                        .then_inc(S("act_ready"), 1)
                more = ve.value_load(nri[0:1, 0:1], min_val=0, max_val=MORE)
                for b in range(MORE):
                    with ve.If(more > b):
                        ve.wait_ge(S(f"x_act{l}"), b * 4 + 2)
                        ve.scalar_tensor_tensor(silu_t[0:CAP, :], silu_t[0:CAP, :], 1.0, G[0][0:CAP, :], ALU.add, ALU.mult)\
                            .then_inc(S(f"x_silu{l}"), 1)
                        ve.wait_ge(S(f"x_silu{l}"), b + 1)
                        ve.scalar_tensor_tensor(act[0:CAP, :], silu_t[0:CAP, :], 0.5, G[1][0:CAP, :], ALU.mult, ALU.mult)\
                            .then_inc(S(f"x_dve{l}"), 1)
                    with ve.Else():
                        ve.nop()
                for t in range(TT):
                    ve.wait_ge(S("back0"), 16 * (l * TT + t + 1))
                    ve.wait_ge(S("back1"), 16 * (l * TT + t + 1))
                    if t:
                        ve.wait_ge(S("tran_done"), T_AT[(l, "comb", 2 * t - 1)] + 1)
                    link(ve.tensor_scalar(ysum, yg[0], gates[:, 0, t:t + 1], None, ALU.mult))
                    ve.scalar_tensor_tensor(ysum, yg[1], gates[:, 1, t:t + 1], ysum, ALU.mult, ALU.add)\
                        .then_inc(S("ysum_ready"), 1)
                    st = 0 if t == 0 else 1
                    for i in range(2):
                        g = (l, "comb", t * 2 + i)
                        bank = t_ready(ve, g)
                        for k in range(4):
                            kk = i * 4 + k
                            x = xT[:, kk, t * P:(t + 1) * P]
                            ins = ve.scalar_tensor_tensor(x, bank[:, k * P:(k + 1) * P], modA[:, 3, kk, st:st + 1], x,
                                                          ALU.mult, ALU.add)
                        ins.then_inc(t_free(g), 1)
                    for i in range(2):
                        t_read(ve, (l, "comb", t * 2 + i))
                    squares_of_tile(t)
            rstd()
            for k in range(KT):
                link(ve.tensor_tensor(hT[:, k, :], xT[:, k, :], rs, ALU.mult))
                ve.tensor_scalar(hT[:, k, :], hT[:, k, :], cvec[:, 16 + k:17 + k], None, ALU.mult).then_inc(S("final_h"), 1)

        @block.gpsimd
        def _(po):
            po.memset(gatew[:, :, :, :], 0.0).then_inc(S("gatew_zero"), 1)
            po.wait_ge(S("gatew_zero"), 1)
            po.wait_ge(S("zeroed"), 1)
            for b in range(MORE):
                row = (NE + b) * CAP
                po.dma_start(yd[row:row + CAP, :], zrow[0:CAP, :]).then_inc(S("rows_zero"), 16)
            for l in range(DEPTH):
                def modulated(which):
                    base = (2 * l + which) * KT
                    for k in range(KT):
                        po.wait_ge(S("xn_ready"), base + k + 1)
                        po.tensor_scalar(hT[:, k, 0:CTX], hT[:, k, 0:CTX], modA[:, which, k, 0:1],
                                         modT[:, which * 24 + k, 0:1], ALU.mult, ALU.add).then_inc(S("h_ready_p"), 1)

                modulated(0)
                for n, (d, j) in enumerate(PAIRS):
                    m = l * 16 + n
                    if m >= 2:
                        q = m - 2
                        po.wait_ge(S("gemm_done"), G_AT[(q // 16, "gate_x", q % 16)] + 1)
                    for which, w in enumerate((lru_wa, lru_wx)):
                        for half in range(2):
                            po.dma_start(gatew[half * 64:half * 64 + 64, which, n % 2, half * 64:half * 64 + 64],
                                         w[l, d, 2 * j + half]).then_inc(S(f"gatew_loaded{n % 2}"), 16)
                modulated(1)
                t_read(po, (l, "ids", 0))
                po.wait_ge(S("h2_stored"), (l + 1) * TT * 16)

                def gather(dst, idx, sem):
                    po.indirect_dma_start(out=dst, out_offset=None, in_=h2d[:, :],
                                          in_offset=bass.IndirectOffsetOnAxis(ap=idx, axis=0)).then_inc(sem, 16)

                for e in range(NE):
                    n = l * NE + e
                    if e >= 2:
                        po.wait_ge(S("x_turned"), n - 1)
                    gather(xg[e % 2][0:CAP, :], ids[0:CAP, e:e + 1], S(f"row_gathered{e % 2}"))
                po.wait_ge(S("blocks_known"), l + 1)
                more = po.value_load(nri[0:1, 0:1], min_val=0, max_val=MORE)
                for b in range(MORE):
                    with po.If(more > b):
                        po.wait_ge(S("experts_done"), l + 1)
                        if b:
                            po.wait_ge(S(f"x_pe{l}"), 4 * b)
                        gather(xg[0][0:CAP, :], ids[0:CAP, NE + b:NE + b + 1], S(f"x_gathered{l}"))
                    with po.Else():
                        po.nop()
                po.wait_ge(S("experts_done"), l + 1)
                po.wait_ge(S("blocks_over"), l + 1)
                po.wait_ge(S("rows_zero"), 16 * MORE)
                for t in range(TT):
                    if t:
                        po.wait_ge(S("ysum_ready"), l * TT + t)
                    for pick in range(2):
                        po.indirect_dma_start(out=yg[pick], out_offset=None, in_=yd[:, :],
                                              in_offset=bass.IndirectOffsetOnAxis(ap=posu[:, pick, t:t + 1], axis=0))\
                            .then_inc(S(f"back{pick}"), 16)


_INS = ["x_prompt", "x_sample", "cache_k", "cache_v", "state_h", "c", "c_ctx", "norm1_g", "norm2_g", "w_ada",
        "b_ada", "w_in", "conv_w", "conv_b", "lru_wa", "lru_ba", "lru_wx", "lru_bx", "lru_lambda", "attn_sink",
        "w_attn_proj", "w_rnn_proj", "w_out", "router_w", "router_b", "w_gate_up", "w_down", "final_norm_g"]
_OUTS = [(1, CTX, D), (1, LAT, D), (1, DEPTH, CTX, KVH, HD), (1, DEPTH, CTX, KVH, HD), (1, DEPTH, 2, D)]


def shape_constants():
    ident = np.eye(P, dtype=np.float32)
    rot = np.zeros((P, P), np.float32)
    half = HD // 2
    for i in range(half):
        rot[half + i, i] = -1.0
        rot[i, half + i] = 1.0
    t = np.arange(LAT)
    inv = (np.float32(10000.0) ** (-np.arange(HD // 4, dtype=np.float32) / np.float32(HD // 4))).astype(np.float32)
    ang = np.concatenate([(t // 64).astype(np.float32)[:, None] * inv, (t % 64).astype(np.float32)[:, None] * inv], 1)
    ang = np.concatenate([ang, ang], 1).T.astype(np.float32)
    i, j = np.meshgrid(np.arange(P), np.arange(P), indexing="ij")
    m0 = np.where(j <= i, 0.0, -BIG)
    m1 = np.where(j >= i, 0.0, -BIG)
    before = (i < j).astype(np.float32)
    sumsel = np.zeros((P, 2))
    sumsel[0::32, 0] = 1
    sumsel[1::32, 1] = 1
    row = lambda v: np.tile(np.asarray(v, np.float32)[None, :], (P, 1))
    tok = np.arange(T).reshape(TT, P).T
    parts = [ident, rot, np.cos(ang), np.sin(ang), m0, m1, before, sumsel, row(NE - np.arange(NE)),
             row(NG - np.arange(NG)), tok, row(np.arange(NE)), row(np.arange(BLOCKS)), row(np.arange(CAP))]
    return np.concatenate([np.asarray(p, np.float32) for p in parts], 1)


def kernel(**inputs):
    import concourse.bacc as _bacc
    from concourse.bass_utils import run_bass_kernel_spmd as _run

    nc = _bacc.Bacc("TRN2", target_bir_lowering=False, num_devices=1)
    arrays, args = {}, []
    for name in _INS:
        a = np.ascontiguousarray(inputs[name])
        arrays[f"in_{name}"] = a
        args.append(nc.dram_tensor(f"in_{name}", a.shape, mybir.dt.from_np(a.dtype), kind="ExternalInput").ap())
    a = shape_constants()
    arrays["shape_constants"] = a
    args.append(nc.dram_tensor("shape_constants", a.shape, F32, kind="ExternalInput").ap())
    for i, shape in enumerate(_OUTS):
        args.append(nc.dram_tensor(f"out_{i}", shape, F32, kind="ExternalOutput").ap())
    build(nc, *args)
    r = _run(nc, [arrays], core_ids=[0])
    return tuple(r.results[0][f"out_{i}"] for i in range(len(_OUTS)))
```

```python
import math
from contextlib import ExitStack

import numpy as np
import concourse.bass as bass
from concourse import mybir

F32 = mybir.dt.float32
F32R = mybir.dt.float32r
U32 = mybir.dt.uint32
I32 = mybir.dt.int32
ALU = mybir.AluOpType
ACT = mybir.ActivationFunctionType
AX = mybir.AxisListType

P = 128
D = 1024
KT = D // P
DEPTH = 2
CTX, LAT = 128, 256
T = CTX + LAT
TT = T // P
HEADS, KVH, HD = 8, 2, 128
GRP = HEADS // KVH
SCALE = HD ** -0.5
LATK = LAT + P
NADA = 6
NE, NG, EG = 16, 4, 4
DE = 512
EPS = 1e-6
CHUNK = 512
SLOTS = 3
CAP = 128
MORE = (2 * T - 1) // CAP
BLOCKS = NE + MORE
SEG = 3
CW = CTX + SEG + LAT
XW = CW + 3
LAT0 = CTX + SEG
GELU_C = math.sqrt(2.0 / math.pi)
BIG = 1e30

W_IN_COL = {"q0": 0, "q1": 512, "kv": 1024, "xr0": 1536, "xr1": 2048, "gr0": 2560, "gr1": 3072,
            "ga0": 3584, "ga1": 4096, "gb0": 4608, "gb1": 5120}
ADA_FIRST = range(4)


def chunk_order():
    o = [(0, f"ada{c}") for c in ADA_FIRST]
    for l in range(DEPTH):
        o += [(l, n) for n in ("kv", "q0", "ada4", "q1", "ada5", "xr0", "ada6", "xr1", "ada7", "gr0", "ada8",
                               "gr1", "ada9", "ga0", "ga1", "gb0", "gb1", "ap0", "ap1", "ada10", "rp0", "ada11",
                               "rp1")]
        nxt = [[(l + 1, f"ada{c}")] if l + 1 < DEPTH else [] for c in ADA_FIRST]
        o += nxt[0] + [(l, "wo0")] + nxt[1] + [(l, "wo1")] + nxt[2] + nxt[3]
        for e in range(NE):
            o += [(l, f"gu{e}.0"), (l, f"gu{e}.1")]
            if e:
                o.append((l, f"dn{e - 1}"))
        o.append((l, f"dn{NE - 1}"))
    return o


CHUNKS = chunk_order()
CHUNK_AT = {c: n for n, c in enumerate(CHUNKS)}


def chunk_slots():
    last, uses, out = [-1] * (SLOTS + 1), [0] * (SLOTS + 1), []
    for n, (_, name) in enumerate(CHUNKS):
        s = min(range(SLOTS + 1 if name[:2] in ("gu", "dn") else SLOTS), key=lambda i: last[i])
        out.append((s, uses[s], last[s]))
        last[s] = n
        uses[s] += 1
    return out


CHUNK_SLOT = chunk_slots()

SPLIT = [(kind, n) for kind in ("q", "xr", "gr", "ap", "rp", "wo") for n in range(KT)]
SPLIT_AT = {t: n for n, t in enumerate(SPLIT)}
EARLY = 3 * KT
AHEAD = 2
PAIRS_OF_PARTS = 3

UNITS = [(h, b) for h in range(HEADS) for b in range(3)]
PAIRS = [(d, j) for j in range(KT) for d in range(2)]


ADA_AFTER = {("ap", 7): (0, 10), ("rp", 3): (0, 11), ("rp", 7): (1, 0), ("wo", 3): (1, 1)}
ADA_SUM_AFTER = {("rp", 0): (0, 10), ("rp", 4): (0, 11), ("wo", 0): (1, 0), ("wo", 4): (1, 1)}


def gemm_order():
    o = [(0, "ada", c) for c in ADA_FIRST]
    for l in range(DEPTH):
        o += [(l, "k", 0), (l, "k", 1), (l, "kvc", 0), (l, "vl", 0), (l, "vl", 1)]
        for h in range(HEADS):
            o += [(l, "q", h), (l, "krot", h) if h < 2 else (l, "qrot", h - 2)]
            if h % 4 == 3:
                o.append((l, "ada", 4 + h // 4))
        for j in range(KT):
            o.append((l, "xr", j))
            if j < 2:
                o.append((l, "qrot", 6 + j))
            if j % 4 == 3:
                o.append((l, "ada", 6 + j // 4))
        for i in range(3 * KT):
            o.append((l, ("gr", "ga", "gb")[i // KT], i % KT))
            if i in (3, 7):
                o.append((l, "ada", 8 + i // 4))
            if i >= KT:
                o += [(l, "gate_a", i - KT), (l, "gate_x", i - KT)]
        for kind in ("ap", "rp", "wo"):
            for n in range(KT):
                o.append((l, kind, n))
                if (kind, n) in ADA_AFTER and ADA_AFTER[kind, n][0] + l < DEPTH:
                    o.append((l + ADA_AFTER[kind, n][0], "ada", ADA_AFTER[kind, n][1]))
        if l + 1 < DEPTH:
            o += [(l + 1, "ada", c) for c in (2, 3)]
        o.append((l, "logits", 0))
    return o


def tran_order():
    o = [(l, "vec", 0) for l in range(DEPTH)] + [(0, "mod", c) for c in ADA_FIRST]
    o += [(l, "kc", 0) for l in range(DEPTH)]
    for l in range(DEPTH):
        o += [(l, "mod", c) for c in range(4, 8)]
        for i in range(len(UNITS)):
            o.append((l, "pt", i))
            if i in (3, 7):
                o.append((l, "mod", 8 + i // 4))
        o += [(l, "mod", 10), (l, "mod", 11)]
        if l + 1 < DEPTH:
            o += [(l + 1, "mod", c) for c in ADA_FIRST]
        o += [(l, "h2", 0), (l, "h2", 1), (l, "logit", 0)] + [(l, "h2", i) for i in range(2, 2 * TT)]
        o += [(l, "state", 0), (l, "rank", 0)]
        o += [(l, "ids", 0)]
        o += [(l, "comb", i) for i in range(2 * TT)]
    return o


G_AT = {g: n for n, g in enumerate(gemm_order())}
T_AT = {g: n for n, g in enumerate(tran_order())}


def build(nc, x_prompt, x_sample, cache_k, cache_v, state_h, c, c_ctx, norm1_g, norm2_g, w_ada, b_ada,
          w_in, conv_w, conv_b, lru_wa, lru_ba, lru_wx, lru_bx, lru_lambda, attn_sink, w_attn_proj,
          w_rnn_proj, w_out, router_w, router_b, w_gate_up, w_down, final_norm_g,
          consts, y_prompt, y_sample, new_k, new_v, new_h):
    ctx = ExitStack()
    with ctx:
        sb_at = {}

        def sb(name, shape, dt=F32):
            sb_at[name] = nc.sbuf_base, shape
            return ctx.enter_context(nc.sbuf_tensor(name, shape, dt))

        def sb_r(name):
            base, shape = sb_at[name]
            return nc.alloc_sbuf_tensor_at(name + "_r", shape, F32R, offset=-(-base // 32) * 32)

        sems = {}

        def S(name):
            if name not in sems:
                sems[name] = ctx.enter_context(nc.semaphore(name))
            return sems[name]

        ring = sb("ring", [P, SLOTS, KT * CHUNK])
        xT = sb("xT", [P, KT, T])
        hT = sb("hT", [P, KT, T])
        parts = sb("parts", [P, 2, KT, T])
        qT = sb("qT", [P, HEADS, T])
        kT = sb("kT", [P, KVH, T])
        kcT = sb("kcT", [P, DEPTH, KVH, P])
        kvc = sb("kvc", [P, 512])
        vl = sb("vl", [P, 2, 256])
        vcache = sb("vcache", [P, DEPTH, 256])
        xp = sb("xp", [P, XW])
        xc = sb("xc", [P, KT, CW])
        gr = sb("gr", [P, KT, T])
        ga = sb("ga", [P, KT, T])
        gb = sb("gb", [P, KT, T])
        con = sb("con", [P, consts.shape[1]])
        ident, rotm, cosT, sinT = con[:, 0:128], con[:, 128:256], con[:, 256:512], con[:, 512:768]
        mask = [con[:, 768:896], con[:, 896:1024]]
        before = con[:, 1024:1152]
        sumsel = con[:, 1152:1154]
        iota_e = con[:, 1154:1170]
        iota_g = con[:, 1170:1174]
        tokid = con[:, 1174:1177]
        num_e = con[:, 1177:1193]
        num_b = con[:, 1193:1193 + BLOCKS]
        num_c = con[:, 1193 + BLOCKS:1193 + BLOCKS + CAP]
        sel_e = con[:, 1193 + BLOCKS + CAP:1193 + BLOCKS + CAP + NE]
        ones = sb("ones", [P, P])
        vec = sb("vec", [P, DEPTH, 2, P])
        crow = sb("crow", [24, P])
        cvec = sb("cvec", [P, 24])
        cpad = sb("cpad", [P, KT, 32])
        modT = sb("modT", [P, 48, 2])
        modA = sb("modA", [P, 4, KT, 2])
        sinkb = sb("sinkb", [P, DEPTH, HEADS])
        nsink = sb("nsink", [P, DEPTH, HEADS])
        sp = sb("sp", [P, 8, DEPTH, 16])
        hb = sb("hb", [P, 2, DEPTH, 16])
        gatew = sb("gatew", [P, 2, 2, P])
        hyb = sb("hyb", [P, CW])
        rs = hyb[:, 0:T]
        pr = sb("pr", [P, 2, LATK])
        pt = sb("pt", [P, 2, LATK])
        smx = sb("smx", [P, 2, 8])
        tmp = sb("tmp", [P, 7, CW])
        gelu_t = tmp[:, 4:6, 0:T]
        a2 = tmp[:, 6, :]
        adap = tmp[:, :, :].rearrange("p i n -> p (i n)")[:, 0:1024].rearrange("p (i n) -> p i n", i=2)
        hlast = sb("hlast", [P, 16])
        hrow = crow[0:16, :]
        rb = sb("rb", [P, NE])
        rw = sb("rw", [P, KT, 32])
        rt = pt[:, :, :].rearrange("p i n -> p (i n)")[:, 0:14 * TT * NE].rearrange("p (i t e) -> p i t e", i=14, t=TT)
        rt4 = sb("rt4", [P, 10, TT * NG])
        rt1 = sb("rt1", [P, 4, TT])
        rt2 = sb("rt2", [P, 9, 2, TT])
        rms_c = sb("rms_c", [P, 2, TT])
        lpart = tmp[:, 3, 0:T]
        gates = sb("gates", [P, 2, TT])
        posu = sb("posu", [P, 2, TT], U32)
        nrt = sb("nrt", [P, 4])
        nri = sb("nri", [1, 1 + MORE], I32)
        ids = sb("ids", [P, BLOCKS], U32)
        spare = sb("spare", [P, 1024])
        grf = gr[:, :, :].rearrange("p k t -> p (k t)")
        gaf = ga[:, :, :].rearrange("p k t -> p (k t)")
        gbf = gb[:, :, :].rearrange("p k t -> p (k t)")
        xg = [grf[:, 0:1024], grf[:, 1024:2048]]
        silu_t = grf[:, 2048:2560]
        act = grf[:, 2560:3072]
        xgT = [gaf[:, 0:1024].rearrange("p (k c) -> p k c", k=KT),
               gaf[:, 1024:2048].rearrange("p (k c) -> p k c", k=KT)]
        actT = [gaf[:, 2048 + 512 * i:2560 + 512 * i].rearrange("p (k c) -> p k c", k=4) for i in range(2)]
        parts_r, qT_r, gr_r = sb_r("parts"), sb_r("qT"), sb_r("gr")
        flat_r = lambda name: sb_r(name)[:, :, :].rearrange("p k t -> p (k t)")
        hTf, xcf, gaf_r, gbf_r, spare_r = flat_r("hT"), flat_r("xc"), flat_r("ga"), flat_r("gb"), sb_r("spare")
        part = lambda flat, i: flat[:, i * 1024:(i + 1) * 1024].rearrange("p (k c) -> p k c", k=KT)
        w_parts = [[(part(gaf_r, i), part(gbf_r, i)) for i in range(PAIRS_OF_PARTS)],
                   [(part(hTf, 0), part(hTf, 1)), (part(hTf, 2), part(spare_r, 0)), (part(xcf, 0), part(xcf, 1))]]
        yo = [gbf[:, 0:1024], gbf[:, 1024:2048]]
        yg = [[(grf, gaf)[pick][:, t * 1024:(t + 1) * 1024] for pick in range(2)] for t in range(TT)]
        diag = qT[:, :, :].rearrange("p h t -> p (h t)")[:, 0:2 * TT * P].rearrange("p (i c) -> p i c", c=P)
        zrow = gbf[:, 2048:3072]
        y_rows = gbf
        vrow = gaf[:, 0:DEPTH * 2 * P].rearrange("p (l i n) -> p l i n", l=DEPTH, i=2)
        kcache = gaf[:, 512:512 + DEPTH * 256].rearrange("p (l n) -> p l n", l=DEPTH)
        hot_c = gbf[:, 0:6 * CAP].rearrange("p (i c) -> p i c", i=6)
        hot_b = gbf[:, 768:768 + 6 * BLOCKS].rearrange("p (i b) -> p i b", i=6)

        banks = [ctx.enter_context(nc.psum_tensor(f"bank{i}", [P, 512], F32)) for i in range(8)]
        G, TB, SB, OB = banks[0:3], banks[3:5], banks[5:7], banks[7]
        out_banks = SB + G

        h2d = nc.dram_tensor("h2_rows", (T, D), F32, kind="Internal").ap()
        yd = nc.dram_tensor("expert_rows", (BLOCKS * CAP, D), F32, kind="Internal").ap()

        def g_ready(eng, g):
            eng.wait_ge(S("gemm_done"), G_AT[g] + 1)
            return G[G_AT[g] % 3]

        def g_free(g):
            return S(f"gbank_read{G_AT[g] % 3}")

        def g_read(eng, g):
            eng.wait_ge(g_free(g), G_AT[g] // 3 + 1)

        def t_ready(eng, g):
            eng.wait_ge(S("tran_done"), T_AT[g] + 1)
            return TB[T_AT[g] % 2]

        def t_free(g):
            return S(f"tbank_read{T_AT[g] % 2}")

        def t_read(eng, g):
            eng.wait_ge(t_free(g), T_AT[g] // 2 + 1)

        def split_no(l, kind, n):
            return l * len(SPLIT) + SPLIT_AT[kind, n]

        def w_part(kind, n):
            at = SPLIT_AT[kind, n]
            return w_parts[at // EARLY][at % EARLY % PAIRS_OF_PARTS]

        def released(n):
            l, name = CHUNKS[n]
            if name.startswith("gu"):
                e, half = name[2:].split(".")
                return S(("gu_half", "gu_done")[int(half)]), l * NE + int(e) + 1
            if name.startswith("dn"):
                return S("down_done"), l * NE + int(name[2:]) + 1
            if name.startswith("ada"):
                g = (l, "ada", int(name[3:]))
            elif name == "kv":
                g = (l, "vl", 1)
            else:
                g = (l, name[:-1], 4 * int(name[-1]) + 3)
                if g[1:] in SPLIT_AT:
                    return S("w_low"), split_no(*g) + 1
            return S("gemm_done"), G_AT[g] + 1

        gu_w = w_gate_up.rearrange("l e (h k p) n -> l e h p k n", p=P, h=2)
        dn_w = w_down.rearrange("l e (k p) n -> l e p k n", p=P)

        def chunk_src(l, name):
            if name.startswith("gu"):
                e, half = name[2:].split(".")
                return gu_w[l, int(e), int(half)]
            if name.startswith("dn"):
                return dn_w[l, int(name[2:])]
            if name.startswith("ada"):
                c0, w = int(name[3:]) * CHUNK, w_ada
            elif name in W_IN_COL:
                c0, w = W_IN_COL[name], w_in
            else:
                c0, w = int(name[2]) * CHUNK, {"ap": w_attn_proj, "rp": w_rnn_proj, "wo": w_out}[name[0:2]]
            return w[l].rearrange("(k p) n -> p k n", p=P)[:, :, c0:c0 + CHUNK]

        def slot_flat(s):
            return ring[:, s, :] if s < SLOTS else parts[:, :, :, :].rearrange("p i k t -> p (i k t)")[:, 0:KT * CHUNK]

        def slot_kn(s):
            return slot_flat(s).rearrange("p (k n) -> p k n", k=KT)

        def slot_wide(s):
            return slot_flat(s).rearrange("p (k n) -> p k n", k=4)

        def v_ada(l, j0, j1):
            return vec[:, l, 0, j0:j1]

        def v_conv(l, i, j):
            return vec[:, l, 0, 48 + i * 8 + j:49 + i * 8 + j]

        def v_convb(l, j):
            return vec[:, l, 0, 80 + j:81 + j]

        def v_state(l, d, j):
            return vec[:, l, 1, 48 + d * 8 + j:49 + d * 8 + j]

        STREAM = [slice(0, CTX), slice(CTX, T)]

        block = ctx.enter_context(nc.Block())

        @block.sync
        def _(sy):
            sy.dma_start(con[:, :], consts).then_inc(S("const_loaded"), 16)
            sy.dma_start(crow[0:8, :], c_ctx.rearrange("(k p) -> k p", p=P)).then_inc(S("const_loaded"), 16)
            sy.dma_start(crow[8:16, :], c.rearrange("b (k p) -> (b k) p", p=P)).then_inc(S("const_loaded"), 16)
            sy.dma_start(crow[16:24, :], final_norm_g.rearrange("(k p) -> k p", p=P)).then_inc(S("const_loaded"), 16)
            xs = grf[:, 0:3072].rearrange("p (t n) -> p t n", t=TT)
            for t in range(TT):
                src = x_prompt[0] if t == 0 else x_sample[0, (t - 1) * P:t * P, :]
                sy.dma_start(xs[:, t, :], src).then_inc(S(f"x_loaded{t}"), 16)

            def more_blocks(l):
                sy.wait_ge(S("blocks_known"), l + 1)
                more = sy.value_load(nri[0:1, 0:1], min_val=0, max_val=MORE)
                for b in range(MORE):
                    with sy.If(more > b):
                        e = sy.value_load(nri[0:1, 1 + b:2 + b], min_val=0, max_val=NE - 1)
                        if b == 0:
                            sy.wait_ge(S("experts_done"), l + 1)
                        for half in range(2):
                            sy.dma_start(slot_wide(half), gu_w[l, bass.ds(e, 1), half][0]).then_inc(S(f"x_loaded_w{l}"), 16)
                        sy.dma_start(slot_wide(2), dn_w[l, bass.ds(e, 1)][0]).then_inc(S(f"x_loaded_w{l}"), 16)
                        sy.wait_ge(S(f"x_y_ready{l}"), b + 1)
                        row = (NE + b) * CAP
                        sy.dma_start(yd[row:row + CAP, :], yo[0][0:CAP, :]).then_inc(S(f"x_stored{l}"), 16)
                        sy.wait_ge(S(f"x_stored{l}"), 16 * (b + 1))
                    with sy.Else():
                        sy.nop()
                sy.nop().then_inc(S("blocks_over"), 1)

            for n, (l, name) in enumerate(CHUNKS):
                s, use, before_it = CHUNK_SLOT[n]
                if before_it >= 0:
                    sy.wait_ge(*released(before_it))
                if s == SLOTS and name == "gu0.0":
                    sy.wait_ge(S("gemm_done"), G_AT[(l, "wo", KT - 1)] + 1)
                dst = slot_wide(s) if name[:2] in ("gu", "dn") else slot_kn(s)
                sy.dma_start(dst, chunk_src(l, name)).then_inc(S(f"w_loaded{s}"), 16)
                if name == f"dn{NE - 1}":
                    more_blocks(l)
                    if l + 1 < DEPTH:
                        for t in range(TT):
                            sy.wait_ge(S(f"back{t}"), 32 * (l + 1))
            for t in range(TT):
                sy.wait_ge(S("y_out_b"), t + 1)
                dst = y_prompt[0] if t == 0 else y_sample[0, (t - 1) * P:t * P, :]
                sy.dma_start(dst[:, 512:1024], y_rows[:, (2 * t + 1) * 512:(2 * t + 2) * 512]).then_inc(S("y_out_stored"), 16)

        @block.tensor
        def _(pe):
            def g_take(g):
                n = G_AT[g]
                if n >= 3:
                    pe.wait_ge(S(f"gbank_read{n % 3}"), n // 3)
                return G[n % 3]

            def t_take(g):
                n = T_AT[g]
                if n >= 2:
                    pe.wait_ge(S(f"tbank_read{n % 2}"), n // 2)
                return TB[n % 2]

            def weights(l, name):
                n = CHUNK_AT[(l, name)]
                s, use, _ = CHUNK_SLOT[n]
                pe.wait_ge(S(f"w_loaded{s}"), 16 * (use + 1))
                return s

            def product(g, slot, n, rhs, width=T):
                bank = g_take(g)
                for k in range(KT):
                    mm = pe.matmul(bank[:, 0:width], slot_kn(slot)[:, k, n * P:(n + 1) * P], rhs(k),
                                   start=(k == 0), stop=(k == KT - 1))
                mm.then_inc(S("gemm_done"), 1)

            def split_product(l, kind, n, high, low):
                pe.wait_ge(S("w_low"), split_no(l, kind, n) + 1)
                bank = g_take((l, kind, n))
                w_high, w_low = w_part(kind, n)
                for k in range(KT):
                    for i, (w, x) in enumerate(((w_high, high), (w_high, low), (w_low, high))):
                        mm = pe.matmul(bank[:, 0:T], w[:, k, :], x[:, k, :],
                                       start=(k == 0 and i == 0), stop=(k == KT - 1 and i == 2))
                mm.then_inc(S("gemm_done"), 1)

            def modulation(l, cc):
                s = weights(l, f"ada{cc}")
                bank = g_take((l, "ada", cc))
                for k in range(KT):
                    g = 32 * (k % 4)
                    mm = pe.matmul(bank[g:g + 32, :], cpad[:, k, :], slot_kn(s)[:, k, :],
                                   start=(k < 4), stop=(k >= 4), tile_position=(0, g))
                mm.then_inc(S("gemm_done"), 1)

            def mod_sum(l, cc):
                g_read(pe, (l, "ada", cc))
                bank = t_take((l, "mod", cc))
                for j in range(4):
                    mm = pe.matmul(bank[:, 2 * j:2 * j + 2], adap[:, cc % 2, j * P:(j + 1) * P], sumsel,
                                   start=(j == 0), stop=(j == 3), skip_group_check=True)
                mm.then_inc(S("tran_done"), 1)

            def square_sum(src, k, cols, count):
                pe.wait_ge(S("sq_ready"), count)
                return pe.matmul(OB[:, cols], ones[:, :], src[:, k, cols], start=(k == 0), stop=(k == KT - 1),
                                 skip_group_check=True)

            def square_sum_tiles(base, done):
                for t in range(TT):
                    cols = slice(t * P, (t + 1) * P)
                    for k in range(KT):
                        mm = square_sum(hT, k, cols, base + t + 1)
                mm.then_inc(done, 1)

            pe.wait_ge(S("const_loaded"), 64)
            pe.transpose(OB[:, 0:24], crow[:, :], ident[0:24, 0:24]).then_inc(S("cond_tran"), 1)
            xs = grf[:, 0:3072].rearrange("p (t n) -> p t n", t=TT)
            for t in range(TT):
                pe.wait_ge(S(f"x_loaded{t}"), 16)
                for i in range(2):
                    n = t * 2 + i
                    if n >= 2:
                        pe.wait_ge(S("x_taken"), n - 1)
                    for k in range(4):
                        kk = i * 4 + k
                        mm = pe.transpose(SB[i][:, k * P:(k + 1) * P], xs[:, t, kk * P:(kk + 1) * P], ident)
                    mm.then_inc(S("x_tran"), 1)
            pe.wait_ge(S("cond_ready"), 1)
            modulation(0, 0)
            square_sum_tiles(0, S("ss_done"))
            modulation(0, 1)
            pe.wait_ge(S("vec_loaded"), DEPTH * 9 * 16)
            for l in range(DEPTH):
                bank = t_take((l, "vec", 0))
                pe.transpose(bank[:, 0:104], vrow[0:104, l, 0, :], ident[0:104, 0:104])
                pe.transpose(bank[:, 128:192], vrow[0:64, l, 1, :], ident[0:64, 0:64]).then_inc(S("tran_done"), 1)
            mod_sum(0, 0)
            modulation(0, 2)
            mod_sum(0, 1)
            modulation(0, 3)
            mod_sum(0, 2)
            mod_sum(0, 3)
            pe.wait_ge(S("cache_loaded"), DEPTH * 32)
            for l in range(DEPTH):
                bank = t_take((l, "kc", 0))
                for g in range(KVH):
                    mm = pe.transpose(bank[:, g * P:(g + 1) * P], kcache[:, l, g * P:(g + 1) * P], ident)
                mm.then_inc(S("tran_done"), 1)

            for l in range(DEPTH):
                sq_base = TT + l * (KT + TT)

                def h_all(k):
                    return hT[:, k, :]

                s = weights(l, "kv")
                pe.wait_ge(S("h_ready_p"), 2 * l * KT + KT)
                pe.wait_ge(S("h_ready_a"), 2 * l * KT + KT)
                for g in range(KVH):
                    product((l, "k", g), s, g, h_all)
                bank = g_take((l, "kvc", 0))
                for k in range(KT):
                    mm = pe.matmul(bank[:, :], hT[:, k, 0:P], slot_kn(s)[:, k, :], start=(k == 0), stop=(k == KT - 1))
                mm.then_inc(S("gemm_done"), 1)
                for t in range(2):
                    bank = g_take((l, "vl", t))
                    for k in range(KT):
                        mm = pe.matmul(bank[:, 0:256], hT[:, k, (t + 1) * P:(t + 2) * P],
                                       slot_kn(s)[:, k, 256:512], start=(k == 0), stop=(k == KT - 1))
                    mm.then_inc(S("gemm_done"), 1)

                def rotated(kind, i):
                    bank = g_take((l, kind, i))
                    src = kT if kind == "krot" else qT
                    g_read(pe, (l, kind[0], i))
                    pe.matmul(bank[:, 0:LAT], rotm, src[:, i, CTX:T], start=True, stop=True).then_inc(S("gemm_done"), 1)

                pe.wait_ge(S("h_split"), (l + 1) * 2)
                for h in range(HEADS):
                    split_product(l, "q", h, parts_r[:, 0], parts_r[:, 1])
                    if h == 4:
                        mod_sum(l, 4)
                    if h < 2:
                        rotated("krot", h)
                    else:
                        rotated("qrot", h - 2)
                    if h % 4 == 3:
                        modulation(l, 4 + h // 4)
                for j in range(KT):
                    split_product(l, "xr", j, parts_r[:, 0], parts_r[:, 1])
                    if j < 2:
                        rotated("qrot", 6 + j)
                    if j % 4 == 0:
                        mod_sum(l, 5 + j // 4)
                    if j % 4 == 3:
                        modulation(l, 6 + j // 4)

                def scores(u):
                    h, b = UNITS[u]
                    n = l * len(UNITS) + u
                    g = h // GRP
                    if n >= 2:
                        pe.wait_ge(S("exp_done"), n - 1)
                    if b == 0:
                        pe.matmul(SB[u % 2][:, 0:P], qT[:, h, 0:P], kT[:, g, 0:P], start=True, stop=True)\
                            .then_inc(S("scores_done"), 1)
                        return
                    q = qT[:, h, b * P:(b + 1) * P]
                    pe.matmul(SB[u % 2][:, 0:LAT], q, kT[:, g, CTX:T], start=True, stop=True, skip_group_check=True)
                    pe.matmul(SB[u % 2][:, LAT:LATK], q, kcT[:, l, g, :], start=True, stop=True,
                              skip_group_check=True).then_inc(S("scores_done"), 1)

                def probs_turned(u):
                    h, b = UNITS[u]
                    bank = t_take((l, "pt", u))
                    pe.wait_ge(S("probs_ready"), l * len(UNITS) + u + 1)
                    for i in range(1 if b == 0 else 3):
                        mm = pe.transpose(bank[:, i * P:(i + 1) * P], pr[:, u % 2, i * P:(i + 1) * P], ident)
                    mm.then_inc(S("tran_done"), 1)

                def attend(u):
                    h, b = UNITS[u]
                    g = h // GRP
                    n = l * len(UNITS) + u
                    t_read(pe, (l, "pt", u))
                    if n >= 1:
                        pe.wait_ge(S("att_copied"), n)
                    vals = [kvc[:, 256 + g * P:256 + (g + 1) * P]] if b == 0 else \
                        [vl[:, 0, g * P:(g + 1) * P], vl[:, 1, g * P:(g + 1) * P], vcache[:, l, g * P:(g + 1) * P]]
                    for i, v in enumerate(vals):
                        mm = pe.matmul(OB[:, 0:P], v, pt[:, u % 2, i * P:(i + 1) * P],
                                       start=(i == 0), stop=(i == len(vals) - 1))
                    mm.then_inc(S("att_done"), 1)

                pe.wait_ge(S("rope_done"), (l + 1) * 10)
                for i in range(3 * KT):
                    kind = ("gr", "ga", "gb")[i // KT]
                    if i % 4 == 0 and kind != "gr":
                        s = weights(l, kind + str(i % KT // 4))
                    scores(i)
                    if kind == "gr":
                        split_product(l, kind, i, parts_r[:, 0], parts_r[:, 1])
                    else:
                        product((l, kind, i % KT), s, i % 4, h_all)
                    if i % 4 == 0 and i <= KT:
                        mod_sum(l, 7 + i // 4)
                    probs_turned(i)
                    if i in (3, 7):
                        modulation(l, 8 + i // 4)
                    if i >= KT:
                        n = i - KT
                        d, j = PAIRS[n]
                        pe.wait_ge(S("xc_ready"), l * KT + j + 1)
                        pe.wait_ge(S(f"gatew_loaded{n % 2}"), (l * 8 + n // 2 + 1) * 64)
                        for which, name in ((0, "gate_a"), (1, "gate_x")):
                            bank = g_take((l, name, n))
                            pe.matmul(bank[:, 0:CW], gatew[:, which, n % 2, :], xc[:, j, :],
                                      start=True, stop=True).then_inc(S("gemm_done"), 1)
                    if i >= 1:
                        attend(i - 1)
                attend(3 * KT - 1)
                pe.wait_ge(S("att_split"), (l + 1) * HEADS)
                for name, high, low in (("ap", parts_r[:, 0], parts_r[:, 1]), ("rp", qT_r, gr_r),
                                        ("wo", parts_r[:, 0], parts_r[:, 1])):
                    for n in range(KT):
                        if n == 0 and name == "rp":
                            pe.wait_ge(S("rnn_ready"), (l + 1) * KT)
                        if n == 0 and name == "wo":
                            pe.wait_ge(S("merged_ready"), (l + 1) * KT)
                        split_product(l, name, n, high, low)
                        if n and name == "wo":
                            square_sum(gr, n - 1, slice(0, T), sq_base + n)
                        for plan, do in ((ADA_SUM_AFTER, mod_sum), (ADA_AFTER, modulation)):
                            if (name, n) in plan and plan[name, n][0] + l < DEPTH:
                                do(l + plan[name, n][0], plan[name, n][1])
                square_sum(gr, KT - 1, slice(0, T), sq_base + KT).then_inc(S("ss_done"), 1)
                if l + 1 < DEPTH:
                    modulation(l + 1, 2)
                    modulation(l + 1, 3)
                    mod_sum(l + 1, 2)
                    mod_sum(l + 1, 3)
                bank = g_take((l, "logits", 0))
                for k in range(KT):
                    pe.wait_ge(S("h_ready_p"), (2 * l + 1) * KT + k + 1)
                    pe.wait_ge(S("h_ready_a"), (2 * l + 1) * KT + k + 1)
                    g = 32 * (k % 4)
                    mm = pe.matmul(bank[g:g + 32, 0:T], rw[:, k, :], hT[:, k, :],
                                   start=(k < 4), stop=(k >= 4), tile_position=(0, g))
                mm.then_inc(S("gemm_done"), 1)

                def h2_rows(i):
                    bank = t_take((l, "h2", i))
                    for k in range(4):
                        mm = pe.transpose(bank[:, k * P:(k + 1) * P], hT[:, i % 2 * 4 + k, i // 2 * P:(i // 2 + 1) * P], ident)
                    mm.then_inc(S("tran_done"), 1)

                h2_rows(0)
                h2_rows(1)
                bank = t_take((l, "logit", 0))
                pe.wait_ge(S("logits_copied"), l + 1)
                for t in range(TT):
                    mm = pe.matmul(bank[:, t * NE:(t + 1) * NE], lpart[:, t * P:(t + 1) * P], sel_e,
                                   start=True, stop=True, skip_group_check=True)
                mm.then_inc(S("tran_done"), 1)
                for i in range(2, 2 * TT):
                    h2_rows(i)
                bank = t_take((l, "state", 0))
                pe.wait_ge(S("hlast_ready"), (l + 1) * 16)
                pe.transpose(bank[0:16, 0:P], hlast[:, :], ident).then_inc(S("tran_done"), 1)
                bank = t_take((l, "rank", 0))
                pe.wait_ge(S("picked"), l + 1)
                for t in range(TT + 1):
                    for i in range(min(t + 1, TT)):
                        lhs = before if i == t else ones[:, :]
                        mm = pe.matmul(bank[:, t * NE:(t + 1) * NE], lhs, rt[:, 8, i, :],
                                       start=(i == 0), stop=(i == min(t, TT - 1)), skip_group_check=True)
                mm.then_inc(S("tran_done"), 1)
                bank = t_take((l, "ids", 0))
                pe.wait_ge(S("hot_ready"), l + 1)
                for i in range(6):
                    mm = pe.matmul(bank[0:CAP, 0:BLOCKS], hot_c[:, i, :], hot_b[:, i, :], start=(i == 0), stop=(i == 5))
                mm.then_inc(S("tran_done"), 1)

                def turn_rows(e, xrows, x_done, dst_banks):
                    for i in range(2):
                        for k in range(4):
                            kk = i * 4 + k
                            mm = pe.transpose(dst_banks[i][:, k * CAP:(k + 1) * CAP],
                                              xrows[0:CAP, kk * P:(kk + 1) * P], ident[0:CAP, 0:CAP])
                    mm.then_inc(x_done, 1)

                def gate_up(slots, xt, done, half_done):
                    for half in range(2):
                        for n in range(2):
                            for k in range(4):
                                mm = pe.matmul(G[n][0:CAP, :], xt[:, half * 4 + k, 0:CAP],
                                               slot_wide(slots[half])[:, k, n * 512:(n + 1) * 512],
                                               start=(half == 0 and k == 0), stop=(half == 1 and k == 3))
                        if half == 1:
                            mm.then_inc(done, 1)
                        elif half_done is not None:
                            mm.then_inc(half_done, 1)

                def down(slot, at, done):
                    for n in range(2):
                        for k in range(4):
                            mm = pe.matmul(SB[n][0:CAP, :], at[:, k, 0:CAP], slot_wide(slot)[:, k, n * 512:(n + 1) * 512],
                                           start=(k == 0), stop=(k == 3))
                    mm.then_inc(done, 1)

                def xturn(e):
                    n = l * NE + e
                    pe.wait_ge(S(f"row_gathered{e % 2}"), 16 * (l * NE // 2 + e // 2 + 1))
                    if e == 0:
                        for b in range(2):
                            pe.wait_ge(S(f"tbank_read{b}"), len(range(b, T_AT[(l, "comb", 0)], 2)))
                    else:
                        pe.wait_ge(S("xgT_copied"), n)
                    turn_rows(e, xg[e % 2], S("x_turned"), TB)

                def gu(e):
                    n = l * NE + e
                    pe.wait_ge(S("xgT_copied"), n + 1)
                    if e == 0:
                        done = G_AT[(l, "logits", 0)]
                        for b in range(2):
                            pe.wait_ge(S(f"gbank_read{b}"), len(range(b, done + 1, 3)))
                    slots = [weights(l, f"gu{e}.{half}") for half in range(2)]
                    gate_up(slots, xgT[e % 2], S("gu_done"), S("gu_half"))

                def dn(e):
                    n = l * NE + e
                    if n >= 1:
                        pe.wait_ge(S("y_copied"), n)
                    pe.wait_ge(S("actT_copied"), n + 1)
                    down(weights(l, f"dn{e}"), actT[e % 2], S("down_done"))

                def aturn(e):
                    n = l * NE + e
                    pe.wait_ge(S("act_ready"), n + 1)
                    for k in range(4):
                        mm = pe.transpose(OB[:, k * CAP:(k + 1) * CAP], act[0:CAP, k * P:(k + 1) * P], ident[0:CAP, 0:CAP])
                    mm.then_inc(S("act_turned"), 1)

                xturn(0)
                for e in range(NE):
                    gu(e)
                    if e + 1 < NE:
                        xturn(e + 1)
                    if e >= 1:
                        dn(e - 1)
                    aturn(e)
                dn(NE - 1)
                pe.wait_ge(S("blocks_known"), l + 1)
                more = pe.value_load(nri[0:1, 0:1], min_val=0, max_val=MORE)
                for b in range(MORE):
                    with pe.If(more > b):
                        pe.wait_ge(S("experts_done"), l + 1)
                        pe.wait_ge(S(f"x_gathered{l}"), 16 * (b + 1))
                        turn_rows(0, xg[0], S(f"x_pe{l}"), TB)
                        pe.wait_ge(S(f"x_act{l}"), b * 4 + 1)
                        pe.wait_ge(S(f"x_loaded_w{l}"), 48 * (b + 1))
                        gate_up([0, 1], xgT[0], S(f"x_pe{l}"), None)
                        pe.wait_ge(S(f"x_dve{l}"), b + 1)
                        for k in range(4):
                            mm = pe.transpose(OB[:, k * CAP:(k + 1) * CAP], act[0:CAP, k * P:(k + 1) * P],
                                              ident[0:CAP, 0:CAP])
                        mm.then_inc(S(f"x_pe{l}"), 1)
                        pe.wait_ge(S(f"x_act{l}"), b * 4 + 3)
                        down(2, actT[0], S(f"x_pe{l}"))
                    with pe.Else():
                        pe.nop()
                def combined(t):
                    pe.wait_ge(S("diag_ready"), l + 1)
                    pe.wait_ge(S(f"back{t}"), 32 * (l + 1))
                    for i in range(2):
                        g = (l, "comb", t * 2 + i)
                        if t == 0:
                            pe.wait_ge(S("xgT_copied"), (l + 1) * NE)
                            bank = TB[T_AT[g] % 2]
                        else:
                            bank = t_take(g)
                        for k in range(4):
                            kk = i * 4 + k
                            for pick in range(2):
                                mm = pe.matmul(bank[:, k * P:(k + 1) * P], yg[t][pick][:, kk * P:(kk + 1) * P],
                                               diag[:, pick * TT + t, :], start=(pick == 0), stop=(pick == 1),
                                               skip_group_check=True)
                        mm.then_inc(S("tran_done"), 1)

                if l + 1 < DEPTH:
                    for t in range(TT):
                        combined(t)
                    square_sum_tiles(sq_base + KT, S("ss_done"))
                    continue

                def final_rows(t):
                    cols = slice(t * P, (t + 1) * P)
                    pe.wait_ge(S("sq_ready"), sq_base + KT + t + 1)
                    if t:
                        pe.wait_ge(S("final_rms"), t)
                    for k in range(KT):
                        mm = pe.matmul(OB[:, t:t + 1], hT[:, k, cols], ones[:, 0:1], start=(k == 0), stop=(k == KT - 1),
                                       skip_group_check=True)
                    mm.then_inc(S("final_ss"), 1)
                    pe.wait_ge(S("xg_ready"), t + 1)
                    for i in range(2):
                        n = 2 * t + i
                        if n >= len(out_banks):
                            pe.wait_ge(S("y_out_a"), 1)
                        for k in range(4):
                            mm = pe.transpose(out_banks[n % len(out_banks)][:, k * P:(k + 1) * P],
                                              xc[:, i * 4 + k, cols], ident)
                        mm.then_inc(S("y_out_turned"), 1)

                for t in range(TT + 1):
                    if t < TT:
                        combined(t)
                    if t:
                        final_rows(t - 1)

        @block.scalar
        def _(ac):
            chain = [0]

            def link(ins):
                chain[0] += 1
                ins.then_inc(S("act_chain"), 1)
                ac.wait_ge(S("act_chain"), chain[0])

            def small_loads(l):
                rows = [(0, 0, 48, b_ada[l].rearrange("(k p) -> k p", p=P)),
                        (0, 48, 32, conv_w[l].rearrange("i (k p) -> (i k) p", p=P)),
                        (0, 80, 8, conv_b[l].rearrange("(k p) -> k p", p=P)),
                        (0, 88, 8, norm1_g[l].rearrange("(k p) -> k p", p=P)),
                        (0, 96, 8, norm2_g[l].rearrange("(k p) -> k p", p=P)),
                        (1, 0, 16, lru_ba[l].rearrange("d (k p) -> (d k) p", p=P)),
                        (1, 16, 16, lru_bx[l].rearrange("d (k p) -> (d k) p", p=P)),
                        (1, 32, 16, lru_lambda[l].rearrange("d (k p) -> (d k) p", p=P)),
                        (1, 48, 16, state_h[0, l].rearrange("d (k p) -> (d k) p", p=P))]
                for which, r0, n, src in rows:
                    ac.dma_start(vrow[r0:r0 + n, l, which, :], src).then_inc(S("vec_loaded"), 16)
                ac.dma_start(kcache[:, l, :], cache_k[0, l].rearrange("t g d -> t (g d)")).then_inc(S("cache_loaded"), 16)
                ac.dma_start(vcache[:, l, :], cache_v[0, l].rearrange("t g d -> t (g d)")).then_inc(S("cache_loaded"), 16)

            for l in range(DEPTH):
                small_loads(l)
            ac.dma_start(rb[:, :], router_b.rearrange("(a n) -> a n", a=1).broadcast_to([P, NE])).then_inc(S("router_loaded"), 16)
            ac.wait_ge(S("zeroed"), 1)
            ac.dma_start(rw[:, :, 0:NE], router_w.rearrange("(k p) n -> p k n", p=P)).then_inc(S("router_loaded"), 16)
            ac.dma_start(sinkb[:, :, :].rearrange("p l h -> p (l h)"),
                         attn_sink.rearrange("(a l) h -> a (l h)", a=1).broadcast_to([P, DEPTH * HEADS])).then_inc(S("router_loaded"), 16)
            ac.wait_ge(S("cond_tran"), 1)
            ac.activation(cvec[:, :], OB[:, 0:24], ACT.Copy).then_inc(S("cvec_ready"), 1)
            ac.activation(tmp[:, 6, 0:16], OB[:, 0:16], ACT.Tanh, scale=0.5).then_inc(S("cond_tanh"), 1)
            def ada_copy(l, cc):
                bank = g_ready(ac, (l, "ada", cc))
                n = l * 12 + cc
                if n >= 2:
                    m = n - 2
                    ac.wait_ge(S("tran_done"), T_AT[(m // 12, "mod", m % 12)] + 1)
                ac.activation(adap[:, cc % 2, :], bank[:, :], ACT.Copy).then_inc(g_free((l, "ada", cc)), 1)

            def rms(n):
                ac.wait_ge(S("ss_done"), n + 1)
                ac.activation(rs, OB[:, 0:T], ACT.Sqrt, bias=EPS, scale=1.0 / D).then_inc(S("rms_ready"), 1)

            ada_copy(0, 0)
            rms(0)
            for cc in (1, 2, 3):
                ada_copy(0, cc)
            ac.wait_ge(S("lam_abs"), 1)
            ac.activation(sp[:, 1, :, :], sp[:, 0, :, :], ACT.Exp, scale=-1.0).then_inc(S("lam_exp"), 1)

            for l in range(DEPTH):

                def high_part(at):
                    kind, n = SPLIT[at]
                    s, use, _ = CHUNK_SLOT[CHUNK_AT[(l, f"{kind}{n // 4}")]]
                    ac.wait_ge(S(f"w_loaded{s}"), 16 * (use + 1))
                    nth = at % EARLY
                    if nth >= PAIRS_OF_PARTS:
                        ac.wait_ge(S("gemm_done"), G_AT[(l, *SPLIT[at - PAIRS_OF_PARTS])] + 1)
                    elif at >= EARLY:
                        ac.wait_ge(S("gemm_done"), G_AT[(l, "gb", KT - 1)] + 1)
                        if nth == 2:
                            ac.wait_ge(S("lru_used"), (l + 1) * 16)
                    elif l == 0:
                        ac.wait_ge(S("tran_done"), T_AT[(DEPTH - 1, "kc", 0)] + 1)
                    ac.activation(w_part(kind, n)[0], slot_kn(s)[:, :, n % 4 * P:(n % 4 + 1) * P], ACT.Copy)\
                        .then_inc(S("w_high"), 1)

                def modulated(which):
                    base = (2 * l + which) * KT
                    for k in range(KT):
                        ac.wait_ge(S("xn_ready"), base + k + 1)
                        ac.activation(hT[:, k, CTX:T], hT[:, k, CTX:T], ACT.Identity,
                                      bias=modT[:, which * 24 + k, 1:2], scale=modA[:, which, k, 1:2])\
                            .then_inc(S("h_ready_a"), 1)

                if l:
                    rms(2 * l)
                ac.wait_ge(S("first_mods"), l + 1)
                modulated(0)

                for at in range(AHEAD):
                    high_part(at)

                def copy_out(g, dst, width):
                    bank = g_ready(ac, g)
                    ac.activation(dst, bank[:, 0:width], ACT.Copy).then_inc(g_free(g), 1)

                for g in range(KVH):
                    copy_out((l, "k", g), kT[:, g, :], T)
                if l:
                    ac.wait_ge(S("cache_stored"), l * 32)
                copy_out((l, "kvc", 0), kvc[:, :], 512)
                for t in range(2):
                    copy_out((l, "vl", t), vl[:, t, :], 256)
                for h in range(HEADS):
                    high_part(h + AHEAD)
                    copy_out((l, "q", h), qT[:, h, :], T)
                    if h == 0:
                        g_read(ac, (l, "kvc", 0))
                        ac.dma_start(new_k[0, l].rearrange("t g d -> t (g d)"), kvc[:, 0:256]).then_inc(S("cache_stored"), 16)
                        ac.dma_start(new_v[0, l].rearrange("t g d -> t (g d)"), kvc[:, 256:512]).then_inc(S("cache_stored"), 16)
                    if h % 4 == 3:
                        ada_copy(l, 4 + h // 4)
                for j in range(KT):
                    high_part(KT + j + AHEAD)
                    bank = g_ready(ac, (l, "xr", j))
                    n = l * KT + j
                    if n >= 1:
                        ac.wait_ge(S("xc_ready"), n)
                    else:
                        ac.wait_ge(S("zeroed"), 1)
                    ac.activation(xp[:, 2:2 + CTX], bank[:, 0:CTX], ACT.Copy)
                    ac.activation(xp[:, 2 + LAT0:2 + CW], bank[:, CTX:T], ACT.Copy).then_inc(g_free((l, "xr", j)), 1)
                    if j % 4 == 3:
                        ada_copy(l, 6 + j // 4)

                def exps(u):
                    h, b = UNITS[u]
                    n = l * len(UNITS) + u
                    w = P if b == 0 else LATK
                    ac.wait_ge(S("max_ready"), n + 1)
                    if n >= 2:
                        m = n - 2
                        ac.wait_ge(S("tran_done"), T_AT[(m // 24, "pt", m % 24)] + 1)
                    ac.activation(pr[:, u % 2, 0:w], SB[u % 2][:, 0:w], ACT.Exp, bias=smx[:, u % 2, 1:2],
                                  scale=SCALE, accum_out=smx[:, u % 2, 2:3])
                    ac.activation(smx[:, u % 2, 3:4], sinkb[:, l, h:h + 1], ACT.Exp, bias=smx[:, u % 2, 1:2])\
                        .then_inc(S("exp_done"), 1)

                def pt_copy(u):
                    h, b = UNITS[u]
                    n = l * len(UNITS) + u
                    w = P if b == 0 else LATK
                    bank = t_ready(ac, (l, "pt", u))
                    if n >= 2:
                        ac.wait_ge(S("att_done"), n - 1)
                    ac.activation(pt[:, u % 2, 0:w], bank[:, 0:w], ACT.Copy).then_inc(t_free((l, "pt", u)), 1)

                def att_copy(u):
                    h, b = UNITS[u]
                    ac.wait_ge(S("att_done"), l * len(UNITS) + u + 1)
                    ac.activation(qT[:, h, b * P:(b + 1) * P], OB[:, 0:P], ACT.Copy).then_inc(S("att_copied"), 1)

                def lru_tables(n):
                    d, j = PAIRS[n]
                    m = l * 16 + n
                    if m >= 2:
                        ac.wait_ge(S("lru_used"), m - 1)
                    if n < 2:
                        ac.wait_ge(S("gelu_done"), (l + 1) * KT)
                    a, th, ti = tmp[:, n % 2, :], tmp[:, 2 + n % 2, :], tmp[:, 4 + n % 2, :]
                    bank = g_ready(ac, (l, "gate_a", n))
                    cb = d * 8 + j
                    c_log = [sp[:, i, l, cb:cb + 1] for i in (6, 7)]
                    ac.activation(a, bank[:, 0:CW], ACT.Tanh, bias=hb[:, 0, l, cb:cb + 1], scale=0.5)\
                        .then_inc(g_free((l, "gate_a", n)), 1)
                    bank = g_ready(ac, (l, "gate_x", n))
                    ac.activation(ti, bank[:, 0:CW], ACT.Tanh, bias=hb[:, 1, l, cb:cb + 1], scale=0.5)\
                        .then_inc(g_free((l, "gate_x", n)), 1)
                    g_read(ac, (l, "gate_a", n))
                    ac.activation(th, a, ACT.Tanh, bias=c_log[1], scale=c_log[1])
                    link(ac.activation(a, a, ACT.Exp, bias=c_log[0], scale=c_log[0]))
                    if m:
                        ac.wait_ge(S("lru_square"), m)
                    ac.activation(a2, a, ACT.Square).then_inc(S("lru_act"), 1)

                def lru_root(n):
                    ac.wait_ge(S("lru_square"), l * 16 + n + 1)
                    th = tmp[:, 2 + n % 2, :]
                    ac.activation(th, th, ACT.Sqrt, scale=0.25).then_inc(S("root_ready"), 1)

                def gelu_tanh(j):
                    ac.wait_ge(S("gelu_arg"), l * KT + j + 1)
                    ac.activation(gelu_t[:, j % 2, :], gelu_t[:, j % 2, :], ACT.Tanh, scale=GELU_C)\
                        .then_inc(S("gelu_tanh"), 1)

                for i in range(3 * KT):
                    kind = ("gr", "ga", "gb")[i // KT]
                    j = i % KT
                    exps(i)
                    if 1 <= i <= KT:
                        gelu_tanh(i - 1)
                    if i > KT:
                        lru_root(i - KT - 1)
                    if i + AHEAD < KT:
                        high_part(2 * KT + i + AHEAD)
                    if kind == "gr":
                        copy_out((l, kind, j), gr[:, j, :], T)
                        g_read(ac, (l, kind, j))
                        if l * KT + j >= 2:
                            ac.wait_ge(S("gelu_done"), l * KT + j - 1)
                        if l and j == 0:
                            ac.wait_ge(S("lru_used"), l * 16)
                        ac.activation(gelu_t[:, j % 2, :], gr[:, j, :], ACT.Square).then_inc(S("gelu_sq"), 1)
                    else:
                        dst = ga if kind == "ga" else gb
                        g = (l, kind, j)
                        bank = g_ready(ac, g)
                        ac.activation(dst[:, j, :], bank[:, 0:T], ACT.Tanh, scale=0.5).then_inc(g_free(g), 1)
                    pt_copy(i)
                    if i in (3, 7):
                        ada_copy(l, 8 + i // 4)
                    if i >= KT:
                        lru_tables(i - KT)
                    if i >= 1:
                        att_copy(i - 1)
                lru_root(15)
                high_part(EARLY)
                att_copy(23)
                high_part(EARLY + 1)
                for at in range(EARLY, len(SPLIT)):
                    if at + AHEAD < len(SPLIT):
                        high_part(at + AHEAD)
                    ahead, cc = ADA_AFTER.get(SPLIT[at], (DEPTH, 0))
                    if l + ahead < DEPTH:
                        ada_copy(l + ahead, cc)
                rms(2 * l + 1)
                if l + 1 < DEPTH:
                    ada_copy(l + 1, 2)
                    ada_copy(l + 1, 3)
                modulated(1)
                bank = g_ready(ac, (l, "logits", 0))
                ac.activation(lpart, bank[:, 0:T], ACT.Copy).then_inc(g_free((l, "logits", 0)), 1)
                g_read(ac, (l, "logits", 0))
                ac.nop().then_inc(S("logits_copied"), 1)
                for t in range(TT):
                    for i in range(2):
                        g = (l, "h2", t * 2 + i)
                        bank = t_ready(ac, g)
                        ac.activation(grf[:, t * 1024 + i * 512:t * 1024 + (i + 1) * 512], bank[:, :], ACT.Copy)\
                            .then_inc(t_free(g), 1)
                    if t == 0:
                        bank = t_ready(ac, (l, "logit", 0))
                        ac.activation(rt[:, 0, :, :].rearrange("p t e -> p (t e)"), bank[:, 0:TT * NE], ACT.Exp, scale=-1.0)\
                            .then_inc(t_free((l, "logit", 0)), 1)
                    for i in range(2):
                        t_read(ac, (l, "h2", t * 2 + i))
                    ac.dma_start(h2d[t * P:(t + 1) * P, :], grf[:, t * 1024:(t + 1) * 1024]).then_inc(S("h2_stored"), 16)
                bank = t_ready(ac, (l, "state", 0))
                if l:
                    ac.wait_ge(S("state_stored"), 16 * l)
                ac.activation(hrow[:, :], bank[0:16, 0:P], ACT.Copy).then_inc(t_free((l, "state", 0)), 1)
                t_read(ac, (l, "state", 0))
                ac.dma_start(new_h[0, l].rearrange("d (k p) -> (d k) p", p=P), hrow[:, :]).then_inc(S("state_stored"), 16)

                def copy_x(e):
                    n = l * NE + e
                    ac.wait_ge(S("x_turned"), n + 1)
                    if n >= 2:
                        ac.wait_ge(S("gu_done"), n - 1)
                    for i in range(2):
                        ins = ac.activation(xgT[e % 2][:, i * 4:(i + 1) * 4, 0:CAP],
                                            TB[i][:, 0:4 * CAP].rearrange("p (k c) -> p k c", k=4), ACT.Copy)
                    ins.then_inc(S("xgT_copied"), 1)

                def tanh_g(e):
                    n = l * NE + e
                    ac.wait_ge(S("gu_done"), n + 1)
                    if n:
                        ac.wait_ge(S("act_ready"), n)
                    ac.activation(silu_t[0:CAP, :], G[0][0:CAP, :], ACT.Tanh, scale=0.5).then_inc(S("silu_tanh"), 1)

                def copy_act(e):
                    n = l * NE + e
                    ac.wait_ge(S("act_turned"), n + 1)
                    if n >= 2:
                        ac.wait_ge(S("down_done"), n - 1)
                    ac.activation(actT[e % 2][:, :, 0:CAP], OB[:, 0:4 * CAP].rearrange("p (k c) -> p k c", k=4),
                                  ACT.Copy).then_inc(S("actT_copied"), 1)

                def copy_y(e):
                    n = l * NE + e
                    ac.wait_ge(S("down_done"), n + 1)
                    if n >= 2:
                        ac.wait_ge(S(f"y_stored{e % 2}"), 16 * (n // 2))
                    for i in range(2):
                        ins = ac.activation(yo[e % 2][0:CAP, i * 512:(i + 1) * 512], SB[i][0:CAP, :], ACT.Copy)
                    ins.then_inc(S("y_copied"), 1)
                    ac.wait_ge(S("y_copied"), n + 1)
                    ac.dma_start(yd[e * CAP:(e + 1) * CAP, :], yo[e % 2][0:CAP, :]).then_inc(S(f"y_stored{e % 2}"), 16)

                copy_x(0)
                for e in range(NE):
                    tanh_g(e)
                    if e + 1 < NE:
                        copy_x(e + 1)
                    if e >= 1:
                        copy_y(e - 1)
                    copy_act(e)
                copy_y(NE - 1)
                for b in range(2):
                    ac.wait_ge(S(f"y_stored{b}"), 16 * (l + 1) * NE // 2)
                ac.nop().then_inc(S("experts_done"), 1)
                ac.wait_ge(S("blocks_known"), l + 1)
                more = ac.value_load(nri[0:1, 0:1], min_val=0, max_val=MORE)
                for b in range(MORE):
                    with ac.If(more > b):
                        ac.wait_ge(S(f"x_pe{l}"), b * 4 + 1)
                        for i in range(2):
                            ins = ac.activation(xgT[0][:, i * 4:(i + 1) * 4, 0:CAP],
                                                TB[i][:, 0:4 * CAP].rearrange("p (k c) -> p k c", k=4), ACT.Copy)
                        ins.then_inc(S(f"x_act{l}"), 1)
                        ac.wait_ge(S(f"x_pe{l}"), b * 4 + 2)
                        ac.activation(silu_t[0:CAP, :], G[0][0:CAP, :], ACT.Tanh, scale=0.5).then_inc(S(f"x_act{l}"), 1)
                        ac.wait_ge(S(f"x_pe{l}"), b * 4 + 3)
                        ac.activation(actT[0][:, :, 0:CAP], OB[:, 0:4 * CAP].rearrange("p (k c) -> p k c", k=4),
                                      ACT.Copy).then_inc(S(f"x_act{l}"), 1)
                        ac.wait_ge(S(f"x_pe{l}"), b * 4 + 4)
                        if b:
                            ac.wait_ge(S(f"x_stored{l}"), 16 * b)
                        ac.activation(yo[0][0:CAP, 0:512], SB[0][0:CAP, :], ACT.Copy).then_inc(S(f"x_act{l}"), 1)
                        ac.activation(yo[0][0:CAP, 512:1024], SB[1][0:CAP, :], ACT.Copy).then_inc(S(f"x_y_ready{l}"), 1)
                    with ac.Else():
                        ac.nop()
                def squares_of_tile(t):
                    for i in range(2):
                        t_read(ac, (l, "comb", t * 2 + i))
                    cols = slice(t * P, (t + 1) * P)
                    ac.activation(hT[:, :, cols], xT[:, :, cols], ACT.Square).then_inc(S("sq_ready"), 1)

                if l + 1 < DEPTH:
                    for t in range(TT):
                        squares_of_tile(t)
                    continue

                def final_half(t):
                    ac.wait_ge(S("final_ss"), t + 1)
                    ac.activation(rms_c[:, 0, t:t + 1], OB[:, t:t + 1], ACT.Sqrt, bias=EPS, scale=1.0 / D)\
                        .then_inc(S("final_rms"), 1)
                    ac.wait_ge(S("y_out_turned"), 2 * t + 1)
                    ac.wait_ge(S("final_rstd"), t + 1)
                    n = 2 * t
                    ac.activation(y_rows[:, n * 512:(n + 1) * 512], out_banks[n % len(out_banks)][:, :], ACT.Copy,
                                  scale=rms_c[:, 1, t:t + 1]).then_inc(S("y_out_a"), 1)
                    ac.wait_ge(S("y_out_a"), t + 1)
                    dst = y_prompt[0] if t == 0 else y_sample[0, (t - 1) * P:t * P, :]
                    ac.dma_start(dst[:, 0:512], y_rows[:, n * 512:(n + 1) * 512]).then_inc(S("y_out_stored"), 16)

                for t in range(TT + 1):
                    if t < TT:
                        squares_of_tile(t)
                    if t:
                        final_half(t - 1)
            ac.wait_ge(S("y_out_stored"), 2 * TT * 16)
            ac.wait_ge(S("cache_stored"), DEPTH * 32)
            ac.wait_ge(S("state_stored"), DEPTH * 16)

        @block.vector
        def _(ve):
            chain = [0]

            def link(ins):
                chain[0] += 1
                ins.then_inc(S("dve_chain"), 1)
                ve.wait_ge(S("dve_chain"), chain[0])
                return ins

            ve.memset(ones[:, :], 1.0)
            ve.memset(cpad[:, :, :], 0.0)
            ve.memset(zrow, 0.0)
            ve.memset(rw[:, :, :], 0.0)
            link(ve.memset(xp[:, :], 0.0))
            ve.nop().then_inc(S("zeroed"), 1)
            ve.wait_ge(S("cvec_ready"), 1)
            ve.wait_ge(S("cond_tanh"), 1)
            link(ve.tensor_scalar(tmp[:, 6, 16:32], tmp[:, 6, 0:16], 0.5, 0.5, ALU.mult, ALU.add))
            ve.tensor_tensor(cpad[:, :, 0], tmp[:, 6, 16:24], cvec[:, 0:8], ALU.mult)
            ve.tensor_tensor(cpad[:, :, 1], tmp[:, 6, 24:32], cvec[:, 8:16], ALU.mult).then_inc(S("cond_ready"), 1)

            def squares_of_tile(t):
                cols = slice(t * P, (t + 1) * P)
                ve.tensor_tensor(hT[:, :, cols], xT[:, :, cols], xT[:, :, cols], ALU.mult).then_inc(S("sq_ready"), 1)

            for t in range(TT):
                for i in range(2):
                    ve.wait_ge(S("x_tran"), t * 2 + i + 1)
                    ve.tensor_copy(xT[:, i * 4:i * 4 + 4, t * P:(t + 1) * P],
                                   SB[i][:, :].rearrange("p (k c) -> p k c", k=4)).then_inc(S("x_taken"), 1)
                ve.wait_ge(S("x_taken"), 2 * t + 2)
                squares_of_tile(t)
            v_lam = vec[:, :, 1, 32:48]
            sp_ = lambda i: sp[:, i, :, :]

            def cached_keys():
                for l in range(DEPTH):
                    bank = t_ready(ve, (l, "kc", 0))
                    ve.tensor_copy(kcT[:, l, :, :], bank[:, 0:256].rearrange("p (g t) -> p g t", g=2))\
                        .then_inc(t_free((l, "kc", 0)), 1)

            def small_vectors():
                for l in range(DEPTH):
                    bank = t_ready(ve, (l, "vec", 0))
                    ve.tensor_copy(vec[:, l, 0, 0:104], bank[:, 0:104])
                    ve.tensor_copy(vec[:, l, 1, 0:64], bank[:, 128:192]).then_inc(t_free((l, "vec", 0)), 1)
                for l in range(DEPTH):
                    t_read(ve, (l, "vec", 0))
                ve.tensor_scalar(sp_(3), v_lam, -1.0, 0.0, ALU.mult, ALU.max)
                link(ve.tensor_scalar(sp_(2), v_lam, -1.0, None, ALU.mult))
                ve.tensor_tensor(sp_(0), sp_(2), v_lam, ALU.max).then_inc(S("lam_abs"), 1)

            def softplus():
                ve.wait_ge(S("lam_exp"), 1)
                link(ve.tensor_scalar(sp_(2), sp_(1), 2.0, None, ALU.add))
                link(ve.reciprocal(sp_(4), sp_(2)))
                link(ve.tensor_tensor(sp_(4), sp_(4), sp_(1), ALU.mult))
                link(ve.tensor_tensor(sp_(5), sp_(4), sp_(4), ALU.mult))
                link(ve.tensor_scalar(sp_(2), sp_(5), 1.0 / 19, 1.0 / 17, ALU.mult, ALU.add))
                for m in range(15, 0, -2):
                    link(ve.tensor_tensor(sp_(2), sp_(2), sp_(5), ALU.mult))
                    link(ve.tensor_scalar(sp_(2), sp_(2), 1.0 / m, None, ALU.add))
                link(ve.tensor_tensor(sp_(2), sp_(2), sp_(4), ALU.mult))
                link(ve.scalar_tensor_tensor(sp_(2), sp_(2), 2.0, sp_(3), ALU.mult, ALU.add))
                ve.tensor_scalar(sp_(6), sp_(2), -4.0, None, ALU.mult)
                ve.tensor_scalar(sp_(7), sp_(2), 4.0, None, ALU.mult)
                ve.tensor_scalar(hb[:, 0, :, :], vec[:, :, 1, 0:16], 0.5, None, ALU.mult)
                ve.tensor_scalar(hb[:, 1, :, :], vec[:, :, 1, 16:32], 0.5, None, ALU.mult)
                ve.wait_ge(S("router_loaded"), 48)
                link(ve.tensor_scalar(nsink[:, :, :], sinkb[:, :, :], -1.0, None, ALU.mult))

            def mod_add(l, cc):
                bank = t_ready(ve, (l, "mod", cc))
                b = v_ada(l, cc * 4, cc * 4 + 4)
                pair = bank[:, 0:8].rearrange("p (j s) -> p j s", s=2)
                ve.tensor_tensor(modT[:, cc * 4:cc * 4 + 4, 0], pair[:, :, 0], b, ALU.add)
                ve.tensor_tensor(modT[:, cc * 4:cc * 4 + 4, 1], pair[:, :, 1], b, ALU.add)\
                    .then_inc(t_free((l, "mod", cc)), 1)
                kk = 4 * (cc % 2)
                m = modT[:, cc * 4:cc * 4 + 4, :]
                if cc // 2 in (1, 4):
                    t_read(ve, (l, "mod", cc))
                    g0 = 88 if cc // 2 == 1 else 96
                    g = vec[:, l, 0, g0 + kk:g0 + kk + 4]
                    for st in range(2):
                        link(ve.scalar_tensor_tensor(modA[:, cc // 8, kk:kk + 4, st], m[:, :, st], 1.0, g, ALU.add, ALU.mult))
                elif cc // 2 == 2:
                    t_read(ve, (l, "mod", cc))
                    link(ve.tensor_scalar(modA[:, 2, kk:kk + 4, :], m, 0.5, None, ALU.mult))
                elif cc // 2 == 5:
                    t_read(ve, (l, "mod", cc))
                    link(ve.tensor_copy(modA[:, 3, kk:kk + 4, :], m))

            norms = [0]

            def rstd():
                norms[0] += 1
                ve.wait_ge(S("rms_ready"), norms[0])
                link(ve.reciprocal(rs, rs))

            for l in range(DEPTH):

                def normed():
                    rstd()
                    for k in range(KT):
                        ve.tensor_tensor(hT[:, k, :], xT[:, k, :], rs, ALU.mult).then_inc(S("xn_ready"), 1)

                normed()
                if l == 0:
                    small_vectors()
                    for cc in ADA_FIRST:
                        mod_add(0, cc)
                    ve.nop().then_inc(S("first_mods"), 1)
                    cached_keys()
                    softplus()

                def halves(high, low, src):
                    link(ve.tensor_copy(high, src))
                    return ve.tensor_tensor(low, src, high.bitcast(F32), ALU.subtract)

                def low_part(at):
                    kind, n = SPLIT[at]
                    s, use, _ = CHUNK_SLOT[CHUNK_AT[(l, f"{kind}{n // 4}")]]
                    if l == 0 and at == 2:
                        ve.wait_ge(S("rows_zero"), 16 * MORE)
                    ve.wait_ge(S("w_high"), split_no(l, kind, n) + 1)
                    high, low = w_part(kind, n)
                    ve.tensor_tensor(low, slot_kn(s)[:, :, n % 4 * P:(n % 4 + 1) * P], high.bitcast(F32), ALU.subtract)\
                        .then_inc(S("w_low"), 1)

                for i in range(2):
                    ve.wait_ge(S("h_ready_p"), 2 * l * KT + 4 * i + 4)
                    ve.wait_ge(S("h_ready_a"), 2 * l * KT + 4 * i + 4)
                    ks = slice(4 * i, 4 * i + 4)
                    halves(parts_r[:, 0, ks, :], parts_r[:, 1, ks, :], hT[:, ks, :]).then_inc(S("h_split"), 1)
                for at in range(AHEAD):
                    low_part(at)

                def rope(kind, i):
                    bank = g_ready(ve, (l, kind, i))
                    x = (kT if kind == "krot" else qT)[:, i, CTX:T]
                    turned = tmp[:, 6, 0:LAT]
                    ve.tensor_tensor(turned, bank[:, 0:LAT], sinT, ALU.mult).then_inc(g_free((l, kind, i)), 1)
                    link(ve.tensor_tensor(x, x, cosT, ALU.mult))
                    g_read(ve, (l, kind, i))
                    link(ve.tensor_tensor(x, x, turned, ALU.add))
                    ve.nop().then_inc(S("rope_done"), 1)

                def conv(j):
                    g_read(ve, (l, "xr", j))
                    x = xp[:, :]
                    link(ve.tensor_scalar(xc[:, j, :], x[:, 0:CW], v_conv(l, 0, j), v_convb(l, j), ALU.mult, ALU.add))
                    for i in range(1, 4):
                        ins = ve.scalar_tensor_tensor(xc[:, j, :], x[:, i:i + CW], v_conv(l, i, j), xc[:, j, :], ALU.mult, ALU.add)
                        if i < 3:
                            link(ins)
                    ins.then_inc(S("xc_ready"), 1)

                for h in range(HEADS):
                    low_part(h + AHEAD)
                    if h < 2:
                        rope("krot", h)
                    else:
                        rope("qrot", h - 2)
                    if h == 4:
                        mod_add(l, 4)
                for j in range(KT):
                    low_part(KT + j + AHEAD)
                    conv(j)
                    if j < 2:
                        rope("qrot", 6 + j)
                    if j % 4 == 0:
                        mod_add(l, 5 + j // 4)

                def softmax_max(u):
                    h, b = UNITS[u]
                    n = l * len(UNITS) + u
                    w = P if b == 0 else LATK
                    ve.wait_ge(S("scores_done"), n + 1)
                    if b:
                        cols = slice(P, LAT) if b == 1 else slice(0, P)
                        link(ve.tensor_tensor(SB[u % 2][:, cols], SB[u % 2][:, cols], mask[b - 1], ALU.add))
                    link(ve.tensor_reduce(smx[:, u % 2, 0:1], SB[u % 2][:, 0:w], AX.X, ALU.max))
                    ve.tensor_scalar(smx[:, u % 2, 1:2], smx[:, u % 2, 0:1], -SCALE, nsink[:, l, h:h + 1], ALU.mult, ALU.min)\
                        .then_inc(S("max_ready"), 1)

                def softmax_norm(u):
                    h, b = UNITS[u]
                    w = P if b == 0 else LATK
                    ve.wait_ge(S("exp_done"), l * len(UNITS) + u + 1)
                    link(ve.tensor_tensor(smx[:, u % 2, 4:5], smx[:, u % 2, 2:3], smx[:, u % 2, 3:4], ALU.add))
                    link(ve.reciprocal(smx[:, u % 2, 5:6], smx[:, u % 2, 4:5]))
                    ve.tensor_scalar(pr[:, u % 2, 0:w], pr[:, u % 2, 0:w], smx[:, u % 2, 5:6], None, ALU.mult)\
                        .then_inc(S("probs_ready"), 1)

                def one_minus_square(n):
                    ve.wait_ge(S("lru_act"), l * 16 + n + 1)
                    th = tmp[:, 2 + n % 2, :]
                    ve.scalar_tensor_tensor(th, a2, 1.0, th, ALU.add, ALU.mult).then_inc(S("lru_square"), 1)

                def scan(n):
                    d, j = PAIRS[n]
                    m = l * 16 + n
                    a, th, ti = tmp[:, n % 2, :], tmp[:, 2 + n % 2, :], tmp[:, 4 + n % 2, :]
                    link(ve.scalar_tensor_tensor(ti, ti, 1.0, xc[:, j, :], ALU.add, ALU.mult))
                    ve.wait_ge(S("root_ready"), m + 1)
                    link(ve.tensor_tensor(th, th, ti, ALU.mult))
                    dst = hyb[:, :] if d == 0 else ti
                    for st in range(2):
                        cs = slice(0, CTX) if st == 0 else slice(LAT0, CW)
                        init = 0.0 if st == 0 else v_state(l, d, j)
                        aa, ww, oo = a[:, cs], th[:, cs], dst[:, cs]
                        if d == 1:
                            aa, ww, oo = aa[:, ::-1], ww[:, ::-1], oo[:, ::-1]
                        ins = ve.tensor_tensor_scan(oo, aa, ww, init, ALU.mult, ALU.add)
                    link(ins)
                    last = dst[:, CTX - 1:CTX] if d == 0 else dst[:, 0:1]
                    if l and n == 0:
                        ve.wait_ge(S("tran_done"), T_AT[(l - 1, "state", 0)] + 1)
                    ve.tensor_copy(hlast[:, d * 8 + j:d * 8 + j + 1], last).then_inc(S("hlast_ready"), 1)
                    if d == 1:
                        for st in range(2):
                            cs = slice(0, CTX) if st == 0 else slice(LAT0, CW)
                            ins = ve.tensor_tensor(th[:, cs], hyb[:, cs], ti[:, cs], ALU.add)
                        link(ins)
                        for st in range(2):
                            cs = slice(0, CTX) if st == 0 else slice(LAT0, CW)
                            ins = ve.scalar_tensor_tensor(gr[:, j, STREAM[st]], gr[:, j, STREAM[st]], 0.5, th[:, cs],
                                                          ALU.mult, ALU.mult)
                        link(ins)
                        halves(qT_r[:, j, :], gr_r[:, j, :], gr[:, j, :]).then_inc(S("rnn_ready"), 1)
                    ve.wait_ge(S("hlast_ready"), m + 1)
                    ve.nop().then_inc(S("lru_used"), 1)

                def gelu_arg(j):
                    ve.wait_ge(S("gelu_sq"), l * KT + j + 1)
                    x = gelu_t[:, j % 2, :]
                    link(ve.tensor_scalar(x, x, 0.044715, 1.0, ALU.mult, ALU.add))
                    ve.tensor_tensor(x, x, gr[:, j, :], ALU.mult).then_inc(S("gelu_arg"), 1)

                def gelu_end(j):
                    ve.wait_ge(S("gelu_tanh"), l * KT + j + 1)
                    ve.scalar_tensor_tensor(gr[:, j, :], gelu_t[:, j % 2, :], 1.0, gr[:, j, :], ALU.add, ALU.mult)\
                        .then_inc(S("gelu_done"), 1)

                def att_split(h):
                    ve.wait_ge(S("att_copied"), l * len(UNITS) + 3 * h + 3)
                    if h == 0:
                        ve.wait_ge(S("gemm_done"), G_AT[(l, "gr", KT - 1)] + 1)
                    halves(parts_r[:, 0, h, :], parts_r[:, 1, h, :], qT[:, h, :]).then_inc(S("att_split"), 1)

                for i in range(3 * KT):
                    softmax_max(i)
                    softmax_norm(i)
                    for h in range(HEADS - 1):
                        if i == max(KT + 1 + h, 3 * h + 4):
                            att_split(h)
                    if 1 <= i <= KT:
                        gelu_end(i - 1)
                    if i % 4 == 0 and i <= KT:
                        mod_add(l, 7 + i // 4)
                    if i < KT:
                        gelu_arg(i)
                    if i + AHEAD < KT:
                        low_part(2 * KT + i + AHEAD)
                    if i > KT:
                        one_minus_square(i - KT - 1)
                        scan(i - KT - 1)
                one_minus_square(15)
                low_part(EARLY)
                att_split(HEADS - 1)
                low_part(EARLY + 1)
                scan(15)

                for n in range(KT):
                    low_part(EARLY + n + AHEAD)
                    bank = g_ready(ve, (l, "ap", n))
                    g_read(ve, (l, "ga", n))
                    ve.scalar_tensor_tensor(ga[:, n, :], ga[:, n, :], 1.0, bank[:, 0:T], ALU.add, ALU.mult)\
                        .then_inc(g_free((l, "ap", n)), 1)
                for n in range(KT):
                    low_part(EARLY + KT + n + AHEAD)
                    bank = g_ready(ve, (l, "rp", n))
                    g_read(ve, (l, "gb", n))
                    ve.scalar_tensor_tensor(gb[:, n, :], gb[:, n, :], 1.0, bank[:, 0:T], ALU.add, ALU.mult)\
                        .then_inc(g_free((l, "rp", n)), 1)
                    g_read(ve, (l, "rp", n))
                    link(ve.tensor_tensor(ga[:, n, :], ga[:, n, :], gb[:, n, :], ALU.add))
                    halves(parts_r[:, 0, n, :], parts_r[:, 1, n, :], ga[:, n, :]).then_inc(S("merged_ready"), 1)
                    if n in (1, 5):
                        mod_add(l, 10 + n // 4)
                for n in range(KT):
                    if n + AHEAD < KT:
                        low_part(EARLY + 2 * KT + n + AHEAD)
                    bank = g_ready(ve, (l, "wo", n))
                    for st in range(2):
                        ins = ve.scalar_tensor_tensor(xT[:, n, STREAM[st]], bank[:, STREAM[st]], modA[:, 2, n, st:st + 1],
                                                      xT[:, n, STREAM[st]], ALU.mult, ALU.add)
                    ins.then_inc(g_free((l, "wo", n)), 1)
                    g_read(ve, (l, "wo", n))
                    ve.tensor_tensor(gr[:, n, :], xT[:, n, :], xT[:, n, :], ALU.mult).then_inc(S("sq_ready"), 1)
                    if n in (1, 5) and l + 1 < DEPTH:
                        mod_add(l + 1, n // 4)
                normed()
                if l + 1 < DEPTH:
                    mod_add(l + 1, 2)
                    mod_add(l + 1, 3)
                    ve.nop().then_inc(S("first_mods"), 1)

                t_read(ve, (l, "logit", 0))
                R = lambda i: rt[:, i, :, :]
                bc_e = lambda v: v.rearrange("p (a e) -> p a e", a=1).broadcast_to([P, TT, NE])
                link(ve.tensor_scalar(R(0), R(0), 1.0, None, ALU.add))
                link(ve.reciprocal(R(1), R(0)))
                link(ve.tensor_tensor(R(2), R(1), bc_e(rb[:, :]), ALU.add))
                quad = rt[:, 2, :, :].rearrange("p t (g i) -> p (t g) i", i=EG)
                q4 = lambda i: rt4[:, i, :]
                mx, mn = ALU.max, ALU.min
                link(ve.tensor_tensor(q4(0), quad[:, :, 0], quad[:, :, 1], mx))
                link(ve.tensor_tensor(q4(1), quad[:, :, 0], quad[:, :, 1], mn))
                link(ve.tensor_tensor(q4(2), quad[:, :, 2], quad[:, :, 3], mx))
                link(ve.tensor_tensor(q4(3), quad[:, :, 2], quad[:, :, 3], mn))
                link(ve.tensor_tensor(q4(4), q4(0), q4(2), mx))
                link(ve.tensor_tensor(q4(5), q4(0), q4(2), mn))
                link(ve.tensor_tensor(q4(6), q4(1), q4(3), mx))
                link(ve.tensor_tensor(q4(6), q4(5), q4(6), mx))
                link(ve.tensor_tensor(q4(4), q4(4), q4(6), ALU.add))
                g3 = lambda i: rt4[:, i, :].rearrange("p (t g) -> p t g", g=NG)
                r1 = lambda i: rt1[:, i, :]
                bc1 = lambda v, w: v.rearrange("p (t a) -> p t a", a=1).broadcast_to([P, TT, w])
                bg = iota_g.rearrange("p (a g) -> p a g", a=1).broadcast_to([P, TT, NG])
                link(ve.tensor_reduce(r1(0), g3(4), AX.X, mx))
                link(ve.tensor_tensor(g3(5), g3(4), bc1(r1(0), NG), ALU.is_equal))
                link(ve.tensor_tensor(g3(5), g3(5), bg, ALU.mult))
                link(ve.tensor_reduce(r1(1), g3(5), AX.X, mx))
                link(ve.tensor_tensor(g3(6), g3(5), bc1(r1(1), NG), ALU.is_equal))
                in_grp = rt4[:, 6, :].rearrange("p (g a) -> p g a", a=1).broadcast_to([P, TT * NG, EG])
                r3 = lambda i: rt[:, i, :, :].rearrange("p t (g i) -> p (t g) i", i=EG)
                link(ve.tensor_tensor(r3(3), r3(2), in_grp, ALU.mult))
                link(ve.tensor_scalar(q4(7), q4(6), BIG, -BIG, ALU.mult, ALU.add))
                off = rt4[:, 7, :].rearrange("p (g a) -> p g a", a=1).broadcast_to([P, TT * NG, EG])
                link(ve.tensor_tensor(r3(3), r3(3), off, ALU.add))
                e16 = rt2[:, 0, :, :]
                for pick in range(2):
                    hot = R(6 + pick)
                    link(ve.tensor_reduce(r1(2), R(3), AX.X, mx))
                    link(ve.tensor_tensor(R(4), R(3), bc1(r1(2), NE), ALU.is_equal))
                    link(ve.tensor_tensor(R(4), R(4), bc_e(iota_e), ALU.mult))
                    link(ve.tensor_reduce(e16[:, pick, :], R(4), AX.X, mx))
                    link(ve.tensor_tensor(hot, R(4), bc1(e16[:, pick, :], NE), ALU.is_equal))
                    if pick == 0:
                        link(ve.scalar_tensor_tensor(R(3), hot, -BIG, R(3), ALU.mult, ALU.add))
                ve.tensor_tensor(R(8), R(6), R(7), ALU.add).then_inc(S("picked"), 1)
                hots = rt[:, 6:8, :, :]
                wide = rt[:, 9:11, :, :]
                p2 = lambda i: rt2[:, i, :, :]
                both = lambda v: v.rearrange("p (a t) e -> p a t e", a=1).broadcast_to([P, 2, TT, NE])
                both_e = lambda v: v.rearrange("p (a b e) -> p a b e", a=1, b=1).broadcast_to([P, 2, TT, NE])
                link(ve.tensor_tensor(wide, hots, both(R(1)), ALU.mult))
                link(ve.tensor_reduce(p2(1), wide, AX.X, ALU.add))
                link(ve.tensor_tensor(r1(2), p2(1)[:, 0, :], p2(1)[:, 1, :], ALU.add))
                link(ve.reciprocal(r1(3), r1(2)))
                ve.tensor_tensor(gates[:, :, :], p2(1), r1(3).rearrange("p (a t) -> p a t", a=1).broadcast_to([P, 2, TT]), ALU.mult)
                expert, rank, share, first, over, row, blk = (p2(i) for i in range(2, 9))
                link(ve.tensor_scalar(expert, e16, -1.0, float(NE), ALU.mult, ALU.add))
                bank = t_ready(ve, (l, "rank", 0))
                ranks = bank[:, 0:TT * NE].rearrange("p (t e) -> p t e", e=NE)
                rows = bank[:, TT * NE:(TT + 1) * NE]
                e_more, e_upto, e_shift = (rt[:, 12, i, :] for i in range(3))
                e_tmp = rt[:, 13, 0, :]
                ve.tensor_tensor(wide, hots, both(ranks), ALU.mult)
                link(ve.tensor_scalar(e_more, rows, float(CAP), None, ALU.is_gt))
                ve.tensor_reduce(rank, wide, AX.X, ALU.add)
                for k in range(2, T // CAP):
                    link(ve.tensor_scalar(e_tmp, rows, float(CAP * k), None, ALU.is_gt))
                    link(ve.tensor_tensor(e_more, e_more, e_tmp, ALU.add))
                ve.nop().then_inc(t_free((l, "rank", 0)), 1)
                ve.tensor_scalar(first, rank, float(CAP), None, ALU.is_ge)
                link(ve.tensor_tensor_scan(e_upto, ones[:, 0:NE], e_more, 0.0, ALU.mult, ALU.add))
                over_ = first
                for k in range(2, T // CAP):
                    ins = ve.scalar_tensor_tensor(over, rank, float(CAP * k), over_, ALU.is_ge, ALU.add)
                    over_ = over
                    if k == 2:
                        link(ve.tensor_tensor(e_shift, e_upto, e_more, ALU.subtract))
                    else:
                        link(ins)
                ve.scalar_tensor_tensor(row, over, -float(CAP), rank, ALU.mult, ALU.add)
                link(ve.scalar_tensor_tensor(e_shift, e_shift, float(NE - 1), num_e, ALU.add, ALU.subtract))
                if l:
                    for t in range(TT):
                        ve.wait_ge(S(f"back{t}"), 32 * l)
                link(ve.tensor_tensor(wide, hots, both_e(e_shift), ALU.mult))
                for i in range(2 * TT):
                    pick, t = divmod(i, TT)
                    ve.tensor_scalar(hot_c[:, i, :], num_c, row[:, pick, t:t + 1], None, ALU.is_equal)
                link(ve.tensor_reduce(share, wide, AX.X, ALU.add))
                link(ve.tensor_tensor(blk, first, share, ALU.mult))
                link(ve.tensor_tensor(blk, blk, over, ALU.add))
                link(ve.tensor_tensor(blk, blk, expert, ALU.add))
                for i in range(2 * TT):
                    pick, t = divmod(i, TT)
                    ins = ve.tensor_scalar(hot_b[:, i, :], num_b, blk[:, pick, t:t + 1], tokid[:, t:t + 1],
                                           ALU.is_equal, ALU.mult)
                ins.then_inc(S("hot_ready"), 1)
                link(ve.scalar_tensor_tensor(posu[:, :, :], blk, float(CAP), row, ALU.mult, ALU.add))
                ve.nop().then_inc(S("places_known"), 1)
                bank = t_ready(ve, (l, "ids", 0))
                ve.tensor_copy(ids[0:CAP, :], bank[0:CAP, 0:BLOCKS]).then_inc(t_free((l, "ids", 0)), 1)
                link(ve.tensor_copy(nri[0:1, 0:1], e_upto[0:1, NE - 1:NE]))
                for b in range(MORE):
                    link(ve.tensor_scalar(e_tmp[0:1, :], e_upto[0:1, :], float(b), None, ALU.is_le))
                    link(ve.tensor_reduce(nrt[0:1, 0:1], e_tmp[0:1, :], AX.X, ALU.add))
                    link(ve.tensor_scalar(nri[0:1, 1 + b:2 + b], nrt[0:1, 0:1], float(NE - 1), None, ALU.min))
                ve.nop().then_inc(S("blocks_known"), 1)
                for i in range(2 * TT):
                    pick, t = divmod(i, TT)
                    ins = ve.tensor_scalar(diag[:, i, :], ident, gates[:, pick, t:t + 1], None, ALU.mult)
                ins.then_inc(S("diag_ready"), 1)

                for e in range(NE):
                    n = l * NE + e
                    ve.wait_ge(S("silu_tanh"), n + 1)
                    if n:
                        ve.wait_ge(S("act_turned"), n)
                    link(ve.scalar_tensor_tensor(silu_t[0:CAP, :], silu_t[0:CAP, :], 1.0, G[0][0:CAP, :], ALU.add, ALU.mult))
                    ve.scalar_tensor_tensor(act[0:CAP, :], silu_t[0:CAP, :], 0.5, G[1][0:CAP, :], ALU.mult, ALU.mult)\
                        .then_inc(S("act_ready"), 1)
                more = ve.value_load(nri[0:1, 0:1], min_val=0, max_val=MORE)
                for b in range(MORE):
                    with ve.If(more > b):
                        ve.wait_ge(S(f"x_act{l}"), b * 4 + 2)
                        ve.scalar_tensor_tensor(silu_t[0:CAP, :], silu_t[0:CAP, :], 1.0, G[0][0:CAP, :], ALU.add, ALU.mult)\
                            .then_inc(S(f"x_silu{l}"), 1)
                        ve.wait_ge(S(f"x_silu{l}"), b + 1)
                        ve.scalar_tensor_tensor(act[0:CAP, :], silu_t[0:CAP, :], 0.5, G[1][0:CAP, :], ALU.mult, ALU.mult)\
                            .then_inc(S(f"x_dve{l}"), 1)
                    with ve.Else():
                        ve.nop()
                def x_update(t):
                    st = 0 if t == 0 else 1
                    for i in range(2):
                        g = (l, "comb", t * 2 + i)
                        bank = t_ready(ve, g)
                        for k in range(4):
                            kk = i * 4 + k
                            x = xT[:, kk, t * P:(t + 1) * P]
                            ins = ve.scalar_tensor_tensor(x, bank[:, k * P:(k + 1) * P], modA[:, 3, kk, st:st + 1], x,
                                                          ALU.mult, ALU.add)
                        ins.then_inc(t_free(g), 1)

                if l + 1 < DEPTH:
                    for t in range(TT):
                        x_update(t)
                    continue

                def final_half(t):
                    ve.wait_ge(S("final_rms"), t + 1)
                    ve.reciprocal(rms_c[:, 1, t:t + 1], rms_c[:, 0, t:t + 1]).then_inc(S("final_rstd"), 1)
                    ve.wait_ge(S("final_rstd"), t + 1)
                    ve.wait_ge(S("y_out_turned"), 2 * t + 2)
                    n = 2 * t + 1
                    ve.tensor_scalar(y_rows[:, n * 512:(n + 1) * 512], out_banks[n % len(out_banks)][:, :],
                                     rms_c[:, 1, t:t + 1], None, ALU.mult).then_inc(S("y_out_b"), 1)

                gain = cvec[:, 16:24].rearrange("p (k a) -> p k a", a=1).broadcast_to([P, KT, P])
                for t in range(TT + 1):
                    if t < TT:
                        x_update(t)
                        for i in range(2):
                            t_read(ve, (l, "comb", 2 * t + i))
                        cols = slice(t * P, (t + 1) * P)
                        ve.tensor_tensor(xc[:, :, cols], xT[:, :, cols], gain, ALU.mult).then_inc(S("xg_ready"), 1)
                    if t:
                        final_half(t - 1)

        @block.gpsimd
        def _(po):
            po.memset(gatew[:, :, :, :], 0.0).then_inc(S("gatew_zero"), 1)
            po.wait_ge(S("gatew_zero"), 1)
            po.wait_ge(S("zeroed"), 1)
            for b in range(MORE):
                row = (NE + b) * CAP
                po.dma_start(yd[row:row + CAP, :], zrow[0:CAP, :]).then_inc(S("rows_zero"), 16)
            for l in range(DEPTH):
                def modulated(which):
                    base = (2 * l + which) * KT
                    for k in range(KT):
                        po.wait_ge(S("xn_ready"), base + k + 1)
                        po.tensor_scalar(hT[:, k, 0:CTX], hT[:, k, 0:CTX], modA[:, which, k, 0:1],
                                         modT[:, which * 24 + k, 0:1], ALU.mult, ALU.add).then_inc(S("h_ready_p"), 1)

                po.wait_ge(S("first_mods"), l + 1)
                modulated(0)
                for n, (d, j) in enumerate(PAIRS):
                    m = l * 16 + n
                    if m >= 2:
                        q = m - 2
                        po.wait_ge(S("gemm_done"), G_AT[(q // 16, "gate_x", q % 16)] + 1)
                    for which, w in enumerate((lru_wa, lru_wx)):
                        for half in range(2):
                            po.dma_start(gatew[half * 64:half * 64 + 64, which, n % 2, half * 64:half * 64 + 64],
                                         w[l, d, 2 * j + half]).then_inc(S(f"gatew_loaded{n % 2}"), 16)
                modulated(1)
                t_read(po, (l, "ids", 0))
                po.wait_ge(S("h2_stored"), (l + 1) * TT * 16)

                def gather(dst, idx, sem):
                    po.indirect_dma_start(out=dst, out_offset=None, in_=h2d[:, :],
                                          in_offset=bass.IndirectOffsetOnAxis(ap=idx, axis=0)).then_inc(sem, 16)

                for e in range(NE):
                    n = l * NE + e
                    if e >= 2:
                        po.wait_ge(S("x_turned"), n - 1)
                    gather(xg[e % 2][0:CAP, :], ids[0:CAP, e:e + 1], S(f"row_gathered{e % 2}"))
                po.wait_ge(S("blocks_known"), l + 1)
                more = po.value_load(nri[0:1, 0:1], min_val=0, max_val=MORE)
                for b in range(MORE):
                    with po.If(more > b):
                        po.wait_ge(S("experts_done"), l + 1)
                        if b:
                            po.wait_ge(S(f"x_pe{l}"), 4 * b)
                        gather(xg[0][0:CAP, :], ids[0:CAP, NE + b:NE + b + 1], S(f"x_gathered{l}"))
                    with po.Else():
                        po.nop()
                po.wait_ge(S("experts_done"), l + 1)
                po.wait_ge(S("blocks_over"), l + 1)
                po.wait_ge(S("rows_zero"), 16 * MORE)
                po.wait_ge(S("places_known"), l + 1)
                for t in range(TT):
                    for pick in range(2):
                        po.indirect_dma_start(out=yg[t][pick], out_offset=None, in_=yd[:, :],
                                              in_offset=bass.IndirectOffsetOnAxis(ap=posu[:, pick, t:t + 1], axis=0))\
                            .then_inc(S(f"back{t}"), 16)


_INS = ["x_prompt", "x_sample", "cache_k", "cache_v", "state_h", "c", "c_ctx", "norm1_g", "norm2_g", "w_ada",
        "b_ada", "w_in", "conv_w", "conv_b", "lru_wa", "lru_ba", "lru_wx", "lru_bx", "lru_lambda", "attn_sink",
        "w_attn_proj", "w_rnn_proj", "w_out", "router_w", "router_b", "w_gate_up", "w_down", "final_norm_g"]
_OUTS = [(1, CTX, D), (1, LAT, D), (1, DEPTH, CTX, KVH, HD), (1, DEPTH, CTX, KVH, HD), (1, DEPTH, 2, D)]


def shape_constants():
    ident = np.eye(P, dtype=np.float32)
    rot = np.zeros((P, P), np.float32)
    half = HD // 2
    for i in range(half):
        rot[half + i, i] = -1.0
        rot[i, half + i] = 1.0
    t = np.arange(LAT)
    inv = (np.float32(10000.0) ** (-np.arange(HD // 4, dtype=np.float32) / np.float32(HD // 4))).astype(np.float32)
    ang = np.concatenate([(t // 64).astype(np.float32)[:, None] * inv, (t % 64).astype(np.float32)[:, None] * inv], 1)
    ang = np.concatenate([ang, ang], 1).T.astype(np.float32)
    i, j = np.meshgrid(np.arange(P), np.arange(P), indexing="ij")
    m0 = np.where(j <= i, 0.0, -BIG)
    m1 = np.where(j >= i, 0.0, -BIG)
    before = (i < j).astype(np.float32)
    sumsel = np.zeros((P, 2))
    sumsel[0::32, 0] = 1
    sumsel[1::32, 1] = 1
    sel_e = np.concatenate([np.eye(32, NE)] * 4, 0)
    row = lambda v: np.tile(np.asarray(v, np.float32)[None, :], (P, 1))
    tok = np.arange(T).reshape(TT, P).T
    parts = [ident, rot, np.cos(ang), np.sin(ang), m0, m1, before, sumsel, row(NE - np.arange(NE)),
             row(NG - np.arange(NG)), tok, row(np.arange(NE)), row(np.arange(BLOCKS)), row(np.arange(CAP)), sel_e]
    return np.concatenate([np.asarray(p, np.float32) for p in parts], 1)


def kernel(**inputs):
    import concourse.bacc as _bacc
    from concourse.bass_utils import run_bass_kernel_spmd as _run

    nc = _bacc.Bacc("TRN2", target_bir_lowering=False, num_devices=1)
    arrays, args = {}, []
    for name in _INS:
        a = np.ascontiguousarray(inputs[name])
        arrays[f"in_{name}"] = a
        args.append(nc.dram_tensor(f"in_{name}", a.shape, mybir.dt.from_np(a.dtype), kind="ExternalInput").ap())
    a = shape_constants()
    arrays["shape_constants"] = a
    args.append(nc.dram_tensor("shape_constants", a.shape, F32, kind="ExternalInput").ap())
    for i, shape in enumerate(_OUTS):
        args.append(nc.dram_tensor(f"out_{i}", shape, F32, kind="ExternalOutput").ap())
    build(nc, *args)
    r = _run(nc, [arrays], core_ids=[0])
    return tuple(r.results[0][f"out_{i}"] for i in range(len(_OUTS)))
```
